# Optimizing a Trainium2 kernel written in Bass

```python
import functools
import jax, jax.numpy as jnp
from jax import lax
import numpy as np

D_MODEL = 2048
BATCH = 1
SEQ = 256
DEPTH = 1
DEC_BATCH = 8
DEC_SEQ = 4
PAST_LEN = 2048
PAGE_SIZE = 128

MIX_WIDTH = D_MODEL
GLA_WIDTH = MIX_WIDTH // 2
GLA_HEADS = 4
GLA_DV = GLA_WIDTH // GLA_HEADS
GLA_DK = GLA_DV // 2
GLA_GATE_RANK = 16
GLA_TAU = 16.0
GLA_CHUNK = 16
MOBA_WIDTH = MIX_WIDTH - GLA_WIDTH
MOBA_HEADS = 8
MOBA_DH = MOBA_WIDTH // MOBA_HEADS
MOBA_BLOCK = 256
MOBA_TOPK = 3
MOBA_QBLOCK = 16
PEER_HEADS = 8
PEER_NKEYS = 128
PEER_EXPERTS = PEER_NKEYS * PEER_NKEYS
PEER_TOPK = 16
PEER_QDIM = 128
PEER_TOKEN_BLOCK = 128
PLE_DIM = 256
RMS_EPS = 1e-6
IN_WIDTHS = (GLA_HEADS * GLA_DK, GLA_HEADS * GLA_DK, GLA_WIDTH, GLA_WIDTH, GLA_GATE_RANK,
             MOBA_WIDTH, MOBA_WIDTH, MOBA_WIDTH)
IN_TOTAL = sum(IN_WIDTHS)

kernel_name = 'hymba_gla_moba_peer_decode_step'

def rmsnorm(x, g):
    xf = x.astype(jnp.float32)
    y = xf * lax.rsqrt(jnp.mean(xf * xf, axis=-1, keepdims=True) + RMS_EPS)
    return (y * g.astype(jnp.float32)).astype(x.dtype)

def alibi_slopes():
    return 2.0 ** (-8.0 * jnp.arange(1, MOBA_HEADS + 1, dtype=jnp.float32) / MOBA_HEADS)

def gla_recurrence(q, k, v, log_a, s0):
    B, T, H, _ = q.shape
    pad = (-T) % GLA_CHUNK
    n = (T + pad) // GLA_CHUNK

    def to_blocks(t):
        t = jnp.pad(t.astype(jnp.float32), ((0, 0), (0, pad), (0, 0), (0, 0)))
        return t.reshape(B, n, GLA_CHUNK, H, t.shape[-1]).transpose(1, 0, 3, 2, 4)

    causal = jnp.tril(jnp.ones((GLA_CHUNK, GLA_CHUNK), dtype=bool))[:, :, None]

    def step(S, blk):
        qc, kc, vc, ac = blk
        b = jnp.cumsum(ac, axis=2)
        decay = jnp.exp(jnp.where(causal, b[:, :, :, None, :] - b[:, :, None, :, :], -jnp.inf))
        scores = jnp.einsum('bhtsd,bhsd->bhts', qc[:, :, :, None, :] * decay, kc)
        o = jnp.einsum('bhtd,bhde->bhte', qc * jnp.exp(b), S) + jnp.einsum('bhts,bhse->bhte', scores, vc)
        b_end = b[:, :, -1:, :]
        S = jnp.exp(b_end[:, :, 0, :])[..., None] * S + jnp.einsum('bhsd,bhse->bhde', kc * jnp.exp(b_end - b), vc)
        return S, o

    s_end, o = lax.scan(step, s0.astype(jnp.float32),
                        (to_blocks(q), to_blocks(k), to_blocks(v), to_blocks(log_a)))
    o = o.transpose(1, 0, 3, 2, 4).reshape(B, n * GLA_CHUNK, H, -1)[:, :T]
    return o, s_end

def moba_select(q, means, n_eligible):
    nbf = means.shape[2]
    s = jnp.einsum('bhqd,bhcd->bhqc', q.astype(jnp.float32), means)
    s = jnp.where(jnp.arange(nbf) < n_eligible, s, -jnp.inf)
    vals, idx = lax.top_k(s, min(MOBA_TOPK, nbf))
    return idx, jnp.isfinite(vals)

def gather_blocks(blocks, idx):
    return jax.vmap(jax.vmap(lambda t, i: t[i]))(blocks, idx)

def moba_attend(q, q_pos, own_k, own_v, own_pos, sel_k=None, sel_v=None, sel_pos=None, sel_valid=None):
    slopes = alibi_slopes()[None, :, None, None]
    scale = MOBA_DH ** -0.5
    dist_own = (q_pos[:, None] - own_pos[None, :]).astype(jnp.float32)
    s_own = jnp.einsum('bhqd,bhkd->bhqk', q, own_k).astype(jnp.float32) * scale - slopes * dist_own
    s_own = jnp.where(dist_own >= 0, s_own, -jnp.inf)
    if sel_k is None:
        p = jax.nn.softmax(s_own, axis=-1)
        return jnp.einsum('bhqk,bhkd->bhqd', p, own_v)
    B, H, Q, S, BL, _ = sel_k.shape
    dist_sel = (q_pos[:, None, None] - sel_pos).astype(jnp.float32)
    s_sel = jnp.einsum('bhqd,bhqnkd->bhqnk', q, sel_k).astype(jnp.float32) * scale - slopes[..., None] * dist_sel
    s_sel = jnp.where(sel_valid[..., None], s_sel, -jnp.inf).reshape(B, H, Q, S * BL)
    p = jax.nn.softmax(jnp.concatenate([s_sel, s_own], axis=-1), axis=-1)
    p_sel = p[..., :S * BL].reshape(B, H, Q, S, BL)
    p_own = p[..., S * BL:]
    return jnp.einsum('bhqnk,bhqnkd->bhqd', p_sel, sel_v) + jnp.einsum('bhqk,bhkd->bhqd', p_own, own_v)

def moba_prompt(q, k, v):
    B, T, H, dh = q.shape
    nb = -(-T // MOBA_BLOCK)
    nbf = T // MOBA_BLOCK
    pad = nb * MOBA_BLOCK - T

    def to_blocks(t):
        t = jnp.pad(t, ((0, 0), (0, pad), (0, 0), (0, 0)))
        return t.reshape(B, nb, MOBA_BLOCK, H, dh).transpose(0, 3, 1, 2, 4)

    kb, vb = to_blocks(k), to_blocks(v)
    means = kb[:, :, :nbf].astype(jnp.float32).mean(axis=3)
    nq = T // MOBA_QBLOCK
    qb = q.reshape(B, nq, MOBA_QBLOCK, H, dh).transpose(1, 0, 3, 2, 4)

    def one(args):
        qi, qc = args
        start = qi * MOBA_QBLOCK
        q_pos = start + jnp.arange(MOBA_QBLOCK)
        j = start // MOBA_BLOCK
        own_k = lax.dynamic_index_in_dim(kb, j, axis=2, keepdims=False)
        own_v = lax.dynamic_index_in_dim(vb, j, axis=2, keepdims=False)
        own_pos = j * MOBA_BLOCK + jnp.arange(MOBA_BLOCK)
        if nbf == 0:
            return moba_attend(qc, q_pos, own_k, own_v, own_pos)
        idx, valid = moba_select(qc, means, j)
        sel_pos = idx[..., None] * MOBA_BLOCK + jnp.arange(MOBA_BLOCK)
        return moba_attend(qc, q_pos, own_k, own_v, own_pos,
                           gather_blocks(kb, idx), gather_blocks(vb, idx), sel_pos, valid)

    o = lax.map(one, (jnp.arange(nq), qb))
    return o.transpose(1, 0, 3, 2, 4).reshape(B, T, H * dh)

def moba_sample(q, k, v, cache_k, cache_v, page_table):
    DB, Tq, H, dh = q.shape
    P = page_table.shape[1] * PAGE_SIZE
    j = P // MOBA_BLOCK
    nbf = j
    q_pos = P + jnp.arange(Tq)
    qh = q.transpose(0, 2, 1, 3)
    past_rows = jnp.arange(j * MOBA_BLOCK, P)

    def paged_rows(cache):
        return cache[page_table[:, past_rows // PAGE_SIZE], past_rows % PAGE_SIZE]

    own_k = jnp.concatenate([paged_rows(cache_k), k], axis=1).transpose(0, 2, 1, 3)
    own_v = jnp.concatenate([paged_rows(cache_v), v], axis=1).transpose(0, 2, 1, 3)
    own_pos = jnp.concatenate([past_rows, q_pos])
    if nbf == 0:
        o = moba_attend(qh, q_pos, own_k, own_v, own_pos)
    else:
        ppb = MOBA_BLOCK // PAGE_SIZE
        page_sums = cache_k.astype(jnp.float32).sum(axis=1)
        means = page_sums[page_table[:, :nbf * ppb]].reshape(DB, nbf, ppb, H, dh).sum(axis=2) / MOBA_BLOCK
        means = means.transpose(0, 2, 1, 3)
        idx, valid = moba_select(qh, means, nbf)
        sel_pos = idx[..., None] * MOBA_BLOCK + jnp.arange(MOBA_BLOCK)
        b_ix = jnp.arange(DB)[:, None, None, None, None]
        h_ix = jnp.arange(H)[None, :, None, None, None]
        pages = page_table[b_ix, sel_pos // PAGE_SIZE]
        offs = sel_pos % PAGE_SIZE
        sel_k = cache_k[pages, offs, h_ix]
        sel_v = cache_v[pages, offs, h_ix]
        o = moba_attend(qh, q_pos, own_k, own_v, own_pos, sel_k, sel_v, sel_pos, valid)
    return o.transpose(0, 2, 1, 3).reshape(DB, Tq, H * dh)

def peer_tokens(c, w_q, sub_keys, u_tab, v_tab):
    n = c.shape[0]
    q = (c @ w_q).reshape(n, PEER_HEADS, 2, PEER_QDIM // 2).astype(jnp.float32)
    s = jnp.einsum('nhpd,hpkd->nhpk', q, sub_keys.astype(jnp.float32))
    s1, i1 = lax.top_k(s[:, :, 0], PEER_TOPK)
    s2, i2 = lax.top_k(s[:, :, 1], PEER_TOPK)
    cand = (s1[..., :, None] + s2[..., None, :]).reshape(n, PEER_HEADS, PEER_TOPK * PEER_TOPK)
    cand_idx = (i1[..., :, None] * PEER_NKEYS + i2[..., None, :]).reshape(n, PEER_HEADS, PEER_TOPK * PEER_TOPK)
    top, pos = lax.top_k(cand, PEER_TOPK)
    experts = jnp.take_along_axis(cand_idx, pos, axis=-1)
    g = jax.nn.softmax(top, axis=-1)
    hid = jax.nn.gelu(jnp.einsum('nd,nhkd->nhk', c, u_tab[experts]).astype(jnp.float32), approximate=False)
    return jnp.einsum('nhk,nhkd->nd', (g * hid).astype(c.dtype), v_tab[experts])

def peer_ffn(c, w_q, sub_keys, u_tab, v_tab):
    shape = c.shape
    c2 = c.reshape(-1, shape[-1])
    n = c2.shape[0]
    blk = min(PEER_TOKEN_BLOCK, n)
    pad = (-n) % blk
    c2 = jnp.pad(c2, ((0, pad), (0, 0))).reshape(-1, blk, shape[-1])
    out = lax.map(lambda cb: peer_tokens(cb, w_q, sub_keys, u_tab, v_tab), c2)
    return out.reshape(-1, shape[-1])[:n].reshape(shape)

def layer(x, p, gla_state, moba_fn, g_mix, w_in, w_gate_up, b_gate, g_gla_out, w_out, g_ffn,
          w_peer_q, peer_sub_keys, peer_u, peer_v, w_ple_gate, w_ple_proj):
    B, T, _ = x.shape
    a = rmsnorm(x, g_mix)
    points = np.cumsum(IN_WIDTHS)[:-1].tolist()
    qg, kg, vg, rg, zg, qm, km, vm = jnp.split(a @ w_in, points, axis=-1)
    log_a = jax.nn.log_sigmoid((zg @ w_gate_up + b_gate).astype(jnp.float32)) / GLA_TAU
    heads_g = lambda t: t.reshape(B, T, GLA_HEADS, -1)
    o_g, s_new = gla_recurrence(heads_g(qg) * GLA_DK ** -0.5, heads_g(kg), heads_g(vg), heads_g(log_a), gla_state)
    o_g = rmsnorm(o_g, g_gla_out).reshape(B, T, GLA_WIDTH) * jax.nn.silu(rg.astype(jnp.float32))
    heads_m = lambda t: t.reshape(B, T, MOBA_HEADS, MOBA_DH)
    k_m, v_m = heads_m(km), heads_m(vm)
    o_m = moba_fn(heads_m(qm), k_m, v_m)
    h = x + jnp.concatenate([o_g.astype(x.dtype), o_m.astype(x.dtype)], axis=-1) @ w_out
    h = h + peer_ffn(rmsnorm(h, g_ffn), w_peer_q, peer_sub_keys, peer_u, peer_v)
    h = h + jax.nn.sigmoid(h @ w_ple_gate) * (p @ w_ple_proj)
    return h, k_m, v_m, s_new

def setup_inputs(seed: int = 0) -> dict:
    key = jax.random.key(seed)
    ks = jax.random.split(key, 24)
    n_pages = PAST_LEN // PAGE_SIZE
    n_used = DEC_BATCH * n_pages
    n_phys = n_used + (n_used + 3) // 4
    D = D_MODEL
    gla_k = GLA_HEADS * GLA_DK

    def nrm(k, shape, s=1.0):
        return s * jax.random.normal(k, shape, jnp.float32)

    return {
        'x_prompt': nrm(ks[0], (BATCH, SEQ, D)),
        'x_sample': nrm(ks[1], (DEC_BATCH, DEC_SEQ, D)),
        'cache_k': nrm(ks[2], (DEPTH, n_phys, PAGE_SIZE, MOBA_HEADS, MOBA_DH)),
        'cache_v': nrm(ks[3], (DEPTH, n_phys, PAGE_SIZE, MOBA_HEADS, MOBA_DH)),
        'state_gla': nrm(ks[4], (DEPTH, DEC_BATCH, GLA_HEADS, GLA_DK, GLA_DV)),
        'page_table': jax.random.permutation(ks[5], n_phys)[:n_used].reshape(DEC_BATCH, n_pages).astype(jnp.int32),
        'p_prompt': nrm(ks[6], (DEPTH, BATCH, SEQ, PLE_DIM)),
        'p_sample': nrm(ks[7], (DEPTH, DEC_BATCH, DEC_SEQ, PLE_DIM)),
        'g_mix': 1.0 + nrm(ks[8], (DEPTH, D), 0.1),
        'w_in': nrm(ks[9], (DEPTH, D, IN_TOTAL), D ** -0.5),
        'w_gate_up': nrm(ks[10], (DEPTH, GLA_GATE_RANK, gla_k), GLA_GATE_RANK ** -0.5),
        'b_gate': nrm(ks[11], (DEPTH, gla_k), 0.1),
        'g_gla_out': 1.0 + nrm(ks[12], (DEPTH, GLA_DV), 0.1),
        'w_out': nrm(ks[13], (DEPTH, MIX_WIDTH, D), MIX_WIDTH ** -0.5),
        'g_ffn': 1.0 + nrm(ks[14], (DEPTH, D), 0.1),
        'w_peer_q': nrm(ks[15], (DEPTH, D, PEER_HEADS * PEER_QDIM), D ** -0.5),
        'peer_sub_keys': nrm(ks[16], (DEPTH, PEER_HEADS, 2, PEER_NKEYS, PEER_QDIM // 2), (PEER_QDIM // 2) ** -0.5),
        'peer_u': nrm(ks[17], (DEPTH, PEER_EXPERTS, D), D ** -0.5),
        'peer_v': nrm(ks[18], (DEPTH, PEER_EXPERTS, D), PEER_HEADS ** -0.5),
        'w_ple_gate': nrm(ks[19], (DEPTH, D, D), D ** -0.5),
        'w_ple_proj': nrm(ks[20], (DEPTH, PLE_DIM, D), PLE_DIM ** -0.5),
        'g_final': 1.0 + nrm(ks[21], (D,), 0.1),
    }

def reference(x_prompt, x_sample, cache_k, cache_v, state_gla, page_table, p_prompt, p_sample,
              g_mix, w_in, w_gate_up, b_gate, g_gla_out, w_out, g_ffn, w_peer_q, peer_sub_keys,
              peer_u, peer_v, w_ple_gate, w_ple_proj, g_final):
    hp, hs = x_prompt, x_sample
    k_p, v_p, s_p, k_s, v_s, s_s = [], [], [], [], [], []
    for i in range(DEPTH):
        w = (g_mix[i], w_in[i], w_gate_up[i], b_gate[i], g_gla_out[i], w_out[i], g_ffn[i],
             w_peer_q[i], peer_sub_keys[i], peer_u[i], peer_v[i], w_ple_gate[i], w_ple_proj[i])
        s0 = jnp.zeros((hp.shape[0], GLA_HEADS, GLA_DK, GLA_DV), jnp.float32)
        hp, kpi, vpi, spi = layer(hp, p_prompt[i], s0, moba_prompt, *w)
        sample_fn = functools.partial(moba_sample, cache_k=cache_k[i], cache_v=cache_v[i], page_table=page_table)
        hs, ksi, vsi, ssi = layer(hs, p_sample[i], state_gla[i], sample_fn, *w)
        k_p.append(kpi); v_p.append(vpi); s_p.append(spi)
        k_s.append(ksi); v_s.append(vsi); s_s.append(ssi)
    y_prompt = rmsnorm(hp, g_final)
    y_sample = rmsnorm(hs, g_final)
    k_prompt, v_prompt, gla_prompt = jnp.stack(k_p), jnp.stack(v_p), jnp.stack(s_p)
    k_sample, v_sample, gla_sample = jnp.stack(k_s), jnp.stack(v_s), jnp.stack(s_s)
    return (y_prompt, y_sample, k_prompt, v_prompt, gla_prompt, k_sample, v_sample, gla_sample)


_drawn_inputs = setup_inputs


def setup_inputs(seed=0):
    import zlib

    import numpy as np

    out = dict(_drawn_inputs(seed))
    spreads = {}
    factors = {}
    for name, (base, spread) in spreads.items():
        noise = np.random.default_rng([zlib.crc32(name.encode()), seed]).standard_normal(out[name].shape)
        drawn = base * np.exp(spread * noise) if base else spread * noise
        out[name] = __import__('jax').numpy.asarray(drawn.astype(out[name].dtype))
    for name, factor in factors.items():
        out[name] = (out[name] * factor).astype(out[name].dtype)
    return out
```

```python
from contextlib import ExitStack

import numpy as np

import concourse.bass as bass
from concourse import mybir

F32 = mybir.dt.float32
I32 = mybir.dt.int32
U32 = mybir.dt.uint32
ALU = mybir.AluOpType
ACT = mybir.ActivationFunctionType
AX = mybir.AxisListType

P = 128
D = 2048
KT = D // P
T = 256
DB, TQ = 8, 4
TS = DB * TQ
N = T + TS
PAST, PAGE = 2048, 128
NPG = PAST // PAGE
NBLK = PAST // 256
GH, GDK, GDV = 4, 128, 256
MH, DH = 8, 128
RANK = 16
PH, PK, PKEYS = 8, 16, 128
NEXP = PKEYS * PKEYS
HK = PH * PK
PLE = 256
EPS = 1e-6
NEG = -1e30
LOW = -3e38
SCALE = float(DH) ** -0.5

QG, KG, RG, VG, VM, QM, KM = 0, 4, 8, 16, 24, 32, 40
OT = VG
NIN = 48
NOUT, NPQ, NPLE = 16, 8, 16
SLOTS = 4
WT = KT * P
WP = (KT + PLE // P) * P
UNITS = 8
LEVELS = (1, 2, 3, 4, 5, 6, 7)
NCONST = 13


class Link:

    def __init__(self, eng, sem):
        self.eng, self.sem, self.n, self.turn, self.per = eng, sem, 0, None, 0

    def count(self):
        return self.n if self.turn is None else self.turn * self.per + self.n

    def __call__(self, ins):
        self.n += 1
        ins.then_inc(self.sem, 1)
        self.eng.wait_ge(self.sem, self.count())

    def enter(self, turn, per):
        self.turn, self.per, self.first = turn, per, self.n

    def leave(self, turns):
        assert self.n - self.first == self.per, (self.n - self.first, self.per)
        self.n = self.first + turns * self.per
        self.turn = None


def program(nc, A, O):
    ctx = ExitStack()
    with ctx:
        def sb(name, shape, dt=F32):
            return ctx.enter_context(nc.sbuf_tensor(name, shape, dt))

        def sem(name):
            return ctx.enter_context(nc.semaphore(name))

        xT = sb("xT", [P, KT, N])
        aT = sb("aT", [P, KT, N])
        wring = sb("wring", [P, SLOTS, WP])
        big = sb("big", [P, 28160])
        ident = sb("ident", [P, P])
        ones = sb("ones", [P, P])
        masks = sb("masks", [P, len(LEVELS), P])
        subk = sb("subk", [P, PH, PKEYS])
        states = sb("states", [P, 3, GH * GDV])
        rstd = sb("rstd", [P, N])
        gmix = sb("gmix", [P, KT])
        gffn = sb("gffn", [P, KT])
        gfin = sb("gfin", [P, KT])
        ggla = sb("ggla", [P, 2])
        bgate = sb("bgate", [P, GH])
        pages = sb("pages", [1, DB * NPG], I32)
        small = sb("small", [P, 64])
        ebend = sb("ebend", [P, GH, DB])
        qe = sb("qe", [P, GH, TS])
        tokb = sb("tokb", [TS, DB])
        fold = sb("fold", [P, TS])

        proj = big[:, 0:NIN * N].rearrange("p (j n) -> p j n", n=N)
        vnat = big[:, NIN * N:NIN * N + 3 * D].rearrange("p (t c) -> p t c", c=D)
        kring = big[:, NIN * N + 3 * D:NIN * N + 3 * D + 8 * 1024].rearrange("p (g h k) -> p g h k", g=8, h=MH)
        vring = big[:, 0:4 * 1024].rearrange("p (g c) -> p g c", g=4)
        flatx = xT[:, :, :].rearrange("p k n -> p (k n)")
        flata = aT[:, :, :].rearrange("p k n -> p (k n)")
        chunk = [r[:, i * GH * N:(i + 1) * GH * N].rearrange("p (h n) -> p h n", n=N)
                 for r in (flatx, flata) for i in range(4)]
        cumb, dist_e, eq, ek = chunk[0:4]
        qk = chunk[4:8]
        st = states[:, :, :].rearrange("p s c -> p (s c)")
        gatt, gatt_s, gatt_top = st[:, 0:1024], st[0:TS, 1024:1152], st[:, 1152:1664]
        gtmp, gtmp_s = st[:, 1664:2688], st[0:TS, 2688:2816]
        kendT = chunk[1]
        kend = flatx[:, 2 * GH * N:2 * GH * N + 3 * 512].rearrange("p (t c) -> p t c", c=512)
        gsp = flata[:, 0:GH * GDV]
        vb = [flata[0:TS, (2 + i) * GH * N:(2 + i) * GH * N + GH * GDV] for i in range(2)]
        pdist = flata[:, 0:384]
        pbias = [flata[:, 384 + i * 384:768 + i * 384] for i in range(2)]
        pprob = [flata[:, 1152 + i * 384:1536 + i * 384] for i in range(2)]
        pprobT = [flata[:, 1920 + i * 384:2304 + i * 384] for i in range(2)]
        NS = PAST + TS
        sprob = flatx[0:TS, 0:NS]
        sbias = flatx[0:TS, NS:NS + PAST]
        sown = flata[0:TS, 2688:2688 + DB * TS].rearrange("p (b k) -> p b k", k=TS)
        so = flata[0:TS, 2944:2944 + MH * DH]
        sprobT = flata[:, 3968:3968 + NPG * TS]
        sownT = small[0:TS, 32:64]
        qpad = st[:, 0:MH * 36]
        s8 = st[0:TS, 512:704]
        cnat = big[:, 0:3 * D].rearrange("p (t c) -> p t c", c=D)
        ring = big[:, 3 * D:3 * D + UNITS * D].rearrange("p (u c) -> p u c", c=D)
        o = 3 * D + UNITS * D
        prod = big[:, o:o + D]
        o += D
        weight = big[:, o:o + 3 * P]
        o += 3 * P
        hid = big[:, o:o + 3 * P]
        o += 3 * P
        eidx = big[:, o:o + 3 * P].bitcast(U32)
        o += 3 * P
        coef = big[:, o:o + 3 * P]
        o += 3 * P
        dots = big[:, o:o + UNITS]
        o += UNITS
        now = big[:, o:o + 2 * UNITS].bitcast(U32).rearrange("p (s u) -> p s u", u=UNITS)
        o += 2 * UNITS
        diag = big[:, o:o + 4 * P].rearrange("p (s c) -> p s c", c=P)
        o += 4 * P
        assert o <= 28160
        r0 = 3 * D
        qpT = big[:, r0:r0 + PH * N].rearrange("p (h n) -> p h n", n=N)
        r0 += PH * N
        score = big[:, r0:r0 + 16 * P].rearrange("p (l k) -> p l k", k=P)
        r0 += 16 * P
        score2 = big[:, r0:r0 + 256]
        r0 += 256
        half = big[:, r0:r0 + 16 * 16].rearrange("p (l k) -> p l k", k=16)
        r0 += 256
        halfi = big[:, r0:r0 + 256].bitcast(U32).rearrange("p (l k) -> p l k", k=16)
        r0 += 256
        halff = big[:, r0:r0 + 256].rearrange("p (l k) -> p l k", k=16)
        r0 += 256
        cand = big[:, r0:r0 + 2048].rearrange("p (h c) -> p h c", c=256)
        r0 += 2048
        onehot = big[:, r0:r0 + 2048].rearrange("p (h k i) -> p h k i", k=16, i=16)
        r0 += 2048
        topv = big[:, r0:r0 + P].rearrange("p (h k) -> p h k", k=16)
        r0 += P
        posu = big[:, r0:r0 + P].bitcast(U32)
        r0 += P
        posi = [big[:, r0 + i * P:r0 + i * P + P].bitcast(U32) for i in range(2)]
        r0 += 2 * P
        posf = [big[:, r0 + i * P:r0 + i * P + P] for i in range(2)]
        r0 += 2 * P
        exf = [big[:, r0 + i * P:r0 + i * P + P] for i in range(3)]
        r0 += 3 * P
        iota16 = big[:, r0:r0 + 16]
        r0 += 16
        hsum = big[:, r0:r0 + 16]
        r0 += 16
        qrep = big[:, r0:r0 + PH * P].rearrange("p (h g n) -> p h g n", g=4, n=TS)
        r0 += PH * P
        crep = big[:, r0:r0 + KT * P].rearrange("p (k g n) -> p k g n", g=4, n=TS)
        assert r0 + KT * P <= 3 * D + UNITS * D
        sq1 = proj[:, 0:KT, :]
        sq = big[:, 3 * D:3 * D + KT * N].rearrange("p (k n) -> p k n", n=N)
        sq2 = big[:, 17000:17000 + KT * N].rearrange("p (k n) -> p k n", n=N)
        pleT = big[:, 0:2 * N].rearrange("p (k n) -> p k n", n=N)
        gate = [big[:, 1024 + i * N:1024 + (i + 1) * N] for i in range(SLOTS)]
        wz = wring[:, 0, WT:WT + KT * RANK].rearrange("p (k r) -> p k r", r=RANK)
        zT = st[0:RANK, 0:N]
        wgu = st[0:RANK, 512:1024]

        ps = ctx.enter_context(nc.psum_tensor("ps", [P, 8, 512], F32))

        epsc = small[:, 20:21]

        def sems(text):
            return [sem(n) for n in text.split()]

        const_in, x_in, x_again, late_in, ple_in = sems("const_in x_in x_again late_in ple_in")
        w_in = [sem(f"w_in{k}") for k in range(SLOTS)]
        w_slots_free = sem("w_slots_free")
        banks_free = sem("banks_free")
        ones_set, eps_set = sems("ones_set eps_set")
        squares, sum_sq, roots, normed, y_ready = sems("squares sum_sq roots normed y_ready")
        z_done, z_out, gate_mm, gate_out, loga_ln = sems("z_done z_out gate_mm gate_out loga_ln")
        vt_done, vt_out, qg_scaled = sems("vt_done vt_out qg_scaled")
        exps_in, exps_out = sems("exps_in exps_out")
        lev_in, lev_mm, lev_out = sems("lev_in lev_mm lev_out")
        kend_in, kend_t, kend_out = sems("kend_in kend_t kend_out")
        og_mm, og_out, gs_mm, gs_out = sems("og_mm og_out gs_mm gs_out")
        state_in = [sem(f"state_in{i}") for i in range(2)]
        state_out, states_gone, vb_done, state_mm, state_new = sems("state_out states_gone vb_done state_mm state_new")
        og_raw, og_sq, og_ssum, og_rt, silu_done, og_done = sems("og_raw og_sq og_ssum og_rt silu_done og_done")
        pb_done, pq_mm, pq_s, pe_done, pp_done, pt_mm, pt_out, po_mm, po_out = sems(
            "pb_done pq_mm pq_s pe_done pp_done pt_mm pt_out po_mm po_out")
        k_in = [sem(f"k_in{i}") for i in range(2)]
        v_in = [sem(f"v_in{i}") for i in range(2)]
        k_free, v_free = sems("k_free v_free")
        qp_done, qk_done, sc_out, sx_done, rden_done, pT_mm, pT_out, pv_done, so_out, sot_mm, sot_out = sems(
            "qp_done qk_done sc_out sx_done rden_done pT_mm pT_out pv_done so_out sot_mm sot_out")
        rep_done, score_mm, score_out, lists_done, cn_mm, cn_out, gmax_done, gexp_done = sems(
            "rep_done score_mm score_out lists_done cn_mm cn_out gmax_done gexp_done")
        row_in = [sem(f"row_in{k}") for k in range(UNITS)]
        now_set, rows_free, hid_part, hid_done, gelu_done, coef_done = sems(
            "now_set rows_free hid_part hid_done gelu_done coef_done")
        diag_set, units_done, yn_out, yt_mm, yt_out = sems("diag_set units_done yn_out yt_mm yt_out")
        sig_done, gate_done = sems("sig_done gate_done")
        dve_own, act_own, stored, kv_stored, waits_over = sems("dve_own act_own stored kv_stored waits_over")

        block = ctx.enter_context(nc.Block())
        TT = [(0, P), (P, P), (T, TS)]
        NG = NPG // 4
        G = [P // UNITS, P // UNITS, TS // UNITS]
        GT = sum(G)
        W_OUT, W_PQ, W_PLE = (x // SLOTS for x in (NIN, NIN + NOUT, NIN + NOUT + NPQ))
        n_pages = A["kT"].shape[0]

        def then_plain(eng):
            eng.sem_inc(waits_over, 1)

        @block.sync
        def _(sp):
            consts = ((ident[:, :], A["ident"]), (masks[:, :, :], A["masks"]), (subk[:, :, :], A["subk"]),
                      (gmix[:, :], A["g_mix"]), (gffn[:, :], A["g_ffn"]), (gfin[:, :], A["g_fin"]),
                      (ggla[:, :], A["g_gla"]), (bgate[:, :], A["b_gate"]), (pages[:, :], A["pages"]),
                      (wz, A["w_z"]), (wgu, A["w_gu"]), (tokb[:, :], A["tokb"]), (fold[:, :], A["fold"]))
            assert len(consts) == NCONST
            for dst, src in consts:
                sp.dma_start(dst, src).then_inc(const_in, 16)

            def weights(turn, width, src, first):
                for k in range(SLOTS):
                    sp.wait_ge(w_slots_free, (turn + first) * SLOTS + k + 1)
                    sp.dma_start(wring[:, k, 0:width], src[bass.ds(turn * SLOTS + k, 1), :, :]
                                 .rearrange("a p w -> p (a w)")).then_inc(w_in[k], 16)

            def k_pages(b, g0, g1):
                for g in range(g0, g1):
                    sp.wait_ge(k_free, b * NG + g + 1)
                    for pg in range(4):
                        page = sp.value_load(pages[0:1, bass.ds(b * NPG + g * 4 + pg, 1)], min_val=0, max_val=n_pages - 1)
                        sp.dma_start(kring[:, (g % 2) * 4 + pg, :, :].rearrange("p h k -> p (h k)"),
                                     A["kT"][bass.ds(page, 1), :, :].rearrange("a p c -> p (a c)")).then_inc(k_in[g % 2], 16)

            def v_pages(b):
                for g in range(2 * NG):
                    sp.wait_ge(v_free, b * 2 * NG + g + 1)
                    for pg in range(2):
                        page = sp.value_load(pages[0:1, bass.ds(b * NPG + g * 2 + pg, 1)], min_val=0, max_val=n_pages - 1)
                        sp.dma_start(vring[:, (g % 2) * 2 + pg, :],
                                     A["v"][bass.ds(page, 1), :, :].rearrange("a p c -> p (a c)")).then_inc(v_in[g % 2], 16)

            with sp.Fori(0, NIN // SLOTS) as i:
                weights(i, WT, A["w_in"], 0)
            sp.wait_ge(const_in, 16 * NCONST)
            k_pages(0, 0, 2)
            weights(0, WT, A["w_out"], W_OUT)
            sp.wait_ge(vt_out, 12)
            for t, (lo, n) in enumerate(TT):
                sp.dma_start(O["v_new"][lo:lo + n, :], vnat[0:n, t, 1024:2048]).then_inc(kv_stored, 16)
            sp.dma_start(O["k_new"], proj[:, KM:KM + MH, :]).then_inc(kv_stored, 16)
            sp.wait_ge(gs_out, 1)
            sp.dma_start(O["s_prompt"], gsp).then_inc(kv_stored, 16)
            sp.wait_ge(kv_stored, 16 * 5)
            sp.wait_ge(og_done, 8)
            sp.wait_ge(state_new, DB)
            sp.dma_start(pdist, A["pdist"]).then_inc(late_in, 16)
            sp.dma_start(sbias, A["sbias"]).then_inc(late_in, 16)
            sp.dma_start(sown, A["sown"]).then_inc(late_in, 16)
            k_pages(0, 2, 4)
            with sp.Fori(0, DB - 1) as b:
                k_pages(b + 1, 0, 4)
                v_pages(b)
            v_pages(DB - 1)
            sp.wait_ge(pT_mm, DB)
            sp.dma_start(xT[:, :, :], A["xT"]).then_inc(x_again, 16)
            with sp.Fori(1, NOUT // SLOTS) as i:
                weights(i, WT, A["w_out"], W_OUT)
            with sp.Fori(0, NPQ // SLOTS) as i:
                weights(i, WT, A["w_pq"], W_PQ)
            weights(0, WP, A["w_ple"], W_PLE)
            sp.wait_ge(yt_out, 3)
            sp.dma_start(pleT, A["pleT"]).then_inc(ple_in, 16)
            with sp.Fori(1, NPLE // SLOTS) as i:
                weights(i, WP, A["w_ple"], W_PLE)
            sp.wait_ge(y_ready, KT)
            sp.dma_start(O["y"], xT[:, :, :]).then_inc(stored, 16)
            sp.wait_ge(stored, 16)

        @block.gpsimd
        def _(pool):
            pool.memset(ones[:, :], 1.0).then_inc(ones_set, 1)

            def state_load(b, par):
                pool.dma_start(states[:, par, :], A["s0"][bass.ds(b, 1), :, :].rearrange("a p c -> p (a c)")).then_inc(state_in[par], 16)

            def state_store(b, par):
                pool.wait_ge(state_new, b + 1)
                then_plain(pool)
                pool.dma_start(O["s_new"][bass.ds(b, 1), :, :].rearrange("a p c -> p (a c)"), states[:, par, :]).then_inc(state_out, 16)
                pool.wait_ge(state_out, (b + 1) * 16)
                then_plain(pool)

            pool.wait_ge(og_out, 8)
            state_load(0, 0)
            state_load(1, 1)
            with pool.Fori(0, DB // 2 - 1) as i:
                for par in range(2):
                    state_store(2 * i + par, par)
                    state_load(2 * i + 2 + par, par)
            for par in range(2):
                state_store(DB - 2 + par, par)
            pool.memset(small[:, 21:22], 0.0).then_inc(states_gone, 1)

            def gather(table, turn, slot, free, base):
                pool.wait_ge(now_set, turn + 1)
                for k in range(UNITS):
                    pool.wait_ge(free, base + k + 1)
                    then_plain(pool)
                    pool.indirect_dma_start(ring[:, k, :], None, table,
                                            bass.IndirectOffsetOnAxis(ap=now[:, slot, k:k + 1], axis=0)).then_inc(row_in[k], 16)

            with pool.Fori(0, GT // 2) as i:
                for s in range(2):
                    gather(A["u"], 2 * i + s, s, rows_free, (2 * i + s) * UNITS)
            for s in range(2):
                gather(A["vt"], GT + s, s, rows_free if s == 0 else units_done, GT * UNITS if s == 0 else 4)
            with pool.Fori(1, GT // 2) as i:
                for s in range(2):
                    gather(A["vt"], GT + 2 * i + s, s, units_done, (2 * i + s - 1) * UNITS + 4)

        @block.scalar
        def _(act):
            own = Link(act, act_own)
            act.dma_start(xT[:, :, :], A["xT"]).then_inc(x_in, 16)

            def squares_of(src, dst):
                for q in range(4):
                    act.activation(dst[:, 4 * q:4 * q + 4, :], src[:, 4 * q:4 * q + 4, :], ACT.Square).then_inc(squares, 1)

            def root(n):
                act.wait_ge(sum_sq, n)
                act.activation(rstd[:, :], ps[:, 7, 0:N], ACT.Sqrt, bias=epsc, scale=1.0 / D).then_inc(roots, 1)

            def copy_out(i, first, dst):
                for k in range(SLOTS):
                    act.wait_ge(w_slots_free, (i + first) * SLOTS + k + 1 + SLOTS)
                    act.activation(dst[:, bass.ds(i * SLOTS + k, 1), :].rearrange("p a n -> p (a n)"), ps[:, k, 0:N],
                                   ACT.Copy).then_inc(banks_free, 1)

            act.wait_ge(eps_set, 1)
            act.wait_ge(x_in, 16)
            squares_of(xT, sq1)
            root(1)
            act.wait_ge(z_done, 1)
            act.activation(zT, ps[0:RANK, 6, 0:N], ACT.Copy).then_inc(z_out, 1)
            act.wait_ge(const_in, 16 * NCONST)
            act.wait_ge(gate_mm, 1)
            for h in range(GH):
                act.activation(eq[:, h, :], ps[:, 4 + h, 0:N],
                               ACT.Identity, bias=bgate[:, h:h + 1]).then_inc(gate_out, 1)
            act.wait_ge(gate_out, GH)
            own(act.activation(ek, eq, ACT.Abs))
            own(act.activation(ek, ek, ACT.Exp, scale=-1.0))
            act.activation(ek, ek, ACT.Ln, bias=1.0).then_inc(loga_ln, 1)
            with act.Fori(0, NIN // SLOTS) as i:
                copy_out(i, 0, proj)
            for t, (lo, n) in enumerate(TT):
                for q in range(4):
                    m = 4 * t + q
                    act.wait_ge(vt_done, m + 1)
                    act.activation(vnat[0:n, t, q * 512:(q + 1) * 512], ps[0:n, m % 4, :], ACT.Copy).then_inc(vt_out, 1)
            for m in range(len(LEVELS) + 1):
                n = N if m < 2 else T
                act.wait_ge(exps_in, 2 * m + 1)
                act.activation(eq[:, :, 0:n], eq[:, :, 0:n], ACT.Exp).then_inc(exps_out, 1)
                act.wait_ge(exps_in, 2 * m + 2)
                act.activation(ek[:, :, 0:n], ek[:, :, 0:n], ACT.Exp).then_inc(exps_out, 1)
            act.wait_ge(exps_in, 2 * len(LEVELS) + 3)
            act.activation(kendT, kendT, ACT.Exp).then_inc(exps_out, 1)
            act.activation(qe[:, :, :], cumb[:, :, T:N], ACT.Exp).then_inc(exps_out, 1)
            act.activation(ebend[:, :, :], cumb[:, :, T + TQ - 1:N:TQ], ACT.Exp).then_inc(exps_out, 1)
            for t, (lo, n) in enumerate(TT):
                act.wait_ge(kend_t, t + 1)
                act.activation(kend[0:n, t, :], ps[0:n, t, :], ACT.Copy).then_inc(kend_out, 1)
            act.wait_ge(gs_mm, 1)
            own(act.activation(gsp[:, 0:512], ps[:, 6, :], ACT.Copy))
            act.activation(gsp[:, 512:1024], ps[:, 7, :], ACT.Copy).then_inc(gs_out, 1)
            act.wait_ge(og_raw, 1)
            for h in range(GH):
                act.activation(cumb[:, 2 * (h % 2):2 * (h % 2) + 2, :], proj[:, OT + 2 * h:OT + 2 * h + 2, :], ACT.Square).then_inc(og_sq, 1)
                act.wait_ge(og_ssum, h + 1)
                act.activation(ek[:, h, :], ps[:, 4 + h % 2, 0:N], ACT.Sqrt, bias=epsc, scale=1.0 / GDV).then_inc(og_rt, 1)
            act.activation(proj[:, RG:RG + 8, :], proj[:, RG:RG + 8, :], ACT.Silu).then_inc(silu_done, 1)

            act.wait_ge(late_in, 48)
            for h in range(MH + 1):
                if h < MH:
                    s = h % 2
                    if h >= 2:
                        act.wait_ge(pq_s, h - 1)
                    act.activation(pbias[s], pdist, ACT.Copy, scale=2.0 ** (-8.0 * (h + 1) / MH)).then_inc(pb_done, 1)
                    act.wait_ge(pq_s, h + 1)
                    for q, (lo, n) in enumerate(((0, P), (P, 2 * P))):
                        act.activation(pprob[s][:, lo:lo + n], pprob[s][:, lo:lo + n], ACT.Exp, bias=small[:, 4 * s + q:4 * s + q + 1],
                                       accum_out=small[:, 8 + 4 * s + q:9 + 4 * s + q]).then_inc(pe_done, 1)
                if h >= 1:
                    g, s = h - 1, (h - 1) % 2
                    act.wait_ge(pt_mm, g + 1)
                    act.activation(pprobT[s], ps[:, 2 + s, 0:384], ACT.Copy).then_inc(pt_out, 1)
                    act.wait_ge(po_mm, g + 1)
                    act.activation(proj[:, OT + 8 + g, 0:T], ps[:, 4 + s, 0:T], ACT.Copy).then_inc(po_out, 1)

            with act.Fori(0, DB) as b:
                act.wait_ge(sc_out, b + 1)
                act.activation(sprob, sprob, ACT.Exp, bias=small[0:TS, 16:17], accum_out=small[0:TS, 17:18]).then_inc(sx_done, 1)
                act.wait_ge(pT_mm, b + 1)
                act.activation(sprobT, ps[:, 5, :], ACT.Copy).then_inc(pT_out, 1)
                act.activation(sownT, ps[0:TS, 6, 0:TS], ACT.Copy).then_inc(pT_out, 1)
                act.wait_ge(pv_done, b + 1)
                act.wait_ge(rden_done, b + 1)
                act.activation(so[:, 0:512], ps[0:TS, 6, :], ACT.Copy, scale=small[0:TS, 18:19]).then_inc(so_out, 1)
                act.activation(so[:, 512:1024], ps[0:TS, 7, :], ACT.Copy, scale=small[0:TS, 18:19]).then_inc(so_out, 1)

            act.wait_ge(banks_free, SLOTS + NIN + NOUT)
            squares_of(xT, sq)
            root(2)
            with act.Fori(0, NPQ // SLOTS) as i:
                copy_out(i, W_PQ, qpT)
            for t in range(3):
                if t:
                    act.wait_ge(lists_done, t)
                for q in range(4):
                    act.wait_ge(score_mm, 4 * t + q + 1)
                    act.activation(score[:, 4 * q:4 * q + 4, :].rearrange("p l k -> p (l k)"), ps[:, q, :], ACT.Copy).then_inc(score_out, 1)
                for q in range(4):
                    act.wait_ge(cn_mm, 4 * t + q + 1)
                    act.activation(cnat[:, t, q * 512:(q + 1) * 512], ps[:, 4 + q, :], ACT.Copy).then_inc(cn_out, 1)
                act.wait_ge(gmax_done, t + 1)
                act.activation(topv, topv, ACT.Exp).then_inc(gexp_done, 1)
            act.wait_ge(hid_done, 1)
            act.activation(hid[:, 0:GT * UNITS], hid[:, 0:GT * UNITS], ACT.Gelu).then_inc(gelu_done, 1)
            act.wait_ge(coef_done, 1)
            done = 0
            for t, (lo, n) in enumerate(TT):
                with act.Fori(done, done + G[t]) as i:
                    for k in range(UNITS):
                        act.wait_ge(units_done, i * UNITS + k + 1)
                        act.activation(diag[:, k % 4, 0:n], ident[:, :] if t < 2 else fold[:, :], ACT.Copy,
                                       scale=coef[:, bass.ds(i * UNITS + k, 1)]).then_inc(diag_set, 1)
                done += G[t]
                act.wait_ge(units_done, 4 + done * UNITS)
                if t:
                    act.wait_ge(yt_mm, t)
                for c in range(4):
                    act.activation(prod[0:n, c * 512:(c + 1) * 512], ps[0:n, 4 * (t % 2) + c, :], ACT.Copy).then_inc(yn_out, 1)
            with act.Fori(0, NPLE // SLOTS) as i:
                for k in range(SLOTS):
                    act.wait_ge(w_slots_free, (i + W_PLE) * SLOTS + k + 1 + SLOTS)
                    act.wait_ge(gate_done, i * SLOTS + k + 1)
                    act.activation(gate[k], ps[:, k, 0:N], ACT.Sigmoid).then_inc(sig_done, 1)
            act.wait_ge(banks_free, SLOTS + NIN + NOUT + NPQ + NPLE)
            squares_of(aT, sq2)
            root(3)

        @block.tensor
        def _(pe):
            for s_, n in ((w_slots_free, SLOTS), (banks_free, SLOTS), (k_free, 2), (v_free, 2), (rows_free, UNITS),
                          (units_done, 4), (gate_done, SLOTS)):
                pe.sem_inc(s_, n)

            def sum_squares(n, src):
                for kt in range(KT):
                    if kt % 4 == 0:
                        pe.wait_ge(squares, 4 * (n - 1) + kt // 4 + 1)
                    mm = pe.matmul(ps[:, 7, 0:N], ones[:, :], src[:, kt, :], start=(kt == 0), stop=(kt == KT - 1))
                mm.then_inc(sum_sq, 1)

            def tiles(i, first, rhs, extra=None):
                for k in range(SLOTS):
                    pe.wait_ge(w_in[k], (i + first + 1) * 16)
                    pe.wait_ge(banks_free, (i + first) * SLOTS + k + 1)
                    for kt in range(KT):
                        mm = pe.matmul(ps[:, k, 0:N], wring[:, k, kt * P:(kt + 1) * P], rhs[:, kt, :],
                                       start=(kt == 0), stop=(kt == KT - 1))
                    if extra is not None:
                        mm = extra(k)
                    mm.then_inc(w_slots_free, 1)

            pe.wait_ge(ones_set, 1)
            sum_squares(1, sq1)
            pe.wait_ge(normed, 1)
            pe.wait_ge(const_in, 16 * NCONST)
            for kt in range(KT):
                mm = pe.matmul(ps[0:RANK, 6, 0:N], wz[:, kt, :], aT[:, kt, :], start=(kt == 0), stop=(kt == KT - 1))
            mm.then_inc(z_done, 1)
            pe.wait_ge(z_out, 1)
            for h in range(GH):
                mm = pe.matmul(ps[:, 4 + h, 0:N], wgu[:, h * P:(h + 1) * P], zT, start=True, stop=True)
            mm.then_inc(gate_mm, 1)
            with pe.Fori(0, NIN // SLOTS) as i:
                tiles(i, 0, aT)
            pe.wait_ge(banks_free, SLOTS + NIN)
            for t, (lo, n) in enumerate(TT):
                for q in range(4):
                    m = 4 * t + q
                    if m >= 4:
                        pe.wait_ge(vt_out, m - 3)
                    for f in range(4):
                        mm = pe.transpose(ps[0:n, m % 4, f * P:(f + 1) * P], proj[:, VG + 4 * q + f, lo:lo + n], ident[:, :])
                    mm.then_inc(vt_done, 1)
            pe.wait_ge(vt_out, 12)
            for m in range(len(LEVELS) + 2):
                par = m % 2
                pe.wait_ge(lev_in, m + 1)
                if m >= 2:
                    pe.wait_ge(lev_out, m - 1)
                q_, k_ = (qk[2 * par], qk[2 * par + 1]) if m else (proj[:, QG:QG + 4, :], proj[:, KG:KG + 4, :])
                if m == len(LEVELS) + 1:
                    for h in range(GH):
                        mm = pe.matmul(ps[:, 3 * par, h * P:(h + 1) * P], k_[:, h, 0:P], q_[:, h, P:T], start=True, stop=True)
                else:
                    for t in range(2):
                        for h in range(GH):
                            mm = pe.matmul(ps[:, 3 * par + t, h * P:(h + 1) * P], k_[:, h, t * P:(t + 1) * P],
                                           q_[:, h, t * P:(t + 1) * P], start=True, stop=True)
                if m <= 2:
                    for h in range(GH):
                        mm = pe.matmul(ps[0:TS, 3 * par + 2, h * TS:(h + 1) * TS], k_[:, h, T:N], q_[:, h, T:N], start=True, stop=True)
                mm.then_inc(lev_mm, 1)
            pe.wait_ge(lev_out, len(LEVELS) + 2)
            pe.wait_ge(kend_in, 1)
            for t, (lo, n) in enumerate(TT):
                for h in range(GH):
                    mm = pe.transpose(ps[0:n, t, h * P:(h + 1) * P], kendT[:, h, lo:lo + n], ident[:, :])
                mm.then_inc(kend_t, 1)
            pe.wait_ge(kend_out, 3)
            for h in range(GH):
                for t in range(2):
                    mm = pe.matmul(ps[:, 6 + h // 2, (h % 2) * GDV:(h % 2 + 1) * GDV], kend[:, t, h * P:(h + 1) * P],
                                   vnat[:, t, h * GDV:(h + 1) * GDV], start=(t == 0), stop=(t == 1))
            mm.then_inc(gs_mm, 1)
            for j in range(8):
                h, c = j // 2, j % 2
                if j >= 2:
                    pe.wait_ge(og_out, j - 1)
                bank = 4 + j % 2
                v0, v1, v2 = (vnat[0:n, t, h * GDV + c * P:h * GDV + (c + 1) * P] for t, (_, n) in enumerate(TT))
                pe.matmul(ps[:, bank, T:N], v2, gatt_s[:, h * TS:(h + 1) * TS], start=True, stop=True)
                pe.matmul(ps[:, bank, 0:P], v0, gatt[:, h * P:(h + 1) * P], start=True, stop=True)
                pe.matmul(ps[:, bank, P:T], v0, gatt_top[:, h * P:(h + 1) * P], start=True, stop=False)
                pe.matmul(ps[:, bank, P:T], v1, gatt[:, 512 + h * P:512 + (h + 1) * P], start=False, stop=True).then_inc(og_mm, 1)
            with pe.Fori(0, DB // 2) as i:
                for par in range(2):
                    pe.wait_ge(state_in[par], (i + 1) * 16)
                    pe.wait_ge(vb_done, 2 * i + par + 1)
                    for j in range(8):
                        pe.matmul(ps[:, 0, j * TQ:(j + 1) * TQ], states[:, par, (j // 2) * GDV + (j % 2) * P:(j // 2) * GDV + (j % 2 + 1) * P],
                                  qe[:, j // 2, bass.ds((2 * i + par) * TQ, TQ)], start=True, stop=True)
                    for h in range(GH):
                        mm = pe.matmul(ps[:, 1 + h // 2, (h % 2) * GDV:(h % 2 + 1) * GDV], kend[0:TS, 2, h * P:(h + 1) * P],
                                       vb[par][:, h * GDV:(h + 1) * GDV], start=True, stop=True)
                    mm.then_inc(state_mm, 1)
            for h in range(GH):
                pe.wait_ge(og_sq, h + 1)
                for c in range(2):
                    mm = pe.matmul(ps[:, 4 + h % 2, 0:N], ones[:, :], cumb[:, 2 * (h % 2) + c, :], start=(c == 0), stop=(c == 1))
                mm.then_inc(og_ssum, 1)

            pe.wait_ge(gs_out, 1)
            pe.wait_ge(og_rt, GH)
            for h in range(MH + 1):
                if h < MH:
                    s = h % 2
                    if h >= 2:
                        pe.wait_ge(pq_s, h - 1)
                    pe.matmul(ps[:, s, 0:P], proj[:, QM + h, 0:P], proj[:, KM + h, 0:P], start=True, stop=True)
                    pe.matmul(ps[:, s, P:3 * P], proj[:, QM + h, P:T], proj[:, KM + h, 0:T], start=True, stop=True).then_inc(pq_mm, 1)
                if h >= 1:
                    g, s = h - 1, (h - 1) % 2
                    pe.wait_ge(pp_done, g + 1)
                    for c in range(3):
                        mm = pe.transpose(ps[:, 2 + s, c * P:(c + 1) * P], pprob[s][:, c * P:(c + 1) * P], ident[:, :])
                    mm.then_inc(pt_mm, 1)
                    pe.wait_ge(pt_out, g + 1)
                    v0, v1 = (vnat[:, t, 1024 + g * DH:1024 + (g + 1) * DH] for t in range(2))
                    pe.matmul(ps[:, 4 + s, 0:P], v0, pprobT[s][:, 0:P], start=True, stop=True)
                    pe.matmul(ps[:, 4 + s, P:T], v0, pprobT[s][:, P:2 * P], start=True, stop=False)
                    pe.matmul(ps[:, 4 + s, P:T], v1, pprobT[s][:, 2 * P:3 * P], start=False, stop=True).then_inc(po_mm, 1)

            def scores(b):
                pe.wait_ge(qp_done, b + 1)
                for g in range(NG):
                    pe.wait_ge(k_in[g % 2], (b * 2 + g // 2 + 1) * 64)
                    for h in range(MH):
                        mm = pe.matmul(ps[0:TS, g, :], qpad[:, h * TS:(h + 1) * TS], kring[:, (g % 2) * 4:(g % 2) * 4 + 4, h, :],
                                       start=(h == 0), stop=(h == MH - 1))
                    mm.then_inc(k_free, 1)
                for h in range(MH):
                    mm = pe.matmul(ps[0:TS, 4, 0:TS], qpad[:, h * TS:(h + 1) * TS], proj[:, KM + h, T:N], start=(h == 0), stop=(h == MH - 1))
                mm.then_inc(qk_done, 1)

            def turn(b):
                pe.wait_ge(sx_done, b + 1)
                then_plain(pe)
                for pg in range(NPG):
                    pe.transpose(ps[:, 5, pg * TS:(pg + 1) * TS], sprob[:, pg * PAGE:(pg + 1) * PAGE], ident[0:TS, 0:TS])
                pe.transpose(ps[0:TS, 6, 0:TS], sprob[:, PAST:NS], ident[0:TS, 0:TS]).then_inc(pT_mm, 1)

            def values(b):
                pe.wait_ge(pT_out, 2 * b + 2)
                for g in range(2 * NG):
                    pe.wait_ge(v_in[g % 2], (b * NG + g // 2 + 1) * 32)
                    for pg in range(2):
                        for c in range(2):
                            mm = pe.matmul(ps[0:TS, 6 + c, :], sprobT[:, (2 * g + pg) * TS:(2 * g + pg + 1) * TS],
                                           vring[:, (g % 2) * 2 + pg, c * 512:(c + 1) * 512], start=(g == 0 and pg == 0), stop=False)
                    mm.then_inc(v_free, 1)
                for c in range(2):
                    mm = pe.matmul(ps[0:TS, 6 + c, :], sownT, vnat[0:TS, 2, 1024 + c * 512:1024 + (c + 1) * 512], start=False, stop=True)
                mm.then_inc(pv_done, 1)

            def own_heads(b):
                pe.wait_ge(so_out, 2 * b + 2)
                then_plain(pe)
                for h in range(MH):
                    mm = pe.matmul(ps[:, 5, h * TQ:(h + 1) * TQ], so[:, h * DH:(h + 1) * DH], ident[0:TS, h * TQ:(h + 1) * TQ], start=True, stop=True)
                mm.then_inc(sot_mm, 1)
                pe.wait_ge(sot_out, b + 1)
                then_plain(pe)

            pe.wait_ge(po_out, MH)
            scores(0)
            scores(1)
            turn(0)
            values(0)
            with pe.Fori(1, DB - 1) as b:
                scores(b + 1)
                own_heads(b - 1)
                turn(b)
                values(b)
            own_heads(DB - 2)
            turn(DB - 1)
            values(DB - 1)
            own_heads(DB - 1)

            with pe.Fori(0, NOUT // SLOTS) as i:
                tiles(i, W_OUT, proj[:, OT:OT + KT, :])
            sum_squares(2, sq)
            pe.wait_ge(normed, 2)
            with pe.Fori(0, NPQ // SLOTS) as i:
                tiles(i, W_PQ, aT)
            pe.wait_ge(banks_free, SLOTS + NIN + NOUT + NPQ)
            pe.wait_ge(roots, 2)
            for t, (lo, n) in enumerate(TT):
                if t == 2:
                    pe.wait_ge(rep_done, 8)
                for q in range(4):
                    if t:
                        pe.wait_ge(score_out, 4 * (t - 1) + q + 1)
                    for f in range(4):
                        h, hf = 4 * (q % 2) + f, q // 2
                        rows = slice(64 * hf, 64 * hf + 64)
                        lhs = qpT[rows, h, lo:lo + n] if t < 2 else qrep[rows, h, :, :].rearrange("p g n -> p (g n)")
                        mm = pe.matmul(ps[:, q, f * P:(f + 1) * P], lhs, subk[rows, h, :], start=True, stop=True)
                    mm.then_inc(score_mm, 1)
                for q in range(4):
                    if t:
                        pe.wait_ge(cn_out, 4 * (t - 1) + q + 1)
                    for f in range(4):
                        kt = 4 * q + f
                        src = aT[:, kt, lo:lo + n] if t < 2 else crep[:, kt, :, :].rearrange("p g n -> p (g n)")
                        mm = pe.transpose(ps[:, 4 + q, f * P:(f + 1) * P], src, ident[:, :])
                    mm.then_inc(cn_mm, 1)

            def unit(w, b0, turn_, k, first=False, last=False):
                pe.wait_ge(diag_set, turn_ * UNITS + k + 1)
                pe.wait_ge(row_in[k], (turn_ + GT + 1) * 16)
                for c in range(4):
                    mm = pe.matmul(ps[0:w, b0 + c, :], diag[:, k % 4, 0:w], ring[:, k, c * 512:(c + 1) * 512],
                                   start=first, stop=last, skip_group_check=True)
                mm.then_inc(units_done, 1)

            def back(t):
                b0, n = 4 * (t % 2), TT[t][1]
                pe.wait_ge(yn_out, 4 * t + 4)
                for kt in range(KT):
                    mm = pe.transpose(ps[:, b0 + kt // 4, (kt % 4) * P:(kt % 4) * P + n], prod[0:n, kt * P:(kt + 1) * P], ident[0:n, 0:n])
                mm.then_inc(yt_mm, 1)

            pe.wait_ge(cn_out, 12)
            done = 0
            for t, (lo, w) in enumerate(TT):
                b0 = 4 * (t % 2)
                if t == 2:
                    pe.wait_ge(yt_out, 1)
                for k in range(UNITS):
                    unit(w, b0, done, k, first=(k == 0))
                with pe.Fori(done + 1, done + G[t] - 1) as i:
                    for k in range(UNITS):
                        unit(w, b0, i, k)
                for k in range(UNITS):
                    unit(w, b0, done + G[t] - 1, k, last=(k == UNITS - 1))
                done += G[t]
                if t == 1:
                    back(0)
            back(1)
            back(2)

            pe.wait_ge(yt_out, 3)
            pe.wait_ge(ple_in, 16)

            def embed(k):
                for kt in range(PLE // P):
                    mm = pe.matmul(ps[:, 4 + k, 0:N], wring[:, k, WT + kt * P:WT + (kt + 1) * P], pleT[:, kt, :],
                                   start=(kt == 0), stop=(kt == PLE // P - 1))
                return mm

            with pe.Fori(0, NPLE // SLOTS) as i:
                tiles(i, W_PLE, xT, embed)
            sum_squares(3, sq2)

        @block.vector
        def _(dve):
            own = Link(dve, dve_own)
            dve.memset(epsc, EPS).then_inc(eps_set, 1)

            def normalise(n, src, dst, gain, then, each):
                dve.wait_ge(roots, n)
                own(dve.reciprocal(rstd[:, :], rstd[:, :]))
                for kt in range(KT):
                    ins = dve.scalar_tensor_tensor(out=dst[:, kt, :], in0=src[:, kt, :], scalar=gain[:, kt:kt + 1],
                                                   in1=rstd[:, :], op0=ALU.mult, op1=ALU.mult)
                    if each or kt == KT - 1:
                        ins.then_inc(then, 1)

            dve.wait_ge(const_in, 16 * NCONST)
            dve.wait_ge(x_in, 16)
            normalise(1, xT, aT, gmix, normed, False)
            dve.wait_ge(gate_out, GH)
            own(dve.tensor_scalar(dist_e, eq, 0.0, 1.0 / 16, ALU.min, ALU.mult))
            dve.wait_ge(loga_ln, 1)
            own(dve.scalar_tensor_tensor(out=dist_e, in0=ek, scalar=-1.0 / 16, in1=dist_e, op0=ALU.mult, op1=ALU.add))
            dve.wait_ge(ones_set, 1)
            for lo in (0, P):
                for h in range(GH):
                    ins = dve.tensor_tensor_scan(cumb[:, h, lo:lo + P], ones[:, :], dist_e[:, h, lo:lo + P],
                                                 0.0 if lo == 0 else cumb[:, h, P - 1:P], ALU.mult, ALU.add)
                own(ins)
            own(dve.tensor_copy(cumb[:, :, T:N:TQ], dist_e[:, :, T:N:TQ]))
            for j in range(1, TQ):
                own(dve.tensor_tensor(cumb[:, :, T + j:N:TQ], cumb[:, :, T + j - 1:N:TQ], dist_e[:, :, T + j:N:TQ], ALU.add))
            dve.wait_ge(banks_free, SLOTS + NIN)
            dve.tensor_scalar(proj[:, QG:QG + 4, :], proj[:, QG:QG + 4, :], float(GDK) ** -0.5, None, ALU.mult).then_inc(lev_in, 1)
            dve.wait_ge(lev_in, 1)

            def add_level(m):
                b0 = 3 * (m % 2)
                dve.wait_ge(lev_mm, m + 1)
                if m == len(LEVELS) + 1:
                    dve.tensor_copy(gatt_top, ps[:, b0, :]).then_inc(lev_out, 1)
                    return
                mask = ident if m == 0 else masks[:, m - 1, :]
                v = lambda a, w: a.rearrange("p (h t) -> p h t", t=w)
                for c in range(3 if m <= 2 else 2):
                    n, w = (P, P) if c < 2 else (TS, TS)
                    to = gatt[:, c * 512:(c + 1) * 512] if c < 2 else gatt_s
                    tmp = gtmp[:, c * 512:(c + 1) * 512] if c < 2 else gtmp_s
                    mk = mask[0:n, 0:w].rearrange("p (o t) -> p o t", o=1).broadcast_to([n, GH, w])
                    own(dve.tensor_tensor(v(to if m == 0 else tmp, w), v(ps[0:n, b0 + c, 0:GH * w], w), mk, ALU.mult))
                    if m:
                        own(dve.tensor_tensor(to, to, tmp, ALU.add))
                dve.sem_inc(lev_out, 1)

            for m in range(len(LEVELS) + 1):
                B = 2 << m
                n = N if m < 2 else T
                blocks = lambda a: a.rearrange("p (c x) -> p c x", x=B)
                par = (m + 1) % 2
                for h in range(GH):
                    src = blocks(cumb[:, h, 0:n])
                    ins = dve.tensor_tensor(blocks(dist_e[:, h, 0:n]), src, src[:, :, B // 2 - 1:B // 2].broadcast_to([P, n // B, B]), ALU.subtract)
                own(ins)
                dve.tensor_scalar(eq[:, :, 0:n], dist_e[:, :, 0:n], 0.0, None, ALU.min).then_inc(exps_in, 1)
                dve.tensor_scalar(ek[:, :, 0:n], dist_e[:, :, 0:n], -1.0, 0.0, ALU.mult, ALU.min).then_inc(exps_in, 1)
                add_level(m)
                dve.wait_ge(exps_out, 2 * m + 2)
                own(dve.tensor_tensor(qk[2 * par][:, :, 0:n], proj[:, QG:QG + 4, 0:n], eq[:, :, 0:n], ALU.mult))
                dve.tensor_tensor(qk[2 * par + 1][:, :, 0:n], proj[:, KG:KG + 4, 0:n], ek[:, :, 0:n], ALU.mult).then_inc(lev_in, 1)
                dve.wait_ge(lev_in, m + 2)
            add_level(len(LEVELS) + 1)
            for h in range(GH):
                own(dve.tensor_scalar(kendT[:, h, 0:T], cumb[:, h, 0:T], -1.0, cumb[:, h, T - 1:T], ALU.mult, ALU.add))
                b_ = cumb[:, h, T:N].rearrange("p (b x) -> p b x", x=TQ)
                own(dve.tensor_tensor(kendT[:, h, T:N].rearrange("p (b x) -> p b x", x=TQ), b_[:, :, TQ - 1:TQ].broadcast_to([P, DB, TQ]), b_, ALU.subtract))
            dve.sem_inc(exps_in, 1)
            dve.wait_ge(exps_out, 2 * len(LEVELS) + 5)
            own(dve.tensor_tensor(qe[:, :, :], qe[:, :, :], proj[:, QG:QG + 4, T:N], ALU.mult))
            dve.tensor_tensor(kendT, kendT, proj[:, KG:KG + 4, :], ALU.mult).then_inc(kend_in, 1)
            for j in range(8):
                dve.wait_ge(og_mm, j + 1)
                dve.tensor_copy(proj[:, OT + j, :], ps[:, 4 + j % 2, 0:N]).then_inc(og_out, 1)
            dve.wait_ge(og_out, 8)
            with dve.Fori(0, DB // 2) as i:
                own.enter(i, 2)
                for par in range(2):
                    dve.tensor_scalar(vb[par], vnat[0:TS, 2, 0:1024], tokb[:, bass.ds(2 * i + par, 1)], None, ALU.mult).then_inc(vb_done, 1)
                    dve.wait_ge(state_mm, 2 * i + par + 1)
                    dst = proj[:, OT:OT + 8, bass.ds(T + (2 * i + par) * TQ, TQ)]
                    own(dve.tensor_tensor(dst, dst, ps[:, 0, 0:8 * TQ].rearrange("p (j t) -> p j t", t=TQ), ALU.add))
                    for h in range(GH):
                        s_ = states[:, par, h * GDV:(h + 1) * GDV]
                        ins = dve.scalar_tensor_tensor(out=s_, in0=s_, scalar=ebend[:, h, bass.ds(2 * i + par, 1)],
                                                       in1=ps[:, 1 + h // 2, (h % 2) * GDV:(h % 2 + 1) * GDV], op0=ALU.mult, op1=ALU.add)
                    ins.then_inc(state_new, 1)
                own.leave(DB // 2)
            dve.wait_ge(state_new, DB)
            dve.sem_inc(og_raw, 1)
            dve.wait_ge(og_rt, GH)
            own(dve.reciprocal(ek, ek))
            for j in range(8):
                ins = dve.scalar_tensor_tensor(out=proj[:, OT + j, :], in0=proj[:, OT + j, :], scalar=ggla[:, j % 2:j % 2 + 1],
                                               in1=ek[:, j // 2, :], op0=ALU.mult, op1=ALU.mult)
            own(ins)
            dve.wait_ge(silu_done, 1)
            for j in range(8):
                dve.tensor_tensor(proj[:, OT + j, :], proj[:, OT + j, :], proj[:, RG + j, :], ALU.mult).then_inc(og_done, 1)

            for h in range(MH + 1):
                if h < MH:
                    s = h % 2
                    dve.wait_ge(pb_done, h + 1)
                    dve.wait_ge(pq_mm, h + 1)
                    if h >= 2:
                        dve.wait_ge(pt_mm, h - 1)
                    own(dve.scalar_tensor_tensor(out=pprob[s], in0=ps[:, s, 0:384], scalar=SCALE, in1=pbias[s], op0=ALU.mult, op1=ALU.add))
                    dve.tensor_reduce(small[:, 4 * s:4 * s + 1], pprob[s][:, 0:P], AX.X, ALU.max, negate=True)
                    dve.tensor_reduce(small[:, 4 * s + 1:4 * s + 2], pprob[s][:, P:3 * P], AX.X, ALU.max, negate=True).then_inc(pq_s, 1)
                if h >= 1:
                    s = (h - 1) % 2
                    dve.wait_ge(pe_done, 2 * h)
                    own(dve.reciprocal(small[:, 8 + 4 * s:10 + 4 * s], small[:, 8 + 4 * s:10 + 4 * s]))
                    dve.tensor_scalar(pprob[s][:, 0:P], pprob[s][:, 0:P], small[:, 8 + 4 * s:9 + 4 * s], None, ALU.mult)
                    dve.tensor_scalar(pprob[s][:, P:3 * P], pprob[s][:, P:3 * P], small[:, 9 + 4 * s:10 + 4 * s], None, ALU.mult).then_inc(pp_done, 1)

            dve.wait_ge(states_gone, 1)
            dve.wait_ge(pp_done, MH)
            own(dve.memset(st[:, 0:512], 0.0))
            iot, bs, top, idx, idf, sel = (s8[:, 8 * j:8 * j + 8] for j in range(6))
            for j in range(NBLK):
                dve.memset(iot[:, j:j + 1], float(j))

            def queries(b):
                dve.tensor_copy(qpad.rearrange("p (h x) -> p h x", x=TS + TQ)[:, :, 0:TQ],
                                proj[:, QM:QM + MH, bass.ds(T + b * TQ, TQ)]).then_inc(qp_done, 1)

            def softmax(b, before=True, after=True):
                dve.wait_ge(qk_done, b + 1)
                own(dve.tensor_reduce(bs, ps[0:TS, 0:4, :].rearrange("q g (c k) -> q g c k", c=2), AX.X, ALU.add))
                then_plain(dve)
                own(dve.max(top, bs))
                then_plain(dve)
                own(dve.max_index(idx.bitcast(U32), top, bs))
                own(dve.tensor_copy(idf, idx.bitcast(U32)))
                own(dve.tensor_scalar(sel, iot, idf[:, 0:1], None, ALU.is_equal))
                for r in (1, 2):
                    own(dve.scalar_tensor_tensor(out=sel, in0=iot, scalar=idf[:, r:r + 1], in1=sel, op0=ALU.is_equal, op1=ALU.add))
                own(dve.tensor_scalar(sel, sel, -1.0, -NEG, ALU.add, ALU.mult))
                if before:
                    dve.wait_ge(pT_mm, b)
                dve.scalar_tensor_tensor(out=sprob[:, 0:PAST], in0=ps[0:TS, 0:4, :].rearrange("q g k -> q (g k)"), scalar=SCALE,
                                         in1=sbias, op0=ALU.mult, op1=ALU.add)
                own(dve.scalar_tensor_tensor(out=sprob[:, PAST:NS], in0=ps[0:TS, 4, 0:TS], scalar=SCALE,
                                             in1=sown[:, bass.ds(b, 1), :].rearrange("p a k -> p (a k)"), op0=ALU.mult, op1=ALU.add))
                if after:
                    queries(b + 1)
                s_ = sprob[:, 0:PAST].rearrange("q (c k) -> q c k", k=PAST // NBLK)
                own(dve.tensor_tensor(s_, s_, sel.rearrange("q (c o) -> q c o", o=1).broadcast_to([TS, NBLK, PAST // NBLK]), ALU.add))
                dve.tensor_reduce(small[0:TS, 16:17], sprob, AX.X, ALU.max, negate=True).then_inc(sc_out, 1)
                dve.wait_ge(sx_done, b + 1)
                dve.reciprocal(small[0:TS, 18:19], small[0:TS, 17:18]).then_inc(rden_done, 1)

            def heads_out(b):
                dve.wait_ge(sot_mm, b + 1)
                dve.tensor_copy(proj[:, OT + 8:OT + 16, bass.ds(T + b * TQ, TQ)],
                                ps[:, 5, 0:TS].rearrange("p (h t) -> p h t", t=TQ)).then_inc(sot_out, 1)

            queries(0)
            dve.wait_ge(late_in, 48)
            softmax(0, before=False)
            with dve.Fori(1, DB - 1) as b:
                own.enter(b - 1, 10)
                softmax(b)
                heads_out(b - 1)
                own.leave(DB - 2)
            softmax(DB - 1, after=False)
            heads_out(DB - 2)
            heads_out(DB - 1)

            dve.wait_ge(x_again, 16)
            with dve.Fori(0, NOUT // SLOTS) as i:
                for k in range(SLOTS):
                    dve.wait_ge(w_slots_free, (i + W_OUT) * SLOTS + k + 1 + SLOTS)
                    x_ = xT[:, bass.ds(i * SLOTS + k, 1), :].rearrange("p a n -> p (a n)")
                    dve.tensor_tensor(x_, x_, ps[:, k, 0:N], ALU.add).then_inc(banks_free, 1)
            dve.wait_ge(banks_free, SLOTS + NIN + NOUT)
            normalise(2, xT, aT, gffn, normed, False)
            dve.wait_ge(normed, 2)
            dve.wait_ge(banks_free, SLOTS + NIN + NOUT + NPQ)
            for g in range(4):
                dve.tensor_copy(qrep[:, :, g, :], qpT[:, :, T:N]).then_inc(rep_done, 1)
                dve.tensor_copy(crep[:, :, g, :], aT[:, :, T:N]).then_inc(rep_done, 1)
            for j in range(16):
                ins = dve.memset(iota16[:, j:j + 1], float(j))
            own(ins)

            def top16(lists, values, index):
                for r in range(2):
                    at = slice(8 * r, 8 * r + 8)
                    for l, x in enumerate(lists):
                        ins = dve.max(values[l][:, at], x)
                    own(ins)
                    then_plain(dve)
                    for l, x in enumerate(lists):
                        ins = dve.max_index(index[l][:, at], values[l][:, at], x)
                    own(ins)
                    then_plain(dve)
                    if r == 0:
                        for l, x in enumerate(lists):
                            ins = dve.match_replace(x, values[l][:, at], x, LOW)
                        own(ins)
                        then_plain(dve)

            with dve.Fori(0, 3) as t:
                own.enter(t, 24)
                dve.wait_ge(score_out, 4 * t + 4)
                then_plain(dve)
                top16([score[:, l, :] for l in range(16)], [half[:, l, :] for l in range(16)], [halfi[:, l, :] for l in range(16)])
                dve.sem_inc(lists_done, 1)
                dve.tensor_copy(halff, halfi)
                for h in range(PH):
                    ins = dve.tensor_tensor(cand[:, h, :].rearrange("p (i j) -> p i j", j=16),
                                            half[:, h, :].rearrange("p (i o) -> p i o", o=1).broadcast_to([P, 16, 16]),
                                            half[:, PH + h, :].rearrange("p (o j) -> p o j", o=1).broadcast_to([P, 16, 16]), ALU.add)
                own(ins)
                then_plain(dve)
                posh = posu.rearrange("p (h k) -> p h k", k=16)
                top16([cand[:, h, :] for h in range(PH)], [topv[:, h, :] for h in range(PH)], [posh[:, h, :] for h in range(PH)])
                dve.tensor_scalar(posi[0], posu, 4, None, ALU.logical_shift_right)
                own(dve.tensor_scalar(posi[1], posu, 15, None, ALU.bitwise_and))
                for s in range(2):
                    ins = dve.tensor_copy(posf[s], posi[s])
                own(ins)
                for s in range(2):
                    for h in range(PH):
                        ins = dve.tensor_tensor(onehot[:, h], iota16.rearrange("p (o i) -> p o i", o=1).broadcast_to([P, 16, 16]),
                                                posf[s][:, h * 16:(h + 1) * 16].rearrange("p (k o) -> p k o", o=1).broadcast_to([P, 16, 16]), ALU.is_equal)
                    own(ins)
                    for h in range(PH):
                        ins = dve.tensor_tensor(onehot[:, h], onehot[:, h],
                                                halff[:, PH * s + h, :].rearrange("p (o i) -> p o i", o=1).broadcast_to([P, 16, 16]), ALU.mult)
                    own(ins)
                    own(dve.tensor_reduce(exf[s].rearrange("p (h k) -> p h k", k=16), onehot, AX.X, ALU.add))
                own(dve.scalar_tensor_tensor(out=exf[2], in0=exf[0], scalar=float(PKEYS), in1=exf[1], op0=ALU.mult, op1=ALU.add))
                dve.tensor_copy(eidx[:, bass.ds(t * P, P)], exf[2])
                for h in range(PH):
                    ins = dve.tensor_scalar(exf[0][:, h * 16:(h + 1) * 16], topv[:, h, :], topv[:, h, 0:1], None, ALU.subtract)
                own(ins)
                dve.tensor_copy(topv, exf[0].rearrange("p (h k) -> p h k", k=16)).then_inc(gmax_done, 1)
                dve.wait_ge(gexp_done, t + 1)
                own(dve.tensor_reduce(hsum[:, 0:PH], topv, AX.X, ALU.add))
                own(dve.reciprocal(hsum[:, 0:PH], hsum[:, 0:PH]))
                own(dve.tensor_tensor(weight[:, bass.ds(t * P, P)].rearrange("p (h k) -> p h k", k=16), topv,
                                      hsum[:, 0:PH].rearrange("p (h o) -> p h o", o=1).broadcast_to([P, PH, 16]), ALU.mult))
                own.leave(3)
            for g in range(1, 4):
                rows = slice(TS * g, TS * g + TS)
                for x in (eidx, weight):
                    dve.tensor_copy(x[rows, 2 * P:2 * P + TS], x[rows, 2 * P + TS * g:2 * P + TS * g + TS])
            own(dve.memset(hid[:, :], 0.0))
            own(dve.tensor_copy(eidx[:, GT * UNITS:GT * UNITS + UNITS], eidx[:, 0:UNITS]))
            dve.wait_ge(cn_out, 12)
            dve.tensor_copy(now[:, 0, :], eidx[:, 0:UNITS]).then_inc(now_set, 1)

            done = 0
            for t in range(3):
                with dve.Fori(done // 2, (done + G[t]) // 2) as i:
                    for s in range(2):
                        turn_ = 2 * i + s
                        dve.tensor_copy(now[:, 1 - s, :], eidx[:, bass.ds((turn_ + 1) * UNITS, UNITS)]).then_inc(now_set, 1)
                        for k in range(UNITS):
                            dve.wait_ge(row_in[k], (turn_ + 1) * 16)
                            dve.wait_ge(rows_free, (turn_ + 1) * UNITS + k)
                            dve.tensor_tensor_reduce(prod, ring[:, k, :], cnat[:, t, :], 1.0, 0.0, ALU.mult, ALU.add,
                                                     dots[:, k:k + 1]).then_inc(rows_free, 1)
                        dve.wait_ge(rows_free, (turn_ + 2) * UNITS)
                        dve.tensor_copy(hid[:, bass.ds(turn_ * UNITS, UNITS)], dots).then_inc(hid_part, 1)
                        dve.wait_ge(hid_part, turn_ + 1)
                done += G[t]
            dve.sem_inc(hid_done, 1)
            dve.wait_ge(gelu_done, 1)
            dve.tensor_tensor(coef[:, 0:GT * UNITS], weight[:, 0:GT * UNITS], hid[:, 0:GT * UNITS], ALU.mult).then_inc(coef_done, 1)

            def add_back(t):
                lo, n = TT[t]
                dve.wait_ge(yt_mm, t + 1)
                for q in range(4):
                    x_ = xT[:, 4 * q:4 * q + 4, lo:lo + n]
                    ins = dve.tensor_tensor(x_, x_, ps[:, 4 * (t % 2) + q, :].rearrange("p (k n) -> p k n", n=P)[:, :, 0:n], ALU.add)
                ins.then_inc(yt_out, 1)

            done = 0
            for t in range(3):
                with dve.Fori(done // 2, (done + G[t]) // 2) as i:
                    for s in range(2):
                        turn_ = 2 * i + s
                        dve.wait_ge(units_done, turn_ * UNITS + 4)
                        dve.tensor_copy(now[:, 1 - s, :], eidx[:, bass.ds((turn_ + 1) * UNITS, UNITS)]).then_inc(now_set, 1)
                done += G[t]
                if t == 1:
                    add_back(0)
            add_back(1)
            add_back(2)

            with dve.Fori(0, NPLE // SLOTS) as i:
                for k in range(SLOTS):
                    dve.wait_ge(sig_done, i * SLOTS + k + 1)
                    a_, x_ = (r[:, bass.ds(i * SLOTS + k, 1), :].rearrange("p a n -> p (a n)") for r in (aT, xT))
                    dve.tensor_tensor(a_, gate[k], ps[:, 4 + k, 0:N], ALU.mult).then_inc(gate_done, 1)
                    dve.wait_ge(gate_done, SLOTS + i * SLOTS + k + 1)
                    dve.tensor_tensor(a_, a_, x_, ALU.add).then_inc(banks_free, 1)
            dve.wait_ge(banks_free, SLOTS + NIN + NOUT + NPQ + NPLE)
            normalise(3, aT, xT, gfin, y_ready, True)


def _weight_tiles(w):
    r, c = w.shape
    return w.reshape(r // P, P, c // P, P).transpose(2, 1, 0, 3).reshape(c // P, P, -1)


def _features(x):
    return x.T.reshape(-1, P, x.shape[0]).transpose(1, 0, 2)


def _constants():
    s, t = np.arange(P)[:, None], np.arange(P)[None, :]
    masks = [((s >> m) == (t >> m)) & ((s >> (m - 1)) % 2 == 0) & ((t >> (m - 1)) % 2 == 1) for m in LEVELS]
    q, k = np.arange(P)[:, None], np.arange(T)[None, :]
    dist = [np.where(q + P * i >= k, k - q - P * i, NEG) for i in range(2)]
    slope = 2.0 ** (-8.0 * np.arange(1, MH + 1) / MH)
    row_slope, row_q = np.repeat(slope, TQ)[:, None], np.tile(np.arange(TQ), MH)[:, None]
    past = row_slope * (np.arange(PAST)[None, :] - PAST - row_q)
    tok = np.arange(TS)
    own = [np.where((tok // TQ == b) & (tok % TQ <= row_q), row_slope * (tok % TQ - row_q), NEG) for b in range(DB)]
    f = lambda a: np.ascontiguousarray(a, dtype=np.float32)
    return {
        "ident": f(np.eye(P)),
        "masks": f(np.stack(masks, 1)),
        "pdist": f(np.concatenate([dist[0][:, 0:P], dist[1]], 1)),
        "sbias": f(past),
        "sown": f(np.stack(own, 1)),
        "tokb": f(tok[:, None] // TQ == np.arange(DB)),
        "fold": f(np.arange(P)[:, None] % TS == tok),
    }


def kernel(**inputs):
    import concourse.bacc as bacc
    from concourse.bass_utils import run_bass_kernel_spmd

    x = {k: np.asarray(v) for k, v in inputs.items()}
    w_in = x["w_in"][0]
    c = np.cumsum([0, 512, 512, 1024, 1024, RANK, 1024, 1024, 1024])
    col = lambda i: w_in[:, c[i]:c[i + 1]]
    gain = lambda g: g.reshape(-1, P).T
    tokens = np.concatenate([x["x_prompt"].reshape(T, D), x["x_sample"].reshape(TS, D)])
    ple = np.concatenate([x["p_prompt"].reshape(T, PLE), x["p_sample"].reshape(TS, PLE)])
    arrays = {
        "xT": _features(tokens),
        "pleT": _features(ple),
        "w_in": _weight_tiles(np.concatenate([col(0), col(1), col(3), col(2), col(7), col(5), col(6)], 1)),
        "w_z": col(4).reshape(KT, P, RANK).transpose(1, 0, 2),
        "w_gu": x["w_gate_up"][0],
        "b_gate": gain(x["b_gate"][0]),
        "g_mix": gain(x["g_mix"][0]),
        "g_ffn": gain(x["g_ffn"][0]),
        "g_fin": gain(x["g_final"]),
        "g_gla": gain(x["g_gla_out"][0]),
        "w_out": _weight_tiles(x["w_out"][0]),
        "w_pq": _weight_tiles(x["w_peer_q"][0]),
        "w_ple": np.concatenate([_weight_tiles(x["w_ple_gate"][0]), _weight_tiles(x["w_ple_proj"][0])], 2),
        "subk": x["peer_sub_keys"][0].transpose(1, 3, 0, 2).reshape(P, PH, PKEYS),
        "u": x["peer_u"][0],
        "vt": x["peer_v"][0],
        "kT": x["cache_k"][0].transpose(0, 3, 2, 1).reshape(-1, DH, MH * PAGE),
        "v": x["cache_v"][0].reshape(-1, PAGE, MH * DH),
        "pages": x["page_table"].reshape(1, DB * NPG),
        "s0": x["state_gla"][0].transpose(0, 2, 1, 3).reshape(DB, GDK, GH * GDV),
        **_constants(),
    }
    arrays = {"in_" + k: np.ascontiguousarray(v) for k, v in arrays.items()}
    outs = {"y": (P, KT, N), "k_new": (P, MH, N), "v_new": (N, MH * DH), "s_prompt": (GDK, GH * GDV), "s_new": (DB, GDK, GH * GDV)}

    nc = bacc.Bacc("TRN2", target_bir_lowering=False, num_devices=1)
    A = {k[3:]: nc.dram_tensor(k, v.shape, mybir.dt.from_np(v.dtype), kind="ExternalInput").ap() for k, v in arrays.items()}
    O = {k: nc.dram_tensor("out_" + k, list(v), F32, kind="ExternalOutput").ap() for k, v in outs.items()}
    program(nc, A, O)
    r = run_bass_kernel_spmd(nc, [arrays], core_ids=[0]).results[0]

    y = r["out_y"].transpose(2, 1, 0).reshape(N, D)
    k_new = r["out_k_new"].transpose(2, 1, 0)
    v_new = r["out_v_new"].reshape(N, MH, DH)
    state = lambda s: s.reshape(-1, GDK, GH, GDV).transpose(0, 2, 1, 3)[None]
    return (y[:T].reshape(1, T, D), y[T:].reshape(DB, TQ, D), k_new[:T].reshape(1, 1, T, MH, DH),
            v_new[:T].reshape(1, 1, T, MH, DH), state(r["out_s_prompt"]), k_new[T:].reshape(1, DB, TQ, MH, DH),
            v_new[T:].reshape(1, DB, TQ, MH, DH), state(r["out_s_new"]))
```

```python
from contextlib import ExitStack

import numpy as np

import concourse.bass as bass
from concourse import mybir

F32 = mybir.dt.float32
I32 = mybir.dt.int32
U32 = mybir.dt.uint32
ALU = mybir.AluOpType
ACT = mybir.ActivationFunctionType
AX = mybir.AxisListType

P = 128
D = 2048
KT = D // P
T = 256
DB, TQ = 8, 4
TS = DB * TQ
N = T + TS
PAST, PAGE = 2048, 128
NPG = PAST // PAGE
NBLK = PAST // 256
GH, GDK, GDV = 4, 128, 256
MH, DH = 8, 128
RANK = 16
PH, PK, PKEYS = 8, 16, 128
NEXP = PKEYS * PKEYS
HK = PH * PK
PLE = 256
EPS = 1e-6
NEG = -1e30
LOW = -3e38
SCALE = float(DH) ** -0.5

QG, KG, RG, VG, VM, QM, KM = 0, 4, 8, 16, 24, 32, 40
OT = VG
NIN = 48
NMO = 24
GT3 = (NIN - NMO) // DB
NOUT, NPQ, NPLE = 16, 8, 16
SLOTS = 4
WT = KT * P
WP = (KT + PLE // P) * P
UNITS = 8
LEVELS = (1, 2, 3, 4, 5, 6, 7)
NCONST = 12


class Link:

    def __init__(self, eng, sem):
        self.eng, self.sem, self.n, self.turn, self.per = eng, sem, 0, None, 0

    def count(self):
        return self.n if self.turn is None else self.turn * self.per + self.n

    def __call__(self, ins):
        self.n += 1
        ins.then_inc(self.sem, 1)
        self.eng.wait_ge(self.sem, self.count())

    def enter(self, turn, per):
        self.turn, self.per, self.first = turn, per, self.n

    def leave(self, turns):
        assert self.n - self.first == self.per, (self.n - self.first, self.per)
        self.n = self.first + turns * self.per
        self.turn = None


def program(nc, A, O):
    ctx = ExitStack()
    with ctx:
        def sb(name, shape, dt=F32):
            return ctx.enter_context(nc.sbuf_tensor(name, shape, dt))

        def sem(name):
            return ctx.enter_context(nc.semaphore(name))

        xT = sb("xT", [P, KT, N])
        aT = sb("aT", [P, KT, N])
        wring = sb("wring", [P, SLOTS, WP])
        big = sb("big", [P, 28160])
        ident = sb("ident", [P, P])
        ones = sb("ones", [P, P])
        masks = sb("masks", [P, len(LEVELS), P])
        subk = sb("subk", [P, PH, PKEYS])
        states = sb("states", [P, 3, GH * GDV])
        rstd = sb("rstd", [P, N])
        gmix = sb("gmix", [P, KT])
        gffn = sb("gffn", [P, KT])
        gfin = sb("gfin", [P, KT])
        ggla = sb("ggla", [P, 2])
        bgate = sb("bgate", [P, GH])
        pages = sb("pages", [1, DB * NPG], I32)
        small = sb("small", [P, 64])
        ebend = sb("ebend", [P, GH, DB])
        qe = sb("qe", [P, GH, TS])
        tokb = sb("tokb", [TS, DB])
        fold = sb("fold", [P, TS])

        proj = big[:, 0:NIN * N].rearrange("p (j n) -> p j n", n=N)
        vnat = big[:, NIN * N:NIN * N + 3 * D].rearrange("p (t c) -> p t c", c=D)
        kring = big[:, NIN * N + 3 * D:NIN * N + 3 * D + 8 * 1024].rearrange("p (g h k) -> p g h k", g=8, h=MH)
        vring = ([wring[:, SLOTS - 1, j * 1024:(j + 1) * 1024] for j in range(2)] + [states[:, j, :] for j in (1, 2)] +
                 [vnat[:, t, 0:1024] for t in range(3)] + [subk[:, :, :].rearrange("p h k -> p (h k)")])
        flatx = xT[:, :, :].rearrange("p k n -> p (k n)")
        flata = aT[:, :, :].rearrange("p k n -> p (k n)")
        chunk = [r[:, i * GH * N:(i + 1) * GH * N].rearrange("p (h n) -> p h n", n=N)
                 for r in (flatx, flata) for i in range(4)]
        cumb, dist_e, eq, ek = chunk[0:4]
        qk = chunk[4:8]
        st = states[:, :, :].rearrange("p s c -> p (s c)")
        gatt, gatt_s, gatt_top = st[:, 0:1024], st[0:TS, 1024:1152], st[:, 1152:1664]
        gtmp, gtmp_s = st[:, 1664:2688], st[0:TS, 2688:2816]
        kendT = chunk[1]
        kend = flatx[:, 2 * GH * N:2 * GH * N + 3 * 512].rearrange("p (t c) -> p t c", c=512)
        gsp = flata[:, 0:GH * GDV]
        vb = [flata[0:TS, (2 + i) * GH * N:(2 + i) * GH * N + GH * GDV] for i in range(2)]
        pdist = flata[:, 0:384]
        pbias = [flata[:, 384 + i * 384:768 + i * 384] for i in range(2)]
        pprob = [flata[:, 1152 + i * 384:1536 + i * 384] for i in range(2)]
        pprobT = [flata[:, 1920 + i * 384:2304 + i * 384] for i in range(2)]
        late = flatx[:, GH * N:]
        sbias, sprob, sprobT, so = (late[:, a:b] for a, b in ((0, 512), (512, 1024), (1024, 1536), (1536, 2560)))
        sown = late[0:TS, 2560:2560 + DB * TS].rearrange("p (b k) -> p b k", k=TS)
        sownp, sownT = late[0:TS, 2816:2848], late[0:TS, 2848:2880]
        rows = late[:, 2880:3072]
        rowpair = [rows[:, i * TS:(i + 1) * TS] for i in range(2)]
        rowof = [rows[:, (2 + i) * TS:(3 + i) * TS] for i in range(4)]
        torows = late[0:TS, 3072:3072 + 3 * P]
        alike = st[:, 720:720 + P]
        qpad = st[:, 0:MH * 36]
        s8 = st[0:TS, 512:704]
        psum8 = st[:, 704:712]
        cnat = big[:, 0:3 * D].rearrange("p (t c) -> p t c", c=D)
        ring = big[:, 3 * D:3 * D + UNITS * D].rearrange("p (u c) -> p u c", c=D)
        o = 3 * D + UNITS * D
        prod = big[:, o:o + D]
        o += D
        weight = big[:, o:o + 3 * P]
        o += 3 * P
        hid = big[:, o:o + 3 * P]
        o += 3 * P
        eidx = big[:, o:o + 3 * P].bitcast(U32)
        o += 3 * P
        coef = big[:, o:o + 3 * P]
        o += 3 * P
        dots = big[:, o:o + UNITS]
        o += UNITS
        now = big[:, o:o + 2 * UNITS].bitcast(U32).rearrange("p (s u) -> p s u", u=UNITS)
        o += 2 * UNITS
        diag = big[:, o:o + 4 * P].rearrange("p (s c) -> p s c", c=P)
        o += 4 * P
        assert o <= 28160
        r0 = 3 * D
        qpT = big[:, r0:r0 + PH * N].rearrange("p (h n) -> p h n", n=N)
        r0 += PH * N
        score0 = big[:, r0:r0 + 16 * P]
        r0 += 16 * P
        qrep = big[:, r0:r0 + PH * P].rearrange("p (h g n) -> p h g n", g=4, n=TS)
        r0 += PH * P
        crep = big[:, r0:r0 + KT * P].rearrange("p (k g n) -> p k g n", g=4, n=TS)
        assert r0 + KT * P <= 3 * D + UNITS * D
        score = [score0, st[:, 0:16 * P], flata[:, 0:16 * P]]
        topv = st[:, 2560:2560 + 3 * P]
        acc = [flata[:, i * D:(i + 1) * D] for i in range(2)]
        hsum = st[:, 2048:2048 + 3 * PH]
        r0 = o
        two = big[:, r0:r0 + 2 * P].rearrange("p (s k) -> p s k", k=P)
        r0 += 2 * P
        half = big[:, r0:r0 + 32].rearrange("p (s k) -> p s k", k=16)
        r0 += 32
        halfi = big[:, r0:r0 + 32].bitcast(U32).rearrange("p (s k) -> p s k", k=16)
        r0 += 32
        halff = big[:, r0:r0 + 32].rearrange("p (s k) -> p s k", k=16)
        r0 += 32
        cand = big[:, r0:r0 + 256]
        r0 += 256
        onehot = big[:, r0:r0 + 512].rearrange("p (s k i) -> p s k i", k=16, i=16)
        r0 += 512
        top1 = big[:, r0:r0 + 16]
        r0 += 16
        pos1 = big[:, r0:r0 + 16].bitcast(U32)
        r0 += 16
        posi = big[:, r0:r0 + 32].bitcast(U32).rearrange("p (s k) -> p s k", k=16)
        r0 += 32
        posf = big[:, r0:r0 + 32].rearrange("p (s k) -> p s k", k=16)
        r0 += 32
        exf = big[:, r0:r0 + 48].rearrange("p (s k) -> p s k", k=16)
        r0 += 48
        iota16 = big[:, r0:r0 + 16]
        assert r0 + 16 <= 28160
        sq1 = proj[:, 0:KT, :]
        sq = big[:, 3 * D:3 * D + KT * N].rearrange("p (k n) -> p k n", n=N)
        sq2 = big[:, 17000:17000 + KT * N].rearrange("p (k n) -> p k n", n=N)
        pleT = big[:, 0:2 * N].rearrange("p (k n) -> p k n", n=N)
        gate = [big[:, 1024 + i * N:1024 + (i + 1) * N] for i in range(SLOTS)]
        wz = wring[:, 0, WT:WT + KT * RANK].rearrange("p (k r) -> p k r", r=RANK)
        zT = st[0:RANK, 0:N]
        wgu = st[0:RANK, 512:1024]

        ps = ctx.enter_context(nc.psum_tensor("ps", [P, 8, 512], F32))

        epsc = small[:, 20:21]

        def sems(text):
            return [sem(n) for n in text.split()]

        subk_in = sem("subk_in")
        const_in, x_in, x_again, late_in, ple_in = sems("const_in x_in x_again late_in ple_in")
        sums_done, attn_in, gproj_free, gbank_free = sems("sums_done attn_in gproj_free gbank_free")
        gproj_in = [sem(f"gproj_in{j}") for j in range(GT3)]
        w_in = [sem(f"w_in{k}") for k in range(SLOTS)]
        w_slots_free = sem("w_slots_free")
        banks_free = sem("banks_free")
        ones_set, eps_set = sems("ones_set eps_set")
        squares, sum_sq, roots, normed, y_ready = sems("squares sum_sq roots normed y_ready")
        z_done, z_out, gate_mm, gate_out, loga_ln = sems("z_done z_out gate_mm gate_out loga_ln")
        vt_done, vt_out, qg_scaled = sems("vt_done vt_out qg_scaled")
        exps_in, exps_out = sems("exps_in exps_out")
        lev_in, lev_mm, lev_out = sems("lev_in lev_mm lev_out")
        kend_in, kend_t, kend_out = sems("kend_in kend_t kend_out")
        og_mm, og_out, gs_mm, gs_out = sems("og_mm og_out gs_mm gs_out")
        state_in = [sem(f"state_in{i}") for i in range(2)]
        state_out, states_gone, vb_done, state_mm, state_new = sems("state_out states_gone vb_done state_mm state_new")
        og_raw, og_sq, og_ssum, og_rt, silu_done, og_done = sems("og_raw og_sq og_ssum og_rt silu_done og_done")
        pb_done, pq_mm, pq_s, pe_done, pp_done, pt_mm, pt_out, po_mm, po_out = sems(
            "pb_done pq_mm pq_s pe_done pp_done pt_mm pt_out po_mm po_out")
        k_in = [sem(f"k_in{i}") for i in range(2)]
        v_in = [sem(f"v_in{i}") for i in range(4)]
        k_free, v_free = sems("k_free v_free")
        qp_done, qk_done, sc_out, sx_done, rden_done, pT_mm, pT_out, pv_done, so_out, sot_mm, sot_out = sems(
            "qp_done qk_done sc_out sx_done rden_done pT_mm pT_out pv_done so_out sot_mm sot_out")
        psum_in, bsum_mm, sel_in, sel_mm, max_in, max_mm, top_in, top_mm, den_mm = sems(
            "psum_in bsum_mm sel_in sel_mm max_in max_mm top_in top_mm den_mm")
        rep_done, score_mm, score_out, cn_mm, cn_out, gmax_done, gexp_done = sems(
            "rep_done score_mm score_out cn_mm cn_out gmax_done gexp_done")
        row_in = [sem(f"row_in{k}") for k in range(UNITS)]
        now_set, rows_free, hid_part, hid_done, gelu_done, coef_done = sems(
            "now_set rows_free hid_part hid_done gelu_done coef_done")
        diag_set, pe_units, dve_units, acc_done, acc_used, yn_out, yt_mm, yt_out = sems(
            "diag_set pe_units dve_units acc_done acc_used yn_out yt_mm yt_out")
        sig_done, gate_done = sems("sig_done gate_done")
        dve_own, act_own, stored, kv_stored, waits_over = sems("dve_own act_own stored kv_stored waits_over")

        block = ctx.enter_context(nc.Block())
        TT = [(0, P), (P, P), (T, TS)]
        NG = NPG // 4
        G = [P // UNITS, P // UNITS, TS // UNITS]
        GT = sum(G)
        W_OUT, W_PQ, W_PLE = (x // SLOTS for x in (NMO, NMO + NOUT, NMO + NOUT + NPQ))
        n_pages = A["kT"].shape[0]
        ON_DVE = (3, 7)
        ON_PE = tuple(k for k in range(UNITS) if k not in ON_DVE)

        def then_plain(eng):
            eng.sem_inc(waits_over, 1)

        @block.sync
        def _(sp):
            consts = ((ident[:, :], A["ident"]), (masks[:, :, :], A["masks"]),
                      (gmix[:, :], A["g_mix"]), (gffn[:, :], A["g_ffn"]), (gfin[:, :], A["g_fin"]),
                      (ggla[:, :], A["g_gla"]), (bgate[:, :], A["b_gate"]), (pages[:, :], A["pages"]),
                      (wz, A["w_z"]), (wgu, A["w_gu"]), (tokb[:, :], A["tokb"]), (fold[:, :], A["fold"]))
            assert len(consts) == NCONST
            for dst, src in consts:
                sp.dma_start(dst, src).then_inc(const_in, 16)

            def weights(turn, width, src, first):
                for k in range(SLOTS):
                    sp.wait_ge(w_slots_free, (turn + first) * SLOTS + k + 1)
                    sp.dma_start(wring[:, k, 0:width], src[bass.ds(turn * SLOTS + k, 1), :, :]
                                 .rearrange("a p w -> p (a w)")).then_inc(w_in[k], 16)

            def k_pages(b, *groups):
                for g in groups:
                    sp.wait_ge(k_free, b * NG + g + 1)
                    for pg in range(4):
                        page = sp.value_load(pages[0:1, bass.ds(b * NPG + g * 4 + pg, 1)], min_val=0, max_val=n_pages - 1)
                        sp.dma_start(kring[:, (g % 2) * 4 + pg, :, :].rearrange("p h k -> p (h k)"),
                                     A["kT"][bass.ds(page, 1), :, :].rearrange("a p c -> p (a c)")).then_inc(k_in[g % 2], 16)

            def v_pages(b, *pairs):
                for g in pairs:
                    sp.wait_ge(v_free, b * 2 * NG + g + 1)
                    for pg in range(2):
                        page = sp.value_load(pages[0:1, bass.ds(b * NPG + g * 2 + pg, 1)], min_val=0, max_val=n_pages - 1)
                        sp.dma_start(vring[(g % 4) * 2 + pg],
                                     A["v"][bass.ds(page, 1), :, :].rearrange("a p c -> p (a c)")).then_inc(v_in[g % 4], 16)

            def gla_weights(b, j):
                sp.wait_ge(gproj_free, b * GT3 + j + 1)
                sp.dma_start(wring[:, j, 0:WT], A["w_in"][bass.ds(b * GT3 + j, 1), :, :]
                             .rearrange("a p w -> p (a w)")).then_inc(gproj_in[j], 16)

            with sp.Fori(0, NMO // SLOTS) as i:
                for k in range(SLOTS):
                    sp.wait_ge(w_slots_free, i * SLOTS + k + 1)
                    sp.dma_start(wring[:, k, 0:WT], A["w_in"][bass.ds(i * SLOTS + k + NIN - NMO, 1), :, :]
                                 .rearrange("a p w -> p (a w)")).then_inc(w_in[k], 16)
            sp.wait_ge(const_in, 16 * NCONST)
            k_pages(0, 0, 1)
            sp.wait_ge(sums_done, 1)
            for dst, src in ((sbias, "sbias"), (sown, "sown"), (rows, "rows"), (torows, "torows"), (alike, "alike")):
                sp.dma_start(dst, A[src]).then_inc(attn_in, 16)
            for j in range(GT3):
                sp.wait_ge(w_slots_free, NMO + j + 1)
                gla_weights(0, j)
            sp.wait_ge(w_slots_free, NMO + SLOTS)
            k_pages(0, 2, 3)
            sp.wait_ge(vt_out, 6)
            for t, (lo, n) in enumerate(TT):
                sp.dma_start(O["v_new"][lo:lo + n, :], vnat[0:n, t, 1024:2048]).then_inc(kv_stored, 16)
            sp.dma_start(O["k_new"], proj[:, KM:KM + MH, :]).then_inc(kv_stored, 16)
            k_pages(1, 0, 1)

            def request_loads(b, following=True, second=True):
                if following:
                    k_pages(b + 1, 2)
                v_pages(b, 0, 1)
                if following:
                    k_pages(b + 1, 3)
                    gla_weights(b + 1, 0)
                if second:
                    k_pages(b + 2, 0)
                v_pages(b, 2, 3)
                if second:
                    k_pages(b + 2, 1)
                if following:
                    gla_weights(b + 1, 1)
                v_pages(b, 4, 5, 6)
                if following:
                    gla_weights(b + 1, 2)
                v_pages(b, 7)

            with sp.Fori(0, DB - 2) as b:
                request_loads(b)
            request_loads(DB - 2, second=False)
            request_loads(DB - 1, following=False, second=False)
            sp.wait_ge(gproj_free, NIN - NMO + GT3)
            sp.wait_ge(v_free, DB * 2 * NG + 4)
            sp.dma_start(subk[:, :, :], A["subk"]).then_inc(subk_in, 16)
            weights(0, WT, A["w_out"], W_OUT)
            sp.wait_ge(gs_out, 1)
            sp.dma_start(O["s_prompt"], gsp).then_inc(kv_stored, 16)
            sp.wait_ge(kv_stored, 16 * 5)
            sp.wait_ge(og_done, 8)
            sp.wait_ge(state_new, DB)
            sp.dma_start(pdist, A["pdist"]).then_inc(late_in, 16)
            sp.dma_start(xT[:, :, :], A["xT"]).then_inc(x_again, 16)
            with sp.Fori(1, NOUT // SLOTS) as i:
                weights(i, WT, A["w_out"], W_OUT)
            with sp.Fori(0, NPQ // SLOTS) as i:
                weights(i, WT, A["w_pq"], W_PQ)
            weights(0, WP, A["w_ple"], W_PLE)
            sp.wait_ge(yt_out, 3)
            sp.dma_start(pleT, A["pleT"]).then_inc(ple_in, 16)
            with sp.Fori(1, NPLE // SLOTS) as i:
                weights(i, WP, A["w_ple"], W_PLE)
            sp.wait_ge(y_ready, KT)
            sp.dma_start(O["y"], xT[:, :, :]).then_inc(stored, 16)
            sp.wait_ge(stored, 16)

        @block.gpsimd
        def _(pool):
            pool.memset(ones[:, :], 1.0).then_inc(ones_set, 1)

            def state_load(b, par):
                pool.dma_start(states[:, par, :], A["s0"][bass.ds(b, 1), :, :].rearrange("a p c -> p (a c)")).then_inc(state_in[par], 16)

            def state_store(b, par):
                pool.wait_ge(state_new, b + 1)
                then_plain(pool)
                pool.dma_start(O["s_new"][bass.ds(b, 1), :, :].rearrange("a p c -> p (a c)"), states[:, par, :]).then_inc(state_out, 16)
                pool.wait_ge(state_out, (b + 1) * 16)
                then_plain(pool)

            pool.wait_ge(og_out, 8)
            state_load(0, 0)
            state_load(1, 1)
            with pool.Fori(0, DB // 2 - 1) as i:
                for par in range(2):
                    state_store(2 * i + par, par)
                    state_load(2 * i + 2 + par, par)
            for par in range(2):
                state_store(DB - 2 + par, par)
            pool.memset(small[:, 21:22], 0.0).then_inc(states_gone, 1)

            def gather(table, turn, slot, free):
                pool.wait_ge(now_set, turn + 1)
                for k in range(UNITS):
                    pool.wait_ge(*free(k))
                    then_plain(pool)
                    pool.indirect_dma_start(ring[:, k, :], None, table,
                                            bass.IndirectOffsetOnAxis(ap=now[:, slot, k:k + 1], axis=0)).then_inc(row_in[k], 16)

            def after_v(turn):
                return lambda k: ((dve_units, turn * len(ON_DVE) + ON_DVE.index(k) + 1) if k in ON_DVE else
                                  (pe_units, turn * len(ON_PE) + ON_PE.index(k) + 1 + 4))

            with pool.Fori(0, GT // 2) as i:
                for s in range(2):
                    gather(A["u"], 2 * i + s, s, lambda k: (rows_free, (2 * i + s) * UNITS + k + 1))
            gather(A["vt"], GT, 0, lambda k: (rows_free, GT * UNITS + k + 1))
            gather(A["vt"], GT + 1, 1, after_v(0))
            with pool.Fori(1, GT // 2) as i:
                for s in range(2):
                    gather(A["vt"], GT + 2 * i + s, s, after_v(2 * i + s - 1))

        @block.scalar
        def _(act):
            own = Link(act, act_own)
            act.dma_start(xT[:, :, :], A["xT"]).then_inc(x_in, 16)

            def squares_of(src, dst):
                for q in range(4):
                    act.activation(dst[:, 4 * q:4 * q + 4, :], src[:, 4 * q:4 * q + 4, :], ACT.Square).then_inc(squares, 1)

            def root(n):
                act.wait_ge(sum_sq, n)
                act.activation(rstd[:, :], ps[:, 7, 0:N], ACT.Sqrt, bias=epsc, scale=1.0 / D).then_inc(roots, 1)

            def copy_out(i, first, dst):
                for k in range(SLOTS):
                    act.wait_ge(w_slots_free, (i + first) * SLOTS + k + 1 + SLOTS)
                    act.activation(dst[:, bass.ds(i * SLOTS + k, 1), :].rearrange("p a n -> p (a n)"), ps[:, k, 0:N],
                                   ACT.Copy).then_inc(banks_free, 1)

            def values_out(q0):
                for t, (lo, n) in enumerate(TT):
                    for q in range(2):
                        m = 6 * (q0 == 0) + 2 * t + q
                        act.wait_ge(vt_done, m + 1)
                        act.activation(vnat[0:n, t, (q0 + q) * 512:(q0 + q + 1) * 512], ps[0:n, m % 4, :], ACT.Copy).then_inc(vt_out, 1)

            act.wait_ge(eps_set, 1)
            act.wait_ge(x_in, 16)
            squares_of(xT, sq1)
            root(1)
            act.wait_ge(z_done, 1)
            act.activation(zT, ps[0:RANK, 6, 0:N], ACT.Copy).then_inc(z_out, 1)
            act.wait_ge(const_in, 16 * NCONST)
            act.wait_ge(gate_mm, 1)
            for h in range(GH):
                act.activation(eq[:, h, :], ps[:, 4 + h, 0:N],
                               ACT.Identity, bias=bgate[:, h:h + 1]).then_inc(gate_out, 1)
            act.wait_ge(gate_out, GH)
            own(act.activation(ek, eq, ACT.Abs))
            own(act.activation(ek, ek, ACT.Exp, scale=-1.0))
            act.activation(ek, ek, ACT.Ln, bias=1.0).then_inc(loga_ln, 1)
            with act.Fori(0, NMO // SLOTS) as i:
                copy_out(i, 0, proj[:, NIN - NMO:NIN, :])
            values_out(2)
            def gla_out(b, j):
                act.wait_ge(gproj_free, b * GT3 + j + 1 + GT3)
                act.activation(proj[:, bass.ds(b * GT3 + j, 1), :].rearrange("p a n -> p (a n)"), ps[:, 3, 0:N], ACT.Copy).then_inc(gbank_free, 1)

            with act.Fori(0, DB) as b:
                gla_out(b, 0)
                act.wait_ge(sc_out, b + 1)
                act.activation(sprob, sprob, ACT.Exp, bias=small[:, 16:17], accum_out=small[:, 17:18]).then_inc(sx_done, 1)
                act.activation(sownp, sownp, ACT.Exp, bias=small[0:TS, 16:17], accum_out=small[0:TS, 19:20]).then_inc(sx_done, 1)
                gla_out(b, 1)
                act.wait_ge(pT_mm, b + 1)
                act.activation(sprobT, ps[:, 4, :], ACT.Copy).then_inc(pT_out, 1)
                act.activation(sownT, ps[0:TS, 5, 0:TS], ACT.Copy).then_inc(pT_out, 1)
                gla_out(b, 2)
                act.wait_ge(pv_done, b + 1)
                act.wait_ge(rden_done, b + 1)
                act.activation(so[:, 0:512], ps[:, 6, :], ACT.Copy, scale=small[:, 18:19]).then_inc(so_out, 1)
                act.activation(so[:, 512:1024], ps[:, 7, :], ACT.Copy, scale=small[:, 18:19]).then_inc(so_out, 1)
            values_out(0)
            for m in range(len(LEVELS) + 1):
                n = N if m < 2 else T
                act.wait_ge(exps_in, 2 * m + 1)
                act.activation(eq[:, :, 0:n], eq[:, :, 0:n], ACT.Exp).then_inc(exps_out, 1)
                act.wait_ge(exps_in, 2 * m + 2)
                act.activation(ek[:, :, 0:n], ek[:, :, 0:n], ACT.Exp).then_inc(exps_out, 1)
            act.wait_ge(exps_in, 2 * len(LEVELS) + 3)
            act.activation(kendT, kendT, ACT.Exp).then_inc(exps_out, 1)
            act.activation(qe[:, :, :], cumb[:, :, T:N], ACT.Exp).then_inc(exps_out, 1)
            act.activation(ebend[:, :, :], cumb[:, :, T + TQ - 1:N:TQ], ACT.Exp).then_inc(exps_out, 1)
            for t, (lo, n) in enumerate(TT):
                act.wait_ge(kend_t, t + 1)
                act.activation(kend[0:n, t, :], ps[0:n, t, :], ACT.Copy).then_inc(kend_out, 1)
            act.wait_ge(gs_mm, 1)
            own(act.activation(gsp[:, 0:512], ps[:, 6, :], ACT.Copy))
            act.activation(gsp[:, 512:1024], ps[:, 7, :], ACT.Copy).then_inc(gs_out, 1)
            act.wait_ge(og_raw, 1)
            for h in range(GH):
                act.activation(cumb[:, 2 * (h % 2):2 * (h % 2) + 2, :], proj[:, OT + 2 * h:OT + 2 * h + 2, :], ACT.Square).then_inc(og_sq, 1)
                act.wait_ge(og_ssum, h + 1)
                act.activation(ek[:, h, :], ps[:, 4 + h % 2, 0:N], ACT.Sqrt, bias=epsc, scale=1.0 / GDV).then_inc(og_rt, 1)
            act.activation(proj[:, RG:RG + 8, :], proj[:, RG:RG + 8, :], ACT.Silu).then_inc(silu_done, 1)

            act.wait_ge(late_in, 16)
            for h in range(MH + 1):
                if h < MH:
                    s = h % 2
                    if h >= 2:
                        act.wait_ge(pq_s, h - 1)
                    act.activation(pbias[s], pdist, ACT.Copy, scale=2.0 ** (-8.0 * (h + 1) / MH)).then_inc(pb_done, 1)
                    act.wait_ge(pq_s, h + 1)
                    for q, (lo, n) in enumerate(((0, P), (P, 2 * P))):
                        act.activation(pprob[s][:, lo:lo + n], pprob[s][:, lo:lo + n], ACT.Exp, bias=small[:, 4 * s + q:4 * s + q + 1],
                                       accum_out=small[:, 8 + 4 * s + q:9 + 4 * s + q]).then_inc(pe_done, 1)
                if h >= 1:
                    g, s = h - 1, (h - 1) % 2
                    act.wait_ge(pt_mm, g + 1)
                    act.activation(pprobT[s], ps[:, 2 + s, 0:384], ACT.Copy).then_inc(pt_out, 1)
                    act.wait_ge(po_mm, g + 1)
                    act.activation(proj[:, OT + 8 + g, 0:T], ps[:, 4 + s, 0:T], ACT.Copy).then_inc(po_out, 1)

            act.wait_ge(banks_free, SLOTS + NMO + NOUT)
            squares_of(xT, sq)
            root(2)
            with act.Fori(0, NPQ // SLOTS) as i:
                copy_out(i, W_PQ, qpT)
            for t in range(3):
                if t == 1:
                    act.wait_ge(states_gone, 1)
                if t == 2:
                    act.wait_ge(cn_mm, 8)
                for q in range(4):
                    act.wait_ge(score_mm, 4 * t + q + 1)
                    act.activation(score[t][:, q * 512:(q + 1) * 512], ps[:, q, :], ACT.Copy).then_inc(score_out, 1)
                for q in range(4):
                    act.wait_ge(cn_mm, 4 * t + q + 1)
                    act.activation(cnat[:, t, q * 512:(q + 1) * 512], ps[:, 4 + q, :], ACT.Copy).then_inc(cn_out, 1)
            act.wait_ge(gmax_done, 1)
            act.activation(topv, topv, ACT.Exp).then_inc(gexp_done, 1)
            act.wait_ge(hid_done, 1)
            act.activation(hid[:, 0:GT * UNITS], hid[:, 0:GT * UNITS], ACT.Gelu).then_inc(gelu_done, 1)
            act.wait_ge(coef_done, 1)
            done = 0
            for t, (lo, n) in enumerate(TT):
                with act.Fori(done // 2, (done + G[t]) // 2) as i:
                    for s in range(2):
                        for x, k in enumerate(ON_PE):
                            u = (2 * i + s) * len(ON_PE) + x
                            act.wait_ge(pe_units, u + 1)
                            act.activation(diag[:, (s * len(ON_PE) + x) % 4, 0:n], ident[:, :] if t < 2 else fold[:, :], ACT.Copy,
                                           scale=coef[:, bass.ds((2 * i + s) * UNITS + k, 1)]).then_inc(diag_set, 1)
                done += G[t]
                act.wait_ge(acc_used, t + 1)
                if t:
                    act.wait_ge(yt_mm, t)
                for c in range(4):
                    act.activation(prod[0:n, c * 512:(c + 1) * 512], ps[0:n, 4 * (t % 2) + c, :], ACT.Copy).then_inc(yn_out, 1)
            with act.Fori(0, NPLE // SLOTS) as i:
                for k in range(SLOTS):
                    act.wait_ge(w_slots_free, (i + W_PLE) * SLOTS + k + 1 + SLOTS)
                    act.wait_ge(gate_done, i * SLOTS + k + 1)
                    act.activation(gate[k], ps[:, k, 0:N], ACT.Sigmoid).then_inc(sig_done, 1)
            act.wait_ge(banks_free, SLOTS + NMO + NOUT + NPQ + NPLE)
            squares_of(aT, sq2)
            root(3)

        @block.tensor
        def _(pe):
            for s_, n in ((w_slots_free, SLOTS), (banks_free, SLOTS), (k_free, 2), (v_free, 4), (rows_free, UNITS),
                          (pe_units, 4), (gate_done, SLOTS), (sot_out, 1),
                          (gproj_free, GT3), (gbank_free, 1)):
                pe.sem_inc(s_, n)

            def sum_squares(n, src):
                for kt in range(KT):
                    if kt % 4 == 0:
                        pe.wait_ge(squares, 4 * (n - 1) + kt // 4 + 1)
                    mm = pe.matmul(ps[:, 7, 0:N], ones[:, :], src[:, kt, :], start=(kt == 0), stop=(kt == KT - 1))
                mm.then_inc(sum_sq, 1)

            def tiles(i, first, rhs, extra=None):
                for k in range(SLOTS):
                    pe.wait_ge(w_in[k], (i + first + 1) * 16)
                    pe.wait_ge(banks_free, (i + first) * SLOTS + k + 1)
                    for kt in range(KT):
                        mm = pe.matmul(ps[:, k, 0:N], wring[:, k, kt * P:(kt + 1) * P], rhs[:, kt, :],
                                       start=(kt == 0), stop=(kt == KT - 1))
                    if extra is not None:
                        mm = extra(k)
                    mm.then_inc(w_slots_free, 1)

            pe.wait_ge(ones_set, 1)
            sum_squares(1, sq1)
            pe.wait_ge(normed, 1)
            pe.wait_ge(const_in, 16 * NCONST)
            for kt in range(KT):
                mm = pe.matmul(ps[0:RANK, 6, 0:N], wz[:, kt, :], aT[:, kt, :], start=(kt == 0), stop=(kt == KT - 1))
            mm.then_inc(z_done, 1)
            pe.wait_ge(z_out, 1)
            for h in range(GH):
                mm = pe.matmul(ps[:, 4 + h, 0:N], wgu[:, h * P:(h + 1) * P], zT, start=True, stop=True)
            mm.then_inc(gate_mm, 1)
            with pe.Fori(0, NMO // SLOTS) as i:
                tiles(i, 0, aT)

            def turn_values(q0):
                for t, (lo, n) in enumerate(TT):
                    for q in range(2):
                        m = 6 * (q0 == 0) + 2 * t + q
                        if m >= 4:
                            pe.wait_ge(vt_out, m - 3)
                        for f in range(4):
                            mm = pe.transpose(ps[0:n, m % 4, f * P:(f + 1) * P], proj[:, VG + 4 * (q0 + q) + f, lo:lo + n], ident[:, :])
                        mm.then_inc(vt_done, 1)

            pe.wait_ge(banks_free, SLOTS + NMO)
            turn_values(2)
            pe.wait_ge(vt_out, 6)
            def pages_scores(b, g):
                if g == 0:
                    pe.wait_ge(qp_done, b + 1)
                pe.wait_ge(k_in[g % 2], (b * 2 + g // 2 + 1) * 64)
                for h in range(MH):
                    for j in range(4):
                        mm = pe.matmul(ps[j * TS:(j + 1) * TS, 0, g * PAGE:(g + 1) * PAGE], qpad[:, h * TS:(h + 1) * TS],
                                       kring[:, (g % 2) * 4 + j, h, :], start=(h == 0), stop=(h == MH - 1), tile_position=(0, j * TS))
                mm.then_inc(k_free, 1)
                if g == NG - 1:
                    for h in range(MH):
                        mm = pe.matmul(ps[0:TS, 1, 0:TS], qpad[:, h * TS:(h + 1) * TS], proj[:, KM + h, T:N], start=(h == 0), stop=(h == MH - 1))
                    mm.then_inc(qk_done, 1)

            def block_sums(b):
                pe.wait_ge(psum_in, b + 1)
                for a in range(2):
                    mm = pe.matmul(ps[0:TS, 2, a:NBLK:2], rowpair[a], psum8[:, 0:NG], start=True, stop=True)
                mm.then_inc(bsum_mm, 1)

            def masks_back(b):
                pe.wait_ge(sel_in, b + 1)
                for a in range(2):
                    mm = pe.matmul(ps[:, 2, 0:NG], torows[:, a * P:(a + 1) * P], s8[:, 40 + a:48:2], start=(a == 0), stop=(a == 1))
                mm.then_inc(sel_mm, 1)

            def row_maxima(b):
                pe.wait_ge(max_in, b + 1)
                for j in range(4):
                    mm = pe.matmul(ps[0:TS, 2, j:j + 1], rowof[j], psum8[:, 4:5], start=True, stop=True)
                mm.then_inc(max_mm, 1)

            def maximum_back(b):
                pe.wait_ge(top_in, b + 1)
                pe.matmul(ps[:, 2, 0:1], torows[:, 2 * P:3 * P], s8[:, 48:49], start=True, stop=True).then_inc(top_mm, 1)

            def turn(b):
                pe.wait_ge(sx_done, 2 * b + 2)
                then_plain(pe)
                for g in range(NG):
                    pe.transpose(ps[:, 4, g * P:(g + 1) * P], sprob[:, g * PAGE:(g + 1) * PAGE], ident[:, :])
                pe.transpose(ps[0:TS, 5, 0:TS], sownp, ident[0:TS, 0:TS]).then_inc(pT_mm, 1)
                pe.matmul(ps[:, 2, 0:1], alike, small[:, 17:18], start=True, stop=False)
                pe.matmul(ps[:, 2, 0:1], torows[:, 2 * P:3 * P], small[0:TS, 19:20], start=False, stop=True).then_inc(den_mm, 1)

            def gla_tile(b, j, second):
                if not second:
                    pe.wait_ge(gproj_in[j], (b + 1) * 16)
                    pe.wait_ge(gbank_free, b * GT3 + j + 1)
                for kt in range(KT // 2 * second, KT // 2 * (1 + second)):
                    mm = pe.matmul(ps[:, 3, 0:N], wring[:, j, kt * P:(kt + 1) * P], aT[:, kt, :],
                                   start=(kt == 0), stop=(kt == KT - 1))
                if second:
                    mm.then_inc(gproj_free, 1)

            def values(b):
                pe.wait_ge(pT_out, 2 * b + 2)
                for g in range(2 * NG):
                    if g == NG:
                        gla_tile(b, 2, 1)
                    pe.wait_ge(v_in[g % 4], (b * 2 + g // 4 + 1) * 32)
                    for c in range(2):
                        for pg in range(2):
                            j = 2 * (g % 2) + pg
                            mm = pe.matmul(ps[j * TS:(j + 1) * TS, 6 + c, :], sprobT[:, (g // 2) * P + j * TS:(g // 2) * P + (j + 1) * TS],
                                           vring[2 * (g % 4) + pg][:, c * 512:(c + 1) * 512], start=(g < 2), stop=(g >= 2 * NG - 2 and j > 0),
                                           tile_position=(0, j * TS))
                    mm.then_inc(v_free, 1)
                for c in range(2):
                    mm = pe.matmul(ps[0:TS, 6 + c, :], sownT, vnat[0:TS, 2, 1024 + c * 512:1024 + (c + 1) * 512], start=False, stop=True)
                mm.then_inc(pv_done, 1)

            def own_heads(b):
                pe.wait_ge(so_out, 2 * b + 2)
                pe.wait_ge(sot_out, b + 1)
                for h in range(MH):
                    mm = pe.matmul(ps[:, 1, TS + h * TQ:TS + (h + 1) * TQ], so[:, h * DH:(h + 1) * DH], fold[:, h * TQ:(h + 1) * TQ], start=True, stop=True)
                mm.then_inc(sot_mm, 1)

            def request(b, heads=True, following=True):
                steps = [block_sums, masks_back, row_maxima, maximum_back]
                for g in range(NG):
                    if following:
                        pages_scores(b + 1, g)
                    if g == 1:
                        gla_tile(b, 0, 1)
                    if g == 2:
                        gla_tile(b, 1, 0)
                    steps[g](b)
                    if g == 0:
                        gla_tile(b, 0, 0)
                if heads:
                    own_heads(b - 1)
                gla_tile(b, 1, 1)
                turn(b)
                gla_tile(b, 2, 0)
                values(b)

            for g in range(NG):
                pages_scores(0, g)
            request(0, heads=False)
            with pe.Fori(1, DB - 1) as b:
                request(b)
            request(DB - 1, following=False)
            own_heads(DB - 1)
            pe.wait_ge(sot_out, DB + 1)

            pe.wait_ge(gbank_free, 1 + NIN - NMO)
            turn_values(0)
            pe.wait_ge(vt_out, 12)
            for m in range(len(LEVELS) + 2):
                par = m % 2
                pe.wait_ge(lev_in, m + 1)
                if m >= 2:
                    pe.wait_ge(lev_out, m - 1)
                q_, k_ = (qk[2 * par], qk[2 * par + 1]) if m else (proj[:, QG:QG + 4, :], proj[:, KG:KG + 4, :])
                if m == len(LEVELS) + 1:
                    for h in range(GH):
                        mm = pe.matmul(ps[:, 3 * par, h * P:(h + 1) * P], k_[:, h, 0:P], q_[:, h, P:T], start=True, stop=True)
                else:
                    for t in range(2):
                        for h in range(GH):
                            mm = pe.matmul(ps[:, 3 * par + t, h * P:(h + 1) * P], k_[:, h, t * P:(t + 1) * P],
                                           q_[:, h, t * P:(t + 1) * P], start=True, stop=True)
                if m <= 2:
                    for h in range(GH):
                        mm = pe.matmul(ps[0:TS, 3 * par + 2, h * TS:(h + 1) * TS], k_[:, h, T:N], q_[:, h, T:N], start=True, stop=True)
                mm.then_inc(lev_mm, 1)
            pe.wait_ge(lev_out, len(LEVELS) + 2)
            pe.wait_ge(kend_in, 1)
            for t, (lo, n) in enumerate(TT):
                for h in range(GH):
                    mm = pe.transpose(ps[0:n, t, h * P:(h + 1) * P], kendT[:, h, lo:lo + n], ident[:, :])
                mm.then_inc(kend_t, 1)
            pe.wait_ge(kend_out, 3)
            for h in range(GH):
                for t in range(2):
                    mm = pe.matmul(ps[:, 6 + h // 2, (h % 2) * GDV:(h % 2 + 1) * GDV], kend[:, t, h * P:(h + 1) * P],
                                   vnat[:, t, h * GDV:(h + 1) * GDV], start=(t == 0), stop=(t == 1))
            mm.then_inc(gs_mm, 1)
            for j in range(8):
                h, c = j // 2, j % 2
                if j >= 2:
                    pe.wait_ge(og_out, j - 1)
                bank = 4 + j % 2
                v0, v1, v2 = (vnat[0:n, t, h * GDV + c * P:h * GDV + (c + 1) * P] for t, (_, n) in enumerate(TT))
                pe.matmul(ps[:, bank, T:N], v2, gatt_s[:, h * TS:(h + 1) * TS], start=True, stop=True)
                pe.matmul(ps[:, bank, 0:P], v0, gatt[:, h * P:(h + 1) * P], start=True, stop=True)
                pe.matmul(ps[:, bank, P:T], v0, gatt_top[:, h * P:(h + 1) * P], start=True, stop=False)
                pe.matmul(ps[:, bank, P:T], v1, gatt[:, 512 + h * P:512 + (h + 1) * P], start=False, stop=True).then_inc(og_mm, 1)
            with pe.Fori(0, DB // 2) as i:
                for par in range(2):
                    pe.wait_ge(state_in[par], (i + 1) * 16)
                    pe.wait_ge(vb_done, 2 * i + par + 1)
                    for j in range(8):
                        pe.matmul(ps[:, 0, j * TQ:(j + 1) * TQ], states[:, par, (j // 2) * GDV + (j % 2) * P:(j // 2) * GDV + (j % 2 + 1) * P],
                                  qe[:, j // 2, bass.ds((2 * i + par) * TQ, TQ)], start=True, stop=True)
                    for h in range(GH):
                        mm = pe.matmul(ps[:, 1 + h // 2, (h % 2) * GDV:(h % 2 + 1) * GDV], kend[0:TS, 2, h * P:(h + 1) * P],
                                       vb[par][:, h * GDV:(h + 1) * GDV], start=True, stop=True)
                    mm.then_inc(state_mm, 1)
            for h in range(GH):
                pe.wait_ge(og_sq, h + 1)
                for c in range(2):
                    mm = pe.matmul(ps[:, 4 + h % 2, 0:N], ones[:, :], cumb[:, 2 * (h % 2) + c, :], start=(c == 0), stop=(c == 1))
                mm.then_inc(og_ssum, 1)

            pe.wait_ge(gs_out, 1)
            pe.wait_ge(og_rt, GH)
            for h in range(MH + 1):
                if h < MH:
                    s = h % 2
                    if h >= 2:
                        pe.wait_ge(pq_s, h - 1)
                    pe.matmul(ps[:, s, 0:P], proj[:, QM + h, 0:P], proj[:, KM + h, 0:P], start=True, stop=True)
                    pe.matmul(ps[:, s, P:3 * P], proj[:, QM + h, P:T], proj[:, KM + h, 0:T], start=True, stop=True).then_inc(pq_mm, 1)
                if h >= 1:
                    g, s = h - 1, (h - 1) % 2
                    pe.wait_ge(pp_done, g + 1)
                    for c in range(3):
                        mm = pe.transpose(ps[:, 2 + s, c * P:(c + 1) * P], pprob[s][:, c * P:(c + 1) * P], ident[:, :])
                    mm.then_inc(pt_mm, 1)
                    pe.wait_ge(pt_out, g + 1)
                    v0, v1 = (vnat[:, t, 1024 + g * DH:1024 + (g + 1) * DH] for t in range(2))
                    pe.matmul(ps[:, 4 + s, 0:P], v0, pprobT[s][:, 0:P], start=True, stop=True)
                    pe.matmul(ps[:, 4 + s, P:T], v0, pprobT[s][:, P:2 * P], start=True, stop=False)
                    pe.matmul(ps[:, 4 + s, P:T], v1, pprobT[s][:, 2 * P:3 * P], start=False, stop=True).then_inc(po_mm, 1)

            pe.wait_ge(po_out, MH)
            with pe.Fori(0, NOUT // SLOTS) as i:
                tiles(i, W_OUT, proj[:, OT:OT + KT, :])
            sum_squares(2, sq)
            pe.wait_ge(normed, 2)
            with pe.Fori(0, NPQ // SLOTS) as i:
                tiles(i, W_PQ, aT)
            pe.wait_ge(banks_free, SLOTS + NMO + NOUT + NPQ)
            pe.wait_ge(roots, 2)
            pe.wait_ge(subk_in, 16)
            for t, (lo, n) in enumerate(TT):
                if t == 2:
                    pe.wait_ge(rep_done, 8)
                for q in range(4):
                    if t:
                        pe.wait_ge(score_out, 4 * (t - 1) + q + 1)
                    for f in range(4):
                        h, hf = 4 * (q % 2) + f, q // 2
                        rows = slice(64 * hf, 64 * hf + 64)
                        lhs = qpT[rows, h, lo:lo + n] if t < 2 else qrep[rows, h, :, :].rearrange("p g n -> p (g n)")
                        mm = pe.matmul(ps[:, q, f * P:(f + 1) * P], lhs, subk[rows, h, :], start=True, stop=True)
                    mm.then_inc(score_mm, 1)
                for q in range(4):
                    if t:
                        pe.wait_ge(cn_out, 4 * (t - 1) + q + 1)
                    for f in range(4):
                        kt = 4 * q + f
                        src = aT[:, kt, lo:lo + n] if t < 2 else crep[:, kt, :, :].rearrange("p g n -> p (g n)")
                        mm = pe.transpose(ps[:, 4 + q, f * P:(f + 1) * P], src, ident[:, :])
                    mm.then_inc(cn_mm, 1)

            def unit(w, b0, turn_, s, x, first=False):
                pe.wait_ge(diag_set, turn_ * len(ON_PE) + x + 1)
                pe.wait_ge(row_in[ON_PE[x]], (turn_ + GT + 1) * 16)
                for c in range(4):
                    mm = pe.matmul(ps[0:w, b0 + c, :], diag[:, (s * len(ON_PE) + x) % 4, 0:w], ring[:, ON_PE[x], c * 512:(c + 1) * 512],
                                   start=first, stop=False, skip_group_check=True)
                mm.then_inc(pe_units, 1)

            def back(t):
                b0, n = 4 * (t % 2), TT[t][1]
                pe.wait_ge(yn_out, 4 * t + 4)
                for kt in range(KT):
                    mm = pe.transpose(ps[:, b0 + kt // 4, (kt % 4) * P:(kt % 4) * P + n], prod[0:n, kt * P:(kt + 1) * P], ident[0:n, 0:n])
                mm.then_inc(yt_mm, 1)

            pe.wait_ge(cn_out, 12)
            done = 0
            for t, (lo, w) in enumerate(TT):
                b0 = 4 * (t % 2)
                if t == 2:
                    pe.wait_ge(yt_out, 1)
                for s in range(2):
                    for x in range(len(ON_PE)):
                        unit(w, b0, done + s, s, x, first=(s == 0 and x == 0))
                with pe.Fori(done // 2 + 1, (done + G[t]) // 2) as i:
                    for s in range(2):
                        for x in range(len(ON_PE)):
                            unit(w, b0, 2 * i + s, s, x)
                pe.wait_ge(acc_done, t + 1)
                for c in range(4):
                    mm = pe.matmul(ps[0:w, b0 + c, :], ident[:, :] if t < 2 else fold[:, :], acc[t % 2][:, c * 512:(c + 1) * 512],
                                   start=False, stop=True, skip_group_check=True)
                mm.then_inc(acc_used, 1)
                done += G[t]
                if t == 1:
                    back(0)
            back(1)
            back(2)

            pe.wait_ge(yt_out, 3)
            pe.wait_ge(ple_in, 16)

            def embed(k):
                for kt in range(PLE // P):
                    mm = pe.matmul(ps[:, 4 + k, 0:N], wring[:, k, WT + kt * P:WT + (kt + 1) * P], pleT[:, kt, :],
                                   start=(kt == 0), stop=(kt == PLE // P - 1))
                return mm

            with pe.Fori(0, NPLE // SLOTS) as i:
                tiles(i, W_PLE, xT, embed)
            sum_squares(3, sq2)

        @block.vector
        def _(dve):
            own = Link(dve, dve_own)
            dve.memset(epsc, EPS).then_inc(eps_set, 1)

            def normalise(n, src, dst, gain, then, each):
                dve.wait_ge(roots, n)
                own(dve.reciprocal(rstd[:, :], rstd[:, :]))
                for kt in range(KT):
                    ins = dve.scalar_tensor_tensor(out=dst[:, kt, :], in0=src[:, kt, :], scalar=gain[:, kt:kt + 1],
                                                   in1=rstd[:, :], op0=ALU.mult, op1=ALU.mult)
                    if each or kt == KT - 1:
                        ins.then_inc(then, 1)

            dve.wait_ge(const_in, 16 * NCONST)
            dve.wait_ge(x_in, 16)
            normalise(1, xT, aT, gmix, normed, False)
            dve.wait_ge(gate_out, GH)
            own(dve.tensor_scalar(dist_e, eq, 0.0, 1.0 / 16, ALU.min, ALU.mult))
            dve.wait_ge(loga_ln, 1)
            own(dve.scalar_tensor_tensor(out=dist_e, in0=ek, scalar=-1.0 / 16, in1=dist_e, op0=ALU.mult, op1=ALU.add))
            dve.wait_ge(ones_set, 1)
            for lo in (0, P):
                for h in range(GH):
                    ins = dve.tensor_tensor_scan(cumb[:, h, lo:lo + P], ones[:, :], dist_e[:, h, lo:lo + P],
                                                 0.0 if lo == 0 else cumb[:, h, P - 1:P], ALU.mult, ALU.add)
                own(ins)
            own(dve.tensor_copy(cumb[:, :, T:N:TQ], dist_e[:, :, T:N:TQ]))
            for j in range(1, TQ):
                own(dve.tensor_tensor(cumb[:, :, T + j:N:TQ], cumb[:, :, T + j - 1:N:TQ], dist_e[:, :, T + j:N:TQ], ALU.add))
            dve.sem_inc(sums_done, 1)
            dve.wait_ge(banks_free, SLOTS + NMO)
            own(dve.memset(st[:, 0:512], 0.0))
            iot, bs, top, idx, idf, sel = (s8[:, 8 * j:8 * j + 8] for j in range(6))
            negmax, ownmax = s8[:, 48:49], s8[:, 49:50]
            for j in range(NBLK):
                dve.memset(iot[:, j:j + 1], float(j))

            def queries(b):
                dve.tensor_copy(qpad.rearrange("p (h x) -> p h x", x=TS + TQ)[:, :, 0:TQ],
                                proj[:, QM:QM + MH, bass.ds(T + b * TQ, TQ)]).then_inc(qp_done, 1)

            def softmax(b, before=True, after=True):
                dve.wait_ge(qk_done, b + 1)
                dve.tensor_reduce(psum8[:, 0:NG], ps[:, 0, :].rearrange("q (g k) -> q g k", k=PAGE), AX.X, ALU.add).then_inc(psum_in, 1)
                if before:
                    dve.wait_ge(pT_mm, b)
                dve.scalar_tensor_tensor(out=sprob, in0=ps[:, 0, :], scalar=SCALE, in1=sbias, op0=ALU.mult, op1=ALU.add)
                own(dve.scalar_tensor_tensor(out=sownp, in0=ps[0:TS, 1, 0:TS], scalar=SCALE,
                                             in1=sown[:, bass.ds(b, 1), :].rearrange("p a k -> p (a k)"), op0=ALU.mult, op1=ALU.add))
                if after:
                    queries(b + 1)
                own(dve.tensor_reduce(ownmax, sownp, AX.X, ALU.max))
                dve.wait_ge(bsum_mm, b + 1)
                own(dve.tensor_copy(bs, ps[0:TS, 2, 0:NBLK]))
                then_plain(dve)
                own(dve.max(top, bs))
                then_plain(dve)
                own(dve.max_index(idx.bitcast(U32), top, bs))
                own(dve.tensor_copy(idf, idx.bitcast(U32)))
                own(dve.tensor_scalar(sel, iot, idf[:, 0:1], None, ALU.is_equal))
                for r in (1, 2):
                    own(dve.scalar_tensor_tensor(out=sel, in0=iot, scalar=idf[:, r:r + 1], in1=sel, op0=ALU.is_equal, op1=ALU.add))
                dve.tensor_scalar(sel, sel, -1.0, -NEG, ALU.add, ALU.mult).then_inc(sel_in, 1)
                dve.wait_ge(sel_mm, b + 1)
                s_ = sprob.rearrange("q (g k) -> q g k", k=PAGE)
                own(dve.tensor_tensor(s_, s_, ps[:, 2, 0:NG].rearrange("q (g o) -> q g o", o=1).broadcast_to([P, NG, PAGE]), ALU.add))
                dve.tensor_reduce(psum8[:, 4:5], sprob, AX.X, ALU.max).then_inc(max_in, 1)
                dve.wait_ge(max_mm, b + 1)
                own(dve.tensor_reduce(negmax, ps[0:TS, 2, 0:4], AX.X, ALU.max))
                dve.tensor_scalar(negmax, negmax, ownmax, -1.0, ALU.max, ALU.mult).then_inc(top_in, 1)
                dve.wait_ge(top_mm, b + 1)
                dve.tensor_copy(small[:, 16:17], ps[:, 2, 0:1]).then_inc(sc_out, 1)
                dve.wait_ge(den_mm, b + 1)
                dve.reciprocal(small[:, 18:19], ps[:, 2, 0:1]).then_inc(rden_done, 1)

            def heads_out(b):
                dve.wait_ge(sot_mm, b + 1)
                dve.tensor_copy(proj[:, OT + 8:OT + 16, bass.ds(T + b * TQ, TQ)],
                                ps[:, 1, TS:2 * TS].rearrange("p (h t) -> p h t", t=TQ)).then_inc(sot_out, 1)

            queries(0)
            dve.wait_ge(attn_in, 80)
            softmax(0, before=False)
            with dve.Fori(1, DB - 1) as b:
                own.enter(b - 1, 11)
                softmax(b)
                heads_out(b - 1)
                own.leave(DB - 2)
            softmax(DB - 1, after=False)
            heads_out(DB - 2)
            heads_out(DB - 1)

            dve.wait_ge(gbank_free, 1 + NIN - NMO)
            dve.tensor_scalar(proj[:, QG:QG + 4, :], proj[:, QG:QG + 4, :], float(GDK) ** -0.5, None, ALU.mult).then_inc(lev_in, 1)
            dve.wait_ge(lev_in, 1)

            def add_level(m):
                b0 = 3 * (m % 2)
                dve.wait_ge(lev_mm, m + 1)
                if m == len(LEVELS) + 1:
                    dve.tensor_copy(gatt_top, ps[:, b0, :]).then_inc(lev_out, 1)
                    return
                mask = ident if m == 0 else masks[:, m - 1, :]
                v = lambda a, w: a.rearrange("p (h t) -> p h t", t=w)
                for c in range(3 if m <= 2 else 2):
                    n, w = (P, P) if c < 2 else (TS, TS)
                    to = gatt[:, c * 512:(c + 1) * 512] if c < 2 else gatt_s
                    tmp = gtmp[:, c * 512:(c + 1) * 512] if c < 2 else gtmp_s
                    mk = mask[0:n, 0:w].rearrange("p (o t) -> p o t", o=1).broadcast_to([n, GH, w])
                    own(dve.tensor_tensor(v(to if m == 0 else tmp, w), v(ps[0:n, b0 + c, 0:GH * w], w), mk, ALU.mult))
                    if m:
                        own(dve.tensor_tensor(to, to, tmp, ALU.add))
                dve.sem_inc(lev_out, 1)

            for m in range(len(LEVELS) + 1):
                B = 2 << m
                n = N if m < 2 else T
                blocks = lambda a: a.rearrange("p (c x) -> p c x", x=B)
                par = (m + 1) % 2
                for h in range(GH):
                    src = blocks(cumb[:, h, 0:n])
                    ins = dve.tensor_tensor(blocks(dist_e[:, h, 0:n]), src, src[:, :, B // 2 - 1:B // 2].broadcast_to([P, n // B, B]), ALU.subtract)
                own(ins)
                dve.tensor_scalar(eq[:, :, 0:n], dist_e[:, :, 0:n], 0.0, None, ALU.min).then_inc(exps_in, 1)
                dve.tensor_scalar(ek[:, :, 0:n], dist_e[:, :, 0:n], -1.0, 0.0, ALU.mult, ALU.min).then_inc(exps_in, 1)
                add_level(m)
                dve.wait_ge(exps_out, 2 * m + 2)
                own(dve.tensor_tensor(qk[2 * par][:, :, 0:n], proj[:, QG:QG + 4, 0:n], eq[:, :, 0:n], ALU.mult))
                dve.tensor_tensor(qk[2 * par + 1][:, :, 0:n], proj[:, KG:KG + 4, 0:n], ek[:, :, 0:n], ALU.mult).then_inc(lev_in, 1)
                dve.wait_ge(lev_in, m + 2)
            add_level(len(LEVELS) + 1)
            for h in range(GH):
                own(dve.tensor_scalar(kendT[:, h, 0:T], cumb[:, h, 0:T], -1.0, cumb[:, h, T - 1:T], ALU.mult, ALU.add))
                b_ = cumb[:, h, T:N].rearrange("p (b x) -> p b x", x=TQ)
                own(dve.tensor_tensor(kendT[:, h, T:N].rearrange("p (b x) -> p b x", x=TQ), b_[:, :, TQ - 1:TQ].broadcast_to([P, DB, TQ]), b_, ALU.subtract))
            dve.sem_inc(exps_in, 1)
            dve.wait_ge(exps_out, 2 * len(LEVELS) + 5)
            own(dve.tensor_tensor(qe[:, :, :], qe[:, :, :], proj[:, QG:QG + 4, T:N], ALU.mult))
            dve.tensor_tensor(kendT, kendT, proj[:, KG:KG + 4, :], ALU.mult).then_inc(kend_in, 1)
            for j in range(8):
                dve.wait_ge(og_mm, j + 1)
                dve.tensor_copy(proj[:, OT + j, :], ps[:, 4 + j % 2, 0:N]).then_inc(og_out, 1)
            dve.wait_ge(og_out, 8)
            with dve.Fori(0, DB // 2) as i:
                own.enter(i, 2)
                for par in range(2):
                    dve.tensor_scalar(vb[par], vnat[0:TS, 2, 0:1024], tokb[:, bass.ds(2 * i + par, 1)], None, ALU.mult).then_inc(vb_done, 1)
                    dve.wait_ge(state_mm, 2 * i + par + 1)
                    dst = proj[:, OT:OT + 8, bass.ds(T + (2 * i + par) * TQ, TQ)]
                    own(dve.tensor_tensor(dst, dst, ps[:, 0, 0:8 * TQ].rearrange("p (j t) -> p j t", t=TQ), ALU.add))
                    for h in range(GH):
                        s_ = states[:, par, h * GDV:(h + 1) * GDV]
                        ins = dve.scalar_tensor_tensor(out=s_, in0=s_, scalar=ebend[:, h, bass.ds(2 * i + par, 1)],
                                                       in1=ps[:, 1 + h // 2, (h % 2) * GDV:(h % 2 + 1) * GDV], op0=ALU.mult, op1=ALU.add)
                    ins.then_inc(state_new, 1)
                own.leave(DB // 2)
            dve.wait_ge(state_new, DB)
            dve.sem_inc(og_raw, 1)
            dve.wait_ge(og_rt, GH)
            own(dve.reciprocal(ek, ek))
            for j in range(8):
                ins = dve.scalar_tensor_tensor(out=proj[:, OT + j, :], in0=proj[:, OT + j, :], scalar=ggla[:, j % 2:j % 2 + 1],
                                               in1=ek[:, j // 2, :], op0=ALU.mult, op1=ALU.mult)
            own(ins)
            dve.wait_ge(silu_done, 1)
            for j in range(8):
                dve.tensor_tensor(proj[:, OT + j, :], proj[:, OT + j, :], proj[:, RG + j, :], ALU.mult).then_inc(og_done, 1)

            for h in range(MH + 1):
                if h < MH:
                    s = h % 2
                    dve.wait_ge(pb_done, h + 1)
                    dve.wait_ge(pq_mm, h + 1)
                    if h >= 2:
                        dve.wait_ge(pt_mm, h - 1)
                    own(dve.scalar_tensor_tensor(out=pprob[s], in0=ps[:, s, 0:384], scalar=SCALE, in1=pbias[s], op0=ALU.mult, op1=ALU.add))
                    dve.tensor_reduce(small[:, 4 * s:4 * s + 1], pprob[s][:, 0:P], AX.X, ALU.max, negate=True)
                    dve.tensor_reduce(small[:, 4 * s + 1:4 * s + 2], pprob[s][:, P:3 * P], AX.X, ALU.max, negate=True).then_inc(pq_s, 1)
                if h >= 1:
                    s = (h - 1) % 2
                    dve.wait_ge(pe_done, 2 * h)
                    own(dve.reciprocal(small[:, 8 + 4 * s:10 + 4 * s], small[:, 8 + 4 * s:10 + 4 * s]))
                    dve.tensor_scalar(pprob[s][:, 0:P], pprob[s][:, 0:P], small[:, 8 + 4 * s:9 + 4 * s], None, ALU.mult)
                    dve.tensor_scalar(pprob[s][:, P:3 * P], pprob[s][:, P:3 * P], small[:, 9 + 4 * s:10 + 4 * s], None, ALU.mult).then_inc(pp_done, 1)

            dve.wait_ge(x_again, 16)
            with dve.Fori(0, NOUT // SLOTS) as i:
                for k in range(SLOTS):
                    dve.wait_ge(w_slots_free, (i + W_OUT) * SLOTS + k + 1 + SLOTS)
                    x_ = xT[:, bass.ds(i * SLOTS + k, 1), :].rearrange("p a n -> p (a n)")
                    dve.tensor_tensor(x_, x_, ps[:, k, 0:N], ALU.add).then_inc(banks_free, 1)
            dve.wait_ge(banks_free, SLOTS + NMO + NOUT)
            normalise(2, xT, aT, gffn, normed, False)
            dve.wait_ge(normed, 2)
            dve.wait_ge(banks_free, SLOTS + NMO + NOUT + NPQ)
            for g in range(4):
                dve.tensor_copy(qrep[:, :, g, :], qpT[:, :, T:N]).then_inc(rep_done, 1)
                dve.tensor_copy(crep[:, :, g, :], aT[:, :, T:N]).then_inc(rep_done, 1)
            for j in range(16):
                ins = dve.memset(iota16[:, j:j + 1], float(j))
            own(ins)

            def top16(lists, values, index):
                for r in range(2):
                    at = slice(8 * r, 8 * r + 8)
                    for l, x in enumerate(lists):
                        ins = dve.max(values[l][:, at], x)
                    own(ins)
                    then_plain(dve)
                    for l, x in enumerate(lists):
                        ins = dve.max_index(index[l][:, at], values[l][:, at], x)
                    own(ins)
                    then_plain(dve)
                    if r == 0:
                        for l, x in enumerate(lists):
                            ins = dve.match_replace(x, values[l][:, at], x, LOW)
                        own(ins)
                        then_plain(dve)

            def top_head(t, h):
                own(dve.tensor_copy(two, score[t].rearrange("p (s h k) -> p s h k", s=2, k=P)[:, :, bass.ds(h, 1), :]
                                    .rearrange("p s a k -> p s (a k)")))
                then_plain(dve)
                top16([two[:, s] for s in range(2)], [half[:, s] for s in range(2)], [halfi[:, s] for s in range(2)])
                dve.tensor_copy(halff, halfi)
                own(dve.tensor_tensor(cand.rearrange("p (i j) -> p i j", j=16),
                                      half[:, 0, :].rearrange("p (i o) -> p i o", o=1).broadcast_to([P, 16, 16]),
                                      half[:, 1, :].rearrange("p (o j) -> p o j", o=1).broadcast_to([P, 16, 16]), ALU.add))
                then_plain(dve)
                top16([cand], [top1], [pos1])
                dve.tensor_scalar(posi[:, 0], pos1, 4, None, ALU.logical_shift_right)
                dve.tensor_copy(topv[:, bass.ds(t * P + h * PK, PK)], top1)
                own(dve.tensor_scalar(posi[:, 1], pos1, 15, None, ALU.bitwise_and))
                own(dve.tensor_copy(posf, posi))
                for s in range(2):
                    ins = dve.tensor_tensor(onehot[:, s], iota16.rearrange("p (o i) -> p o i", o=1).broadcast_to([P, 16, 16]),
                                            posf[:, s].rearrange("p (k o) -> p k o", o=1).broadcast_to([P, 16, 16]), ALU.is_equal)
                own(ins)
                for s in range(2):
                    ins = dve.tensor_tensor(onehot[:, s], onehot[:, s], halff[:, s].rearrange("p (o i) -> p o i", o=1).broadcast_to([P, 16, 16]), ALU.mult)
                own(ins)
                own(dve.tensor_reduce(exf[:, 0:2], onehot, AX.X, ALU.add))
                own(dve.scalar_tensor_tensor(out=exf[:, 2], in0=exf[:, 0], scalar=float(PKEYS), in1=exf[:, 1], op0=ALU.mult, op1=ALU.add))
                own(dve.tensor_copy(eidx[:, bass.ds(t * P + h * PK, PK)], exf[:, 2]))

            HEAD = 19
            def turns_u(t, i):
                for s in range(2):
                    turn_ = 2 * i + s
                    dve.tensor_copy(now[:, 1 - s, :], eidx[:, bass.ds((turn_ + 1) * UNITS, UNITS)]).then_inc(now_set, 1)
                    for k in range(UNITS):
                        dve.wait_ge(row_in[k], (turn_ + 1) * 16)
                        dve.wait_ge(rows_free, (turn_ + 1) * UNITS + k)
                        dve.tensor_tensor_reduce(prod, ring[:, k, :], cnat[:, t, :], 1.0, 0.0, ALU.mult, ALU.add,
                                                 dots[:, k:k + 1]).then_inc(rows_free, 1)
                    dve.wait_ge(rows_free, (turn_ + 2) * UNITS)
                    dve.tensor_copy(hid[:, bass.ds(turn_ * UNITS, UNITS)], dots).then_inc(hid_part, 1)
                    dve.wait_ge(hid_part, turn_ + 1)

            dve.wait_ge(score_out, 4)
            with dve.Fori(0, PH) as h:
                own.enter(h, HEAD)
                top_head(0, h)
                own.leave(PH)
            own(dve.memset(hid[:, :], 0.0))
            dve.wait_ge(cn_out, 12)
            dve.tensor_copy(now[:, 0, :], eidx[:, 0:UNITS]).then_inc(now_set, 1)
            for t in range(2):
                first = sum(G[:t]) // 2
                with dve.Fori(first, first + PH - t) as i:
                    own.enter(i - first if first else i, HEAD)
                    top_head(t + 1, i - first if first else i)
                    turns_u(t, i)
                    own.leave(PH - t)
            top_head(2, PH - 1)
            def quarters(x):
                for g in range(1, 4):
                    part = slice(TS * g, TS * g + TS)
                    ins = dve.tensor_copy(x[part, 2 * P:2 * P + TS], x[part, 2 * P + TS * g:2 * P + TS * g + TS])
                own(ins)
            quarters(eidx)
            own(dve.tensor_copy(eidx[:, GT * UNITS:GT * UNITS + UNITS], eidx[:, 0:UNITS]))
            turns_u(1, 2 * PH - 1)
            v3 = lambda x: x.rearrange("p (h k) -> p h k", k=PK)
            own(dve.tensor_copy(hsum, v3(topv)[:, :, 0:1].rearrange("p h o -> p (h o)")))
            h3 = hsum.rearrange("p (h o) -> p h o", o=1).broadcast_to([P, 3 * PH, PK])
            dve.tensor_tensor(v3(topv), v3(topv), h3, ALU.subtract).then_inc(gmax_done, 1)
            dve.wait_ge(gexp_done, 1)
            own(dve.tensor_reduce(hsum, v3(topv), AX.X, ALU.add))
            own(dve.reciprocal(hsum, hsum))
            own(dve.tensor_tensor(v3(weight), v3(topv), h3, ALU.mult))
            quarters(weight)
            with dve.Fori(PH * 2, GT // 2) as i:
                turns_u(2, i)
            dve.sem_inc(hid_done, 1)
            dve.wait_ge(gelu_done, 1)
            dve.tensor_tensor(coef[:, 0:GT * UNITS], weight[:, 0:GT * UNITS], hid[:, 0:GT * UNITS], ALU.mult).then_inc(coef_done, 1)
            dve.wait_ge(coef_done, 1)

            def add_back(t):
                lo, n = TT[t]
                dve.wait_ge(yt_mm, t + 1)
                for q in range(4):
                    x_ = xT[:, 4 * q:4 * q + 4, lo:lo + n]
                    ins = dve.tensor_tensor(x_, x_, ps[:, 4 * (t % 2) + q, :].rearrange("p (k n) -> p k n", n=P)[:, :, 0:n], ALU.add)
                ins.then_inc(yt_out, 1)

            done = 0
            for t in range(3):
                if t == 2:
                    dve.wait_ge(acc_used, 1)
                own(dve.memset(acc[t % 2], 0.0))
                with dve.Fori(done // 2, (done + G[t]) // 2) as i:
                    for s in range(2):
                        turn_ = 2 * i + s
                        dve.wait_ge(pe_units, turn_ * len(ON_PE) + 4)
                        dve.tensor_copy(now[:, 1 - s, :], eidx[:, bass.ds((turn_ + 1) * UNITS, UNITS)]).then_inc(now_set, 1)
                        for x, k in enumerate(ON_DVE):
                            if x or s:
                                dve.wait_ge(dve_units, turn_ * len(ON_DVE) + x)
                            else:
                                dve.wait_ge(hid_part, 1)
                            dve.wait_ge(row_in[k], (turn_ + GT + 1) * 16)
                            dve.scalar_tensor_tensor(out=acc[t % 2], in0=ring[:, k, :], scalar=coef[:, bass.ds(turn_ * UNITS + k, 1)],
                                                     in1=acc[t % 2], op0=ALU.mult, op1=ALU.add).then_inc(dve_units, 1)
                        dve.wait_ge(dve_units, (turn_ + 1) * len(ON_DVE))
                done += G[t]
                dve.sem_inc(acc_done, 1)
                if t == 1:
                    add_back(0)
            add_back(1)
            add_back(2)

            with dve.Fori(0, NPLE // SLOTS) as i:
                for k in range(SLOTS):
                    dve.wait_ge(sig_done, i * SLOTS + k + 1)
                    a_, x_ = (r[:, bass.ds(i * SLOTS + k, 1), :].rearrange("p a n -> p (a n)") for r in (aT, xT))
                    dve.tensor_tensor(a_, gate[k], ps[:, 4 + k, 0:N], ALU.mult).then_inc(gate_done, 1)
                    dve.wait_ge(gate_done, SLOTS + i * SLOTS + k + 1)
                    dve.tensor_tensor(a_, a_, x_, ALU.add).then_inc(banks_free, 1)
            dve.wait_ge(banks_free, SLOTS + NMO + NOUT + NPQ + NPLE)
            normalise(3, aT, xT, gfin, y_ready, True)


def _weight_tiles(w):
    r, c = w.shape
    return w.reshape(r // P, P, c // P, P).transpose(2, 1, 0, 3).reshape(c // P, P, -1)


def _features(x):
    return x.T.reshape(-1, P, x.shape[0]).transpose(1, 0, 2)


def _constants():
    s, t = np.arange(P)[:, None], np.arange(P)[None, :]
    masks = [((s >> m) == (t >> m)) & ((s >> (m - 1)) % 2 == 0) & ((t >> (m - 1)) % 2 == 1) for m in LEVELS]
    q, k = np.arange(P)[:, None], np.arange(T)[None, :]
    dist = [np.where(q + P * i >= k, k - q - P * i, NEG) for i in range(2)]
    slope = 2.0 ** (-8.0 * np.arange(1, MH + 1) / MH)
    row_slope, row_q = np.repeat(slope, TQ)[:, None], np.tile(np.arange(TQ), MH)[:, None]
    past = (row_slope * (np.arange(PAST)[None, :] - PAST - row_q)).reshape(TS, NPG // 4, 4, PAGE).transpose(2, 0, 1, 3).reshape(P, -1)
    row = np.arange(P)[:, None]
    of_query = row % TS == np.arange(TS)
    pair = [of_query & (row // 64 == a) for a in range(2)]
    page = [of_query & (row // TS == j) for j in range(4)]
    tok = np.arange(TS)
    own = [np.where((tok // TQ == b) & (tok % TQ <= row_q), row_slope * (tok % TQ - row_q), NEG) for b in range(DB)]
    f = lambda a: np.ascontiguousarray(a, dtype=np.float32)
    return {
        "ident": f(np.eye(P)),
        "masks": f(np.stack(masks, 1)),
        "pdist": f(np.concatenate([dist[0][:, 0:P], dist[1]], 1)),
        "sbias": f(past),
        "sown": f(np.stack(own, 1)),
        "rows": f(np.concatenate(pair + page, 1)),
        "torows": f(np.concatenate([pair[0].T, pair[1].T, of_query.T], 1)),
        "alike": f(row % TS == row.T % TS),
        "tokb": f(tok[:, None] // TQ == np.arange(DB)),
        "fold": f(np.arange(P)[:, None] % TS == tok),
    }


def kernel(**inputs):
    import concourse.bacc as bacc
    from concourse.bass_utils import run_bass_kernel_spmd

    x = {k: np.asarray(v) for k, v in inputs.items()}
    w_in = x["w_in"][0]
    c = np.cumsum([0, 512, 512, 1024, 1024, RANK, 1024, 1024, 1024])
    col = lambda i: w_in[:, c[i]:c[i + 1]]
    gain = lambda g: g.reshape(-1, P).T
    tokens = np.concatenate([x["x_prompt"].reshape(T, D), x["x_sample"].reshape(TS, D)])
    ple = np.concatenate([x["p_prompt"].reshape(T, PLE), x["p_sample"].reshape(TS, PLE)])
    arrays = {
        "xT": _features(tokens),
        "pleT": _features(ple),
        "w_in": _weight_tiles(np.concatenate([col(0), col(1), col(3), col(2), col(7), col(5), col(6)], 1)),
        "w_z": col(4).reshape(KT, P, RANK).transpose(1, 0, 2),
        "w_gu": x["w_gate_up"][0],
        "b_gate": gain(x["b_gate"][0]),
        "g_mix": gain(x["g_mix"][0]),
        "g_ffn": gain(x["g_ffn"][0]),
        "g_fin": gain(x["g_final"]),
        "g_gla": gain(x["g_gla_out"][0]),
        "w_out": _weight_tiles(x["w_out"][0]),
        "w_pq": _weight_tiles(x["w_peer_q"][0]),
        "w_ple": np.concatenate([_weight_tiles(x["w_ple_gate"][0]), _weight_tiles(x["w_ple_proj"][0])], 2),
        "subk": x["peer_sub_keys"][0].transpose(1, 3, 0, 2).reshape(P, PH, PKEYS),
        "u": x["peer_u"][0],
        "vt": x["peer_v"][0],
        "kT": x["cache_k"][0].transpose(0, 3, 2, 1).reshape(-1, DH, MH * PAGE),
        "v": x["cache_v"][0].reshape(-1, PAGE, MH * DH),
        "pages": x["page_table"].reshape(1, DB * NPG),
        "s0": x["state_gla"][0].transpose(0, 2, 1, 3).reshape(DB, GDK, GH * GDV),
        **_constants(),
    }
    arrays = {"in_" + k: np.ascontiguousarray(v) for k, v in arrays.items()}
    outs = {"y": (P, KT, N), "k_new": (P, MH, N), "v_new": (N, MH * DH), "s_prompt": (GDK, GH * GDV), "s_new": (DB, GDK, GH * GDV)}

    nc = bacc.Bacc("TRN2", target_bir_lowering=False, num_devices=1)
    A = {k[3:]: nc.dram_tensor(k, v.shape, mybir.dt.from_np(v.dtype), kind="ExternalInput").ap() for k, v in arrays.items()}
    O = {k: nc.dram_tensor("out_" + k, list(v), F32, kind="ExternalOutput").ap() for k, v in outs.items()}
    program(nc, A, O)
    r = run_bass_kernel_spmd(nc, [arrays], core_ids=[0]).results[0]

    y = r["out_y"].transpose(2, 1, 0).reshape(N, D)
    k_new = r["out_k_new"].transpose(2, 1, 0)
    v_new = r["out_v_new"].reshape(N, MH, DH)
    state = lambda s: s.reshape(-1, GDK, GH, GDV).transpose(0, 2, 1, 3)[None]
    return (y[:T].reshape(1, T, D), y[T:].reshape(DB, TQ, D), k_new[:T].reshape(1, 1, T, MH, DH),
            v_new[:T].reshape(1, 1, T, MH, DH), state(r["out_s_prompt"]), k_new[T:].reshape(1, DB, TQ, MH, DH),
            v_new[T:].reshape(1, DB, TQ, MH, DH), state(r["out_s_new"]))
```

```python
from contextlib import ExitStack

import numpy as np

import concourse.bass as bass
from concourse import mybir

F32 = mybir.dt.float32
I32 = mybir.dt.int32
U32 = mybir.dt.uint32
ALU = mybir.AluOpType
ACT = mybir.ActivationFunctionType
AX = mybir.AxisListType

P = 128
D = 2048
KT = D // P
T = 256
DB, TQ = 8, 4
TS = DB * TQ
N = T + TS
PAST, PAGE = 2048, 128
NPG = PAST // PAGE
NBLK = PAST // 256
GH, GDK, GDV = 4, 128, 256
MH, DH = 8, 128
RANK = 16
PH, PK, PKEYS = 8, 16, 128
PLE = 256
EPS = 1e-6
NEG = -1e30
LOW = -3e38
SCALE = float(DH) ** -0.5

QG, KG, RG, VG, QM, KM = 0, 4, 8, 16, 32, 40
OT = VG
NIN = 48
NMO = 24
GT3 = (NIN - NMO) // DB
NOUT, NPQ, NPLE = 16, 8, 16
SLOTS = 4
WT = KT * P
WS = WT + KT * RANK
UNITS = 8
LEVELS = (1, 2, 3, 4, 5, 6, 7)
NCONST = 12


class Link:

    def __init__(self, eng, sem):
        self.eng, self.sem, self.n, self.turn, self.per = eng, sem, 0, None, 0

    def count(self):
        return self.n if self.turn is None else self.turn * self.per + self.n

    def __call__(self, ins):
        self.n += 1
        ins.then_inc(self.sem, 1)
        self.eng.wait_ge(self.sem, self.count())

    def enter(self, turn, per):
        self.turn, self.per, self.first = turn, per, self.n

    def leave(self, turns):
        assert self.n - self.first == self.per, (self.n - self.first, self.per)
        self.n = self.first + turns * self.per
        self.turn = None


def program(nc, A, O):
    ctx = ExitStack()
    with ctx:
        def sb(name, shape, dt=F32):
            return ctx.enter_context(nc.sbuf_tensor(name, shape, dt))

        def sem(name):
            return ctx.enter_context(nc.semaphore(name))

        xT = sb("xT", [P, KT, N])
        aT = sb("aT", [P, KT, N])
        wring = sb("wring", [P, SLOTS, WS])
        big = sb("big", [P, 28160])
        ident = sb("ident", [P, P])
        ones = sb("ones", [P, P])
        masks = sb("masks", [P, len(LEVELS), P])
        subk = sb("subk", [P, PH, PKEYS])
        states = sb("states", [P, 3, GH * GDV])
        rstd = sb("rstd", [P, N])
        gmix = sb("gmix", [P, KT])
        gffn = sb("gffn", [P, KT])
        gfin = sb("gfin", [P, KT])
        ggla = sb("ggla", [P, 2])
        bgate = sb("bgate", [P, GH])
        pages = sb("pages", [1, DB * NPG], I32)
        small = sb("small", [P, 64])
        ebend = sb("ebend", [P, GH, DB])
        qe = sb("qe", [P, GH, TS])
        tokb = sb("tokb", [TS, DB])
        fold = sb("fold", [P, TS])

        proj = big[:, 0:NIN * N].rearrange("p (j n) -> p j n", n=N)
        vnat = big[:, NIN * N:NIN * N + 3 * D].rearrange("p (t c) -> p t c", c=D)
        kring = big[:, NIN * N + 3 * D:NIN * N + 3 * D + 8 * 1024].rearrange("p (g h k) -> p g h k", g=8, h=MH)
        vring = ([wring[:, SLOTS - 1, j * 1024:(j + 1) * 1024] for j in range(2)] + [states[:, j, :] for j in (1, 2)] +
                 [vnat[:, t, 0:1024] for t in range(3)] + [subk[:, :, :].rearrange("p h k -> p (h k)")])
        flatx = xT[:, :, :].rearrange("p k n -> p (k n)")
        flata = aT[:, :, :].rearrange("p k n -> p (k n)")
        chunk = [r[:, i * GH * N:(i + 1) * GH * N].rearrange("p (h n) -> p h n", n=N)
                 for r in (flatx, flata) for i in range(4)]
        cumb, dist_e, eq, ek, qs, ks = chunk[0:6]
        osq = flatx[:, 0:8 * N].rearrange("p (j n) -> p j n", n=N)
        st = states[:, :, :].rearrange("p s c -> p (s c)")
        gatt, gatt_s, gatt_top = st[:, 0:1024], st[0:TS, 1024:1152], st[:, 1152:1664]
        gtmp, gtmp_s = st[:, 1664:2688], st[0:TS, 2688:2816]
        gsp = flata[:, 0:GH * GDV]
        pdist = flata[:, 2304:2688]
        pbias = [flata[:, 2688 + i * 384:3072 + i * 384] for i in range(2)]
        pprob = [flata[:, 3456 + i * 384:3840 + i * 384] for i in range(2)]
        kflat = big[:, NIN * N + 3 * D:NIN * N + 3 * D + 8 * 1024]
        gstate = [kflat[:, i * 1024:(i + 1) * 1024] for i in range(2)]
        vb = [kflat[0:TS, (2 + i) * 1024:(3 + i) * 1024] for i in range(2)]
        kend = kflat[:, 4096:4096 + 3 * 512].rearrange("p (t c) -> p t c", c=512)
        kendT = kflat[:, 5632:5632 + GH * N].rearrange("p (h n) -> p h n", n=N)
        pprobT = [kflat[:, 6784 + i * 384:7168 + i * 384] for i in range(2)]
        late = flatx[:, GH * N:]
        sbias, sprob, sprobT, so = (late[:, a:b] for a, b in ((0, 512), (512, 1024), (1024, 1536), (1536, 2560)))
        sown = late[0:TS, 2560:2560 + DB * TS].rearrange("p (b k) -> p b k", k=TS)
        sownp, sownT = late[0:TS, 2816:2848], late[0:TS, 2848:2880]
        rows = late[:, 2880:3072]
        rowpair = [rows[:, i * TS:(i + 1) * TS] for i in range(2)]
        rowof = [rows[:, (2 + i) * TS:(3 + i) * TS] for i in range(4)]
        torows = late[0:TS, 3072:3072 + 3 * P]
        alike = st[:, 720:720 + P]
        qpad = st[:, 0:MH * 36]
        s8 = st[0:TS, 512:704]
        psum8 = st[:, 704:712]
        cnat = big[:, 0:3 * D].rearrange("p (t c) -> p t c", c=D)
        ring = big[:, 3 * D:3 * D + UNITS * D].rearrange("p (u c) -> p u c", c=D)
        o = 3 * D + UNITS * D
        prod = big[:, o:o + D]
        o += D
        weight = big[:, o:o + 3 * P]
        o += 3 * P
        hid = big[:, o:o + 3 * P]
        o += 3 * P
        eidx = big[:, o:o + 3 * P].bitcast(U32)
        o += 3 * P
        coef = big[:, o:o + 3 * P]
        o += 3 * P
        dots = big[:, o:o + UNITS]
        o += UNITS
        now = big[:, o:o + 2 * UNITS].bitcast(U32).rearrange("p (s u) -> p s u", u=UNITS)
        o += 2 * UNITS
        diag = big[:, o:o + 4 * P].rearrange("p (s c) -> p s c", c=P)
        o += 4 * P
        assert o <= 28160
        r0 = 3 * D
        qpT = big[:, r0:r0 + PH * N].rearrange("p (h n) -> p h n", n=N)
        r0 += PH * N
        qrep = big[:, r0:r0 + PH * P].rearrange("p (h g n) -> p h g n", g=4, n=TS)
        r0 += PH * P
        crep = big[:, r0:r0 + KT * P].rearrange("p (k g n) -> p k g n", g=4, n=TS)
        assert r0 + KT * P <= 3 * D + UNITS * D
        wflat = wring[:, :, :].rearrange("p s w -> p (s w)")
        score01 = wflat[:, 0:32 * P].rearrange("p (s a k) -> p s a k", s=2, k=P)
        score2 = st[:, 0:16 * P].rearrange("p (s a k) -> p s a k", s=2, k=P)
        rowsT = wflat[:, 32 * P:32 * P + D]
        topv = st[:, 2560:2560 + 3 * P]
        acc = [flata[:, i * D:(i + 1) * D] for i in range(2)]
        hsum = st[:, 2048:2048 + 3 * PH]
        r0 = o
        two = big[:, r0:r0 + 2 * P].rearrange("p (s k) -> p s k", k=P)
        r0 += 2 * P
        half = big[:, r0:r0 + 32].rearrange("p (s k) -> p s k", k=16)
        r0 += 32
        halfi = big[:, r0:r0 + 32].bitcast(U32).rearrange("p (s k) -> p s k", k=16)
        r0 += 32
        halff = big[:, r0:r0 + 32].rearrange("p (s k) -> p s k", k=16)
        r0 += 32
        cand = big[:, r0:r0 + 256]
        r0 += 256
        onehot = big[:, r0:r0 + 512].rearrange("p (s k i) -> p s k i", k=16, i=16)
        r0 += 512
        top1 = big[:, r0:r0 + 16]
        r0 += 16
        pos1 = big[:, r0:r0 + 16].bitcast(U32)
        r0 += 16
        posi = big[:, r0:r0 + 32].bitcast(U32).rearrange("p (s k) -> p s k", k=16)
        r0 += 32
        posf = big[:, r0:r0 + 32].rearrange("p (s k) -> p s k", k=16)
        r0 += 32
        exf = big[:, r0:r0 + 48].rearrange("p (s k) -> p s k", k=16)
        r0 += 48
        iota16 = big[:, r0:r0 + 16]
        assert r0 + 16 <= 28160
        sq1 = proj[:, 0:KT, :]
        sqt = st[:, 0:N]
        pleT = masks[:, :, :].rearrange("p m t -> p (m t)")[:, 0:PLE // P * N].rearrange("p (k n) -> p k n", n=N)
        proj_w = [wflat[:, 6144 + j * PLE:6144 + (j + 1) * PLE] for j in range(12)] + [
            subk[:, :, :].rearrange("p h k -> p (h k)")[:, j * PLE:(j + 1) * PLE] for j in range(4)]
        emb = big[:, 0:KT * N].rearrange("p (j n) -> p j n", n=N)
        gate = [big[:, (KT + i) * N:(KT + i + 1) * N] for i in range(SLOTS)]
        assert 6144 + 12 * PLE <= SLOTS * WS and (KT + SLOTS) * N <= 3 * D
        wz = wring[:, 0, WT:WT + KT * RANK].rearrange("p (k r) -> p k r", r=RANK)
        zT = st[0:RANK, 0:N]
        wgu = st[0:RANK, 512:1024]

        ps = ctx.enter_context(nc.psum_tensor("ps", [P, 8, 512], F32))

        epsc = small[:, 20:21]

        def sems(text):
            return [sem(n) for n in text.split()]

        subk_in = sem("subk_in")
        const_in, x_again, late_in, ple_in = sems("const_in x_again late_in ple_in")
        x_in = [sem(f"x_in{q}") for q in range(4)]
        sums_done, attn_in = sems("sums_done attn_in")
        gproj_free, gbank_free = sems("gproj_free gbank_free")
        gproj_in = [sem(f"gproj_in{j}") for j in range(GT3)]
        w_in = [sem(f"w_in{k}") for k in range(SLOTS)]
        w_slots_free = sem("w_slots_free")
        banks_free = sem("banks_free")
        ones_set, eps_set = sems("ones_set eps_set")
        squares, sum_sq, roots, normed, y_ready = sems("squares sum_sq roots normed y_ready")
        sq_added, emb_mm, emb_out = sems("sq_added emb_mm emb_out")
        z_done, z_out, gate_mm, gate_out, loga_ln = sems("z_done z_out gate_mm gate_out loga_ln")
        vt_done, vt_out = sems("vt_done vt_out")
        exps_in, exps_out = sems("exps_in exps_out")
        lev_in, lev_mm, lev_out = sems("lev_in lev_mm lev_out")
        kend_in, kexp_out, kend_t, kend_out = sems("kend_in kexp_out kend_t kend_out")
        og_mm, og_out, gs_mm, gs_out = sems("og_mm og_out gs_mm gs_out")
        state_in = [sem(f"state_in{i}") for i in range(2)]
        state_out, states_gone, vb_done, state_mm, state_new = sems("state_out states_gone vb_done state_mm state_new")
        og_sq, og_ssum, og_rt, silu_done, og_done = sems("og_sq og_ssum og_rt silu_done og_done")
        pb_done, pq_mm, pq_s, pe_done, pp_done, pt_mm, pt_out, po_mm, po_out = sems(
            "pb_done pq_mm pq_s pe_done pp_done pt_mm pt_out po_mm po_out")
        k_in = [sem(f"k_in{i}") for i in range(2)]
        v_in = [sem(f"v_in{i}") for i in range(4)]
        k_free, v_free = sems("k_free v_free")
        qp_done, qk_done, sc_out, sx_done, rden_done, pT_mm, pT_out, pv_done, so_out, sot_mm, sot_out = sems(
            "qp_done qk_done sc_out sx_done rden_done pT_mm pT_out pv_done so_out sot_mm sot_out")
        psum_in, bsum_mm, sel_in, sel_mm, max_in, max_mm, top_in, top_mm, den_mm = sems(
            "psum_in bsum_mm sel_in sel_mm max_in max_mm top_in top_mm den_mm")
        rep_done, score_mm, score_out, cn_mm, cn_out, gmax_done, gexp_done = sems(
            "rep_done score_mm score_out cn_mm cn_out gmax_done gexp_done")
        row_in = [sem(f"row_in{k}") for k in range(UNITS)]
        udve_free, rowsT_mm, rowsT_out, udots_mm, udots_read = sems("udve_free rowsT_mm rowsT_out udots_mm udots_read")
        now_set, hid_part, hid_done, gelu_done, coef_done = sems(
            "now_set hid_part hid_done gelu_done coef_done")
        diag_set, pe_units, dve_units, acc_done, acc_used, yn_out, yt_mm, yt_out = sems(
            "diag_set pe_units dve_units acc_done acc_used yn_out yt_mm yt_out")
        sig_done, gate_done = sems("sig_done gate_done")
        dve_own, act_own, stored, kv_stored, waits_over = sems("dve_own act_own stored kv_stored waits_over")

        block = ctx.enter_context(nc.Block())
        TT = [(0, P), (P, P), (T, TS)]
        NG = NPG // 4
        G = [P // UNITS, P // UNITS, TS // UNITS]
        GT = sum(G)
        W_OUT, W_PQ, W_PLE = (x // SLOTS for x in (NMO, NMO + NOUT, NMO + NOUT + NPQ))
        n_pages = A["kT"].shape[0]
        U_PE = (0, 4)
        U_DVE = tuple(k for k in range(UNITS) if k not in U_PE)
        ON_DVE = (1, 3, 5, 7)
        ON_PE = tuple(k for k in range(UNITS) if k not in ON_DVE)

        def then_plain(eng):
            eng.sem_inc(waits_over, 1)

        @block.sync
        def _(sp):
            consts = ((ident[:, :], A["ident"]), (masks[:, :, :], A["masks"]),
                      (gmix[:, :], A["g_mix"]), (gffn[:, :], A["g_ffn"]), (gfin[:, :], A["g_fin"]),
                      (ggla[:, :], A["g_gla"]), (bgate[:, :], A["b_gate"]), (pages[:, :], A["pages"]),
                      (wz, A["w_z"]), (wgu, A["w_gu"]), (tokb[:, :], A["tokb"]), (fold[:, :], A["fold"]))
            assert len(consts) == NCONST
            for dst, src in consts:
                sp.dma_start(dst, src).then_inc(const_in, 16)

            def weights(turn, width, src, first):
                for k in range(SLOTS):
                    sp.wait_ge(w_slots_free, (turn + first) * SLOTS + k + 1)
                    sp.dma_start(wring[:, k, 0:width], src[bass.ds(turn * SLOTS + k, 1), :, :]
                                 .rearrange("a p w -> p (a w)")).then_inc(w_in[k], 16)

            def k_pages(b, *groups):
                for g in groups:
                    sp.wait_ge(k_free, b * NG + g + 1)
                    for pg in range(4):
                        page = sp.value_load(pages[0:1, bass.ds(b * NPG + g * 4 + pg, 1)], min_val=0, max_val=n_pages - 1)
                        sp.dma_start(kring[:, (g % 2) * 4 + pg, :, :].rearrange("p h k -> p (h k)"),
                                     A["kT"][bass.ds(page, 1), :, :].rearrange("a p c -> p (a c)")).then_inc(k_in[g % 2], 16)

            def v_pages(b, *pairs):
                for g in pairs:
                    sp.wait_ge(v_free, b * 2 * NG + g + 1)
                    for pg in range(2):
                        page = sp.value_load(pages[0:1, bass.ds(b * NPG + g * 2 + pg, 1)], min_val=0, max_val=n_pages - 1)
                        sp.dma_start(vring[(g % 4) * 2 + pg],
                                     A["v"][bass.ds(page, 1), :, :].rearrange("a p c -> p (a c)")).then_inc(v_in[g % 4], 16)

            def gla_weights(b, j):
                sp.wait_ge(gproj_free, b * GT3 + j + 1)
                sp.dma_start(wring[:, j, 0:WT], A["w_in"][bass.ds(b * GT3 + j, 1), :, :]
                             .rearrange("a p w -> p (a w)")).then_inc(gproj_in[j], 16)

            with sp.Fori(0, NMO // SLOTS) as i:
                for k in range(SLOTS):
                    sp.wait_ge(w_slots_free, i * SLOTS + k + 1)
                    sp.dma_start(wring[:, k, 0:WT], A["w_in"][bass.ds(i * SLOTS + k + NIN - NMO, 1), :, :]
                                 .rearrange("a p w -> p (a w)")).then_inc(w_in[k], 16)
            sp.wait_ge(const_in, 16 * NCONST)
            k_pages(0, 0, 1)
            sp.wait_ge(sums_done, 1)
            for dst, src in ((sbias, "sbias"), (sown, "sown"), (rows, "rows"), (torows, "torows"), (alike, "alike")):
                sp.dma_start(dst, A[src]).then_inc(attn_in, 16)
            for j in range(GT3):
                sp.wait_ge(w_slots_free, NMO + j + 1)
                gla_weights(0, j)
            sp.wait_ge(w_slots_free, NMO + SLOTS)
            k_pages(0, 2, 3)
            sp.wait_ge(vt_out, 6)
            for t, (lo, n) in enumerate(TT):
                sp.dma_start(O["v_new"][lo:lo + n, :], vnat[0:n, t, 1024:2048]).then_inc(kv_stored, 16)
            sp.dma_start(O["k_new"], proj[:, KM:KM + MH, :]).then_inc(kv_stored, 16)
            k_pages(1, 0, 1, 2)

            def request_loads(b, following=True, second=True):
                v_pages(b, 0)
                v_pages(b, 1)
                if following:
                    k_pages(b + 1, 3)
                    gla_weights(b + 1, 0)
                v_pages(b, 2)
                v_pages(b, 3)
                if second:
                    k_pages(b + 2, 0)
                    k_pages(b + 2, 1)
                if following:
                    gla_weights(b + 1, 1)
                v_pages(b, 4)
                v_pages(b, 5)
                if second:
                    k_pages(b + 2, 2)
                v_pages(b, 6)
                v_pages(b, 7)
                if following:
                    gla_weights(b + 1, 2)

            with sp.Fori(0, DB - 2) as b:
                request_loads(b)
            request_loads(DB - 2, second=False)
            request_loads(DB - 1, following=False, second=False)
            sp.wait_ge(gproj_free, NIN - NMO + GT3)
            sp.dma_start(pdist, A["pdist"]).then_inc(late_in, 16)
            sp.wait_ge(v_free, DB * 2 * NG + 4)
            sp.dma_start(subk[:, :, :], A["subk"]).then_inc(subk_in, 16)
            weights(0, WT, A["w_out"], W_OUT)
            sp.wait_ge(gs_out, 1)
            sp.dma_start(O["s_prompt"], gsp).then_inc(kv_stored, 16)
            sp.wait_ge(kv_stored, 16 * 5)
            sp.wait_ge(og_done, 8)
            sp.dma_start(xT[:, :, :], A["xT"]).then_inc(x_again, 16)
            with sp.Fori(1, NOUT // SLOTS) as i:
                weights(i, WT, A["w_out"], W_OUT)
            with sp.Fori(0, NPQ // SLOTS) as i:
                weights(i, WT, A["w_pq"], W_PQ)
            sp.dma_start(pleT, A["pleT"]).then_inc(ple_in, 16)
            sp.wait_ge(w_slots_free, W_PLE * SLOTS + SLOTS)
            sp.dma_start(wflat[:, 6144:6144 + 12 * PLE], A["w_pp"][:, 0:12 * PLE]).then_inc(ple_in, 16)
            sp.wait_ge(score_mm, 12)
            sp.dma_start(subk[:, :, :].rearrange("p h k -> p (h k)"), A["w_pp"][:, 12 * PLE:16 * PLE]).then_inc(ple_in, 16)
            sp.wait_ge(hid_done, 1)
            sp.wait_ge(emb_mm, 16)
            with sp.Fori(0, NPLE // SLOTS) as i:
                weights(i, WT, A["w_ple"], W_PLE)
            for q in range(4):
                sp.wait_ge(y_ready, 4 * q + 4)
                sp.dma_start(O["y"][:, 4 * q:4 * q + 4, :], xT[:, 4 * q:4 * q + 4, :]).then_inc(stored, 16)
            sp.wait_ge(stored, 64)

        @block.gpsimd
        def _(pool):
            pool.memset(ones[:, :], 1.0).then_inc(ones_set, 1)

            def state_load(b, par):
                pool.dma_start(gstate[par], A["s0"][bass.ds(b, 1), :, :].rearrange("a p c -> p (a c)")).then_inc(state_in[par], 16)

            def state_store(b, par):
                pool.wait_ge(state_new, b + 1)
                then_plain(pool)
                pool.dma_start(O["s_new"][bass.ds(b, 1), :, :].rearrange("a p c -> p (a c)"), gstate[par]).then_inc(state_out, 16)
                pool.wait_ge(state_out, (b + 1) * 16)
                then_plain(pool)

            pool.wait_ge(sot_mm, DB)
            state_load(0, 0)
            state_load(1, 1)
            with pool.Fori(0, DB // 2 - 1) as i:
                for par in range(2):
                    state_store(2 * i + par, par)
                    state_load(2 * i + 2 + par, par)
            for par in range(2):
                state_store(DB - 2 + par, par)
            pool.memset(small[:, 21:22], 0.0).then_inc(states_gone, 1)

            def gather(table, turn, slot, free):
                pool.wait_ge(now_set, turn + 1)
                for k in range(UNITS):
                    pool.wait_ge(*free(k))
                    then_plain(pool)
                    pool.indirect_dma_start(ring[:, k, :], None, table,
                                            bass.IndirectOffsetOnAxis(ap=now[:, slot, k:k + 1], axis=0)).then_inc(row_in[k], 16)

            def after_v(turn):
                return lambda k: ((dve_units, turn * len(ON_DVE) + ON_DVE.index(k) + 1) if k in ON_DVE else
                                  (pe_units, turn * len(ON_PE) + ON_PE.index(k) + 1 + 4))

            def after_u(turn):
                return lambda k: ((rowsT_mm, (turn * len(U_PE) + U_PE.index(k) + 1) * 4) if k in U_PE else
                                  (udve_free, turn * len(U_DVE) + U_DVE.index(k) + 1))

            with pool.Fori(0, GT // 2) as i:
                for s in range(2):
                    gather(A["u"], 2 * i + s, s, after_u(2 * i + s))
            gather(A["vt"], GT, 0, after_u(GT))
            gather(A["vt"], GT + 1, 1, after_v(0))
            with pool.Fori(1, GT // 2) as i:
                for s in range(2):
                    gather(A["vt"], GT + 2 * i + s, s, after_v(2 * i + s - 1))

        @block.scalar
        def _(act):
            own = Link(act, act_own)
            for q in range(4):
                act.dma_start(xT[:, 4 * q:4 * q + 4, :], A["xT"][:, 4 * q:4 * q + 4, :]).then_inc(x_in[q], 16)

            def root(n):
                act.wait_ge(sum_sq, n)
                act.activation(rstd[:, :], ps[:, 7, 0:N], ACT.Sqrt, bias=epsc, scale=1.0 / D).then_inc(roots, 1)

            def copy_out(i, first, dst):
                for k in range(SLOTS):
                    act.wait_ge(w_slots_free, (i + first) * SLOTS + k + 1 + SLOTS)
                    act.activation(dst[:, bass.ds(i * SLOTS + k, 1), :].rearrange("p a n -> p (a n)"), ps[:, k, 0:N],
                                   ACT.Copy).then_inc(banks_free, 1)

            def values_out(q0):
                for t, (lo, n) in enumerate(TT):
                    for q in range(2):
                        m = 6 * (q0 == 0) + 2 * t + q
                        act.wait_ge(vt_done, m + 1)
                        act.activation(vnat[0:n, t, (q0 + q) * 512:(q0 + q + 1) * 512], ps[0:n, m % 4, :], ACT.Copy).then_inc(vt_out, 1)

            act.wait_ge(eps_set, 1)
            for q in range(4):
                act.wait_ge(x_in[q], 16)
                act.activation(sq1[:, 4 * q:4 * q + 4, :], xT[:, 4 * q:4 * q + 4, :], ACT.Square).then_inc(squares, 1)
            root(1)
            act.wait_ge(z_done, 1)
            act.activation(zT, ps[0:RANK, 6, 0:N], ACT.Copy).then_inc(z_out, 1)
            act.wait_ge(const_in, 16 * NCONST)
            act.wait_ge(gate_mm, 1)
            for h in range(GH):
                act.activation(eq[:, h, :], ps[:, 4 + h, 0:N],
                               ACT.Identity, bias=bgate[:, h:h + 1]).then_inc(gate_out, 1)
            act.wait_ge(gate_out, GH)
            own(act.activation(ek, eq, ACT.Abs))
            own(act.activation(ek, ek, ACT.Exp, scale=-1.0))
            act.activation(ek, ek, ACT.Ln, bias=1.0).then_inc(loga_ln, 1)
            with act.Fori(0, NMO // SLOTS) as i:
                copy_out(i, 0, proj[:, NIN - NMO:NIN, :])
            values_out(2)
            def gla_out(b, j):
                act.wait_ge(gproj_free, b * GT3 + j + 1 + GT3)
                act.activation(proj[:, bass.ds(b * GT3 + j, 1), :].rearrange("p a n -> p (a n)"), ps[:, 3, 0:N], ACT.Copy).then_inc(gbank_free, 1)

            with act.Fori(0, DB) as b:
                gla_out(b, 0)
                act.wait_ge(sc_out, b + 1)
                act.activation(sprob, sprob, ACT.Exp, bias=small[:, 16:17], accum_out=small[:, 17:18]).then_inc(sx_done, 1)
                act.activation(sownp, sownp, ACT.Exp, bias=small[0:TS, 16:17], accum_out=small[0:TS, 19:20]).then_inc(sx_done, 1)
                gla_out(b, 1)
                act.wait_ge(pT_mm, b + 1)
                act.activation(sprobT, ps[:, 4, :], ACT.Copy).then_inc(pT_out, 1)
                act.activation(sownT, ps[0:TS, 5, 0:TS], ACT.Copy).then_inc(pT_out, 1)
                gla_out(b, 2)
                act.wait_ge(pv_done, b + 1)
                act.wait_ge(rden_done, b + 1)
                act.activation(so[:, 0:512], ps[:, 6, :], ACT.Copy, scale=small[:, 18:19]).then_inc(so_out, 1)
                act.activation(so[:, 512:1024], ps[:, 7, :], ACT.Copy, scale=small[:, 18:19]).then_inc(so_out, 1)
            values_out(0)
            act.activation(proj[:, RG:RG + 8, :], proj[:, RG:RG + 8, :], ACT.Silu).then_inc(silu_done, 1)
            act.wait_ge(kend_in, 1)
            act.activation(kendT, kendT, ACT.Exp).then_inc(kexp_out, 1)
            act.activation(qe[:, :, :], cumb[:, :, T:N], ACT.Exp).then_inc(kexp_out, 1)
            act.activation(ebend[:, :, :], cumb[:, :, T + TQ - 1:N:TQ], ACT.Exp).then_inc(kexp_out, 1)

            def decays(m):
                n = N if m < 2 else T
                act.wait_ge(exps_in, m + 1)
                act.activation(eq[:, :, 0:n], dist_e[:, :, 0:n], ACT.Relu, scale=-1.0)
                own(act.activation(ek[:, :, 0:n], dist_e[:, :, 0:n], ACT.Relu))
                act.activation(eq[:, :, 0:n], eq[:, :, 0:n], ACT.Exp, scale=-1.0)
                act.activation(ek[:, :, 0:n], ek[:, :, 0:n], ACT.Exp, scale=-1.0).then_inc(exps_out, 1)

            def prompt_exps(h):
                s = h % 2
                if h >= 2:
                    act.wait_ge(pq_s, h - 1)
                act.activation(pbias[s], pdist, ACT.Copy, scale=2.0 ** (-8.0 * (h + 1) / MH)).then_inc(pb_done, 1)
                act.wait_ge(pq_s, h + 1)
                for q, (lo, n) in enumerate(((0, P), (P, 2 * P))):
                    act.activation(pprob[s][:, lo:lo + n], pprob[s][:, lo:lo + n], ACT.Exp, bias=small[:, 4 * s + q:4 * s + q + 1],
                                   accum_out=small[:, 8 + 4 * s + q:9 + 4 * s + q]).then_inc(pe_done, 1)

            def prompt_copies(h):
                act.wait_ge(pt_mm, h + 1)
                act.activation(pprobT[h % 2], ps[:, 7, 0:384], ACT.Copy).then_inc(pt_out, 1)
                act.wait_ge(po_mm, h + 1)
                act.activation(proj[:, OT + 8 + h, 0:T], ps[:, 7, 0:T], ACT.Copy).then_inc(po_out, 1)

            act.wait_ge(late_in, 16)
            for m in range(len(LEVELS) + 1):
                decays(m)
                if m == 0:
                    for t, (lo, n) in enumerate(TT):
                        act.wait_ge(kend_t, t + 1)
                        act.activation(kend[0:n, t, :], ps[0:n, 4 + t, :], ACT.Copy).then_inc(kend_out, 1)
                prompt_exps(m)
                if m:
                    prompt_copies(m - 1)
            prompt_copies(MH - 1)
            for h in range(GH):
                act.wait_ge(og_out, 2 * h + 2)
                act.activation(osq[:, 2 * h:2 * h + 2, :], proj[:, OT + 2 * h:OT + 2 * h + 2, :], ACT.Square).then_inc(og_sq, 1)
            for h in range(GH):
                act.wait_ge(og_ssum, h + 1)
                act.activation(ek[:, h, :], ps[:, 6 + h % 2, 0:N], ACT.Sqrt, bias=epsc, scale=1.0 / GDV).then_inc(og_rt, 1)
            act.wait_ge(gs_mm, 1)
            own(act.activation(gsp[:, 0:512], ps[:, 2, :], ACT.Copy))
            act.activation(gsp[:, 512:1024], ps[:, 3, :], ACT.Copy).then_inc(gs_out, 1)

            root(2)
            with act.Fori(0, NPQ // SLOTS) as i:
                copy_out(i, W_PQ, qpT)
            for t in range(3):
                if t == 2:
                    act.wait_ge(states_gone, 1)
                for q in range(4):
                    act.wait_ge(score_mm, 4 * t + q + 1)
                    to, a0 = (score2, 4 * (q % 2)) if t == 2 else (score01, PH * t + 4 * (q % 2))
                    act.activation(to[:, q // 2, a0:a0 + 4, :].rearrange("p a k -> p (a k)"), ps[:, q, :], ACT.Copy).then_inc(score_out, 1)
                for q in range(4):
                    act.wait_ge(cn_mm, 4 * t + q + 1)
                    act.activation(cnat[:, t, q * 512:(q + 1) * 512], ps[:, 4 + q, :], ACT.Copy).then_inc(cn_out, 1)
            def rows_out(turn_):
                for x in range(len(U_PE)):
                    for c in range(4):
                        u = (turn_ * len(U_PE) + x) * 4 + c
                        act.wait_ge(rowsT_mm, u + 1 + 4 * len(U_PE))
                        act.activation(rowsT[:, c * 512:(c + 1) * 512], ps[:, c, :], ACT.Copy).then_inc(rowsT_out, 1)

            with act.Fori(0, G[0] + G[1]) as i:
                rows_out(i)
            act.wait_ge(gmax_done, 1)
            act.activation(topv, topv, ACT.Exp).then_inc(gexp_done, 1)
            with act.Fori(G[0] + G[1], GT) as i:
                rows_out(i)
            act.wait_ge(hid_done, 1)
            act.activation(hid[:, 0:GT * UNITS], hid[:, 0:GT * UNITS], ACT.Gelu).then_inc(gelu_done, 1)
            for j in range(NPLE):
                act.wait_ge(emb_mm, j + 1)
                act.activation(emb[:, j, :], ps[:, j % 8, 0:N], ACT.Copy).then_inc(emb_out, 1)
            act.wait_ge(coef_done, 1)
            done = 0
            for t, (lo, n) in enumerate(TT):
                with act.Fori(done // 2, (done + G[t]) // 2) as i:
                    for s in range(2):
                        for x, k in enumerate(ON_PE):
                            u = (2 * i + s) * len(ON_PE) + x
                            act.wait_ge(pe_units, u + 1)
                            act.activation(diag[:, (s * len(ON_PE) + x) % 4, 0:n], ident[:, :] if t < 2 else fold[:, :], ACT.Copy,
                                           scale=coef[:, bass.ds((2 * i + s) * UNITS + k, 1)]).then_inc(diag_set, 1)
                done += G[t]
                act.wait_ge(acc_used, t + 1)
                if t:
                    act.wait_ge(yt_mm, t)
                for c in range(4):
                    act.activation(prod[0:n, c * 512:(c + 1) * 512], ps[0:n, 4 * (t % 2) + c, :], ACT.Copy).then_inc(yn_out, 1)
            with act.Fori(0, NPLE // SLOTS) as i:
                for k in range(SLOTS):
                    act.wait_ge(w_slots_free, (i + W_PLE) * SLOTS + k + 1 + SLOTS)
                    act.wait_ge(gate_done, i * SLOTS + k + 1)
                    act.activation(gate[k], ps[:, k, 0:N], ACT.Sigmoid).then_inc(sig_done, 1)
            root(3)

        @block.tensor
        def _(pe):
            for s_, n in ((w_slots_free, SLOTS), (banks_free, SLOTS), (k_free, 2), (v_free, 4), (udve_free, len(U_DVE)),
                          (rowsT_mm, 4 * len(U_PE)), (rowsT_out, 4), (udots_read, len(U_PE)),
                          (pe_units, 4), (gate_done, SLOTS), (sot_out, 1),
                          (gproj_free, GT3), (gbank_free, 1)):
                pe.sem_inc(s_, n)

            def sum_squares(n):
                pe.wait_ge(sq_added, n)
                pe.matmul(ps[:, 7, 0:N], ones[:, :], rstd[:, :], start=True, stop=True).then_inc(sum_sq, 1)

            def tiles(i, first, rhs, normed_first=None):
                for k in range(SLOTS):
                    pe.wait_ge(w_in[k], (i + first + 1) * 16)
                    pe.wait_ge(banks_free, (i + first) * SLOTS + k + 1)
                    for kt in range(KT):
                        if k == 0 and normed_first is not None:
                            pe.wait_ge(normed, normed_first + kt + 1)
                        mm = pe.matmul(ps[:, k, 0:N], wring[:, k, kt * P:(kt + 1) * P], rhs[:, kt, :],
                                       start=(kt == 0), stop=(kt == KT - 1))
                    mm.then_inc(w_slots_free, 1)

            pe.wait_ge(ones_set, 1)
            for kt in range(KT):
                if kt % 4 == 0:
                    pe.wait_ge(squares, kt // 4 + 1)
                mm = pe.matmul(ps[:, 7, 0:N], ones[:, :], sq1[:, kt, :], start=(kt == 0), stop=(kt == KT - 1))
            mm.then_inc(sum_sq, 1)
            pe.wait_ge(const_in, 16 * NCONST)
            for kt in range(KT):
                pe.wait_ge(normed, kt + 1)
                mm = pe.matmul(ps[0:RANK, 6, 0:N], wz[:, kt, :], aT[:, kt, :], start=(kt == 0), stop=(kt == KT - 1))
            mm.then_inc(z_done, 1)
            pe.wait_ge(z_out, 1)
            for h in range(GH):
                mm = pe.matmul(ps[:, 4 + h, 0:N], wgu[:, h * P:(h + 1) * P], zT, start=True, stop=True)
            mm.then_inc(gate_mm, 1)
            with pe.Fori(0, NMO // SLOTS) as i:
                tiles(i, 0, aT)

            def turn_values(q0):
                for t, (lo, n) in enumerate(TT):
                    for q in range(2):
                        m = 6 * (q0 == 0) + 2 * t + q
                        if m >= 4:
                            pe.wait_ge(vt_out, m - 3)
                        for f in range(4):
                            mm = pe.transpose(ps[0:n, m % 4, f * P:(f + 1) * P], proj[:, VG + 4 * (q0 + q) + f, lo:lo + n], ident[:, :])
                        mm.then_inc(vt_done, 1)

            pe.wait_ge(banks_free, SLOTS + NMO)
            turn_values(2)
            pe.wait_ge(vt_out, 6)
            def pages_scores(b, g):
                if g == 0:
                    pe.wait_ge(qp_done, b + 1)
                pe.wait_ge(k_in[g % 2], (b * 2 + g // 2 + 1) * 64)
                for h in range(MH):
                    for j in range(4):
                        mm = pe.matmul(ps[j * TS:(j + 1) * TS, 0, g * PAGE:(g + 1) * PAGE], qpad[:, h * TS:(h + 1) * TS],
                                       kring[:, (g % 2) * 4 + j, h, :], start=(h == 0), stop=(h == MH - 1), tile_position=(0, j * TS))
                mm.then_inc(k_free, 1)
                if g == NG - 1:
                    for h in range(MH):
                        mm = pe.matmul(ps[0:TS, 1, 0:TS], qpad[:, h * TS:(h + 1) * TS], proj[:, KM + h, T:N], start=(h == 0), stop=(h == MH - 1))
                    mm.then_inc(qk_done, 1)

            def block_sums(b):
                pe.wait_ge(psum_in, b + 1)
                for a in range(2):
                    mm = pe.matmul(ps[0:TS, 2, a:NBLK:2], rowpair[a], psum8[:, 0:NG], start=True, stop=True)
                mm.then_inc(bsum_mm, 1)

            def masks_back(b):
                pe.wait_ge(sel_in, b + 1)
                for a in range(2):
                    mm = pe.matmul(ps[:, 2, 0:NG], torows[:, a * P:(a + 1) * P], s8[:, 40 + a:48:2], start=(a == 0), stop=(a == 1))
                mm.then_inc(sel_mm, 1)

            def row_maxima(b):
                pe.wait_ge(max_in, b + 1)
                for j in range(4):
                    mm = pe.matmul(ps[0:TS, 2, j:j + 1], rowof[j], psum8[:, 4:5], start=True, stop=True)
                mm.then_inc(max_mm, 1)

            def maximum_back(b):
                pe.wait_ge(top_in, b + 1)
                pe.matmul(ps[:, 2, 0:1], torows[:, 2 * P:3 * P], s8[:, 48:49], start=True, stop=True).then_inc(top_mm, 1)

            def turn(b):
                pe.wait_ge(sx_done, 2 * b + 2)
                then_plain(pe)
                for g in range(NG):
                    pe.transpose(ps[:, 4, g * P:(g + 1) * P], sprob[:, g * PAGE:(g + 1) * PAGE], ident[:, :])
                pe.transpose(ps[0:TS, 5, 0:TS], sownp, ident[0:TS, 0:TS]).then_inc(pT_mm, 1)
                pe.matmul(ps[:, 2, 0:1], alike, small[:, 17:18], start=True, stop=False)
                pe.matmul(ps[:, 2, 0:1], torows[:, 2 * P:3 * P], small[0:TS, 19:20], start=False, stop=True).then_inc(den_mm, 1)

            def gla_tile(b, j, second):
                if not second:
                    pe.wait_ge(gproj_in[j], (b + 1) * 16)
                    pe.wait_ge(gbank_free, b * GT3 + j + 1)
                for kt in range(KT // 2 * second, KT // 2 * (1 + second)):
                    mm = pe.matmul(ps[:, 3, 0:N], wring[:, j, kt * P:(kt + 1) * P], aT[:, kt, :],
                                   start=(kt == 0), stop=(kt == KT - 1))
                if second:
                    mm.then_inc(gproj_free, 1)

            def values(b, early):
                pe.wait_ge(pT_out, 2 * b + 2)
                for g in range(2 * NG):
                    if g == NG:
                        early(b)
                    if g == NG + 2:
                        gla_tile(b, 2, 1)
                    pe.wait_ge(v_in[g % 4], (b * 2 + g // 4 + 1) * 32)
                    for c in range(2):
                        for pg in range(2):
                            j = 2 * (g % 2) + pg
                            mm = pe.matmul(ps[j * TS:(j + 1) * TS, 6 + c, :], sprobT[:, (g // 2) * P + j * TS:(g // 2) * P + (j + 1) * TS],
                                           vring[2 * (g % 4) + pg][:, c * 512:(c + 1) * 512], start=(g < 2), stop=(g >= 2 * NG - 2 and j > 0),
                                           tile_position=(0, j * TS))
                    mm.then_inc(v_free, 1)
                for c in range(2):
                    mm = pe.matmul(ps[0:TS, 6 + c, :], sownT, vnat[0:TS, 2, 1024 + c * 512:1024 + (c + 1) * 512], start=False, stop=True)
                mm.then_inc(pv_done, 1)

            def own_heads(b):
                pe.wait_ge(so_out, 2 * b + 2)
                pe.wait_ge(sot_out, b + 1)
                for h in range(MH):
                    mm = pe.matmul(ps[:, 1, TS + h * TQ:TS + (h + 1) * TQ], so[:, h * DH:(h + 1) * DH], fold[:, h * TQ:(h + 1) * TQ], start=True, stop=True)
                mm.then_inc(sot_mm, 1)

            def request(b, heads=True, following=2):
                gla_tile(b, 0, 0)
                if following > 0:
                    pages_scores(b + 1, 1)
                gla_tile(b, 0, 1)
                masks_back(b)
                if following > 0:
                    pages_scores(b + 1, 2)
                gla_tile(b, 1, 0)
                row_maxima(b)
                if following > 0:
                    pages_scores(b + 1, 3)
                maximum_back(b)
                if heads:
                    own_heads(b - 1)
                gla_tile(b, 1, 1)
                turn(b)
                gla_tile(b, 2, 0)

                def early(b):
                    if following > 1:
                        pages_scores(b + 2, 0)
                    if following > 0:
                        block_sums(b + 1)

                values(b, early)

            for g in range(NG):
                pages_scores(0, g)
            pages_scores(1, 0)
            block_sums(0)
            request(0, heads=False)
            with pe.Fori(1, DB - 2) as b:
                request(b)
            request(DB - 2, following=1)
            request(DB - 1, following=0)
            own_heads(DB - 1)
            pe.wait_ge(sot_out, DB + 1)

            pe.wait_ge(gbank_free, 1 + NIN - NMO)
            turn_values(0)
            def level(m):
                pe.wait_ge(lev_in, m + 1)
                q_, k_ = (qs, ks) if m else (proj[:, QG:QG + 4, :], proj[:, KG:KG + 4, :])
                if m == len(LEVELS) + 1:
                    for h in range(GH):
                        mm = pe.matmul(ps[:, 0, h * P:(h + 1) * P], k_[:, h, 0:P], q_[:, h, P:T], start=True, stop=True)
                else:
                    for t in range(2):
                        for h in range(GH):
                            mm = pe.matmul(ps[:, t, h * P:(h + 1) * P], k_[:, h, t * P:(t + 1) * P],
                                           q_[:, h, t * P:(t + 1) * P], start=True, stop=True)
                if m <= 2:
                    for h in range(GH):
                        mm = pe.matmul(ps[0:TS, 2, h * TS:(h + 1) * TS], k_[:, h, T:N], q_[:, h, T:N], start=True, stop=True)
                mm.then_inc(lev_mm, 1)

            def request_state(b):
                pe.wait_ge(state_in[b % 2], (b // 2 + 1) * 16)
                pe.wait_ge(vb_done, b + 1)
                if b:
                    pe.wait_ge(state_new, b)
                for j in range(8):
                    pe.matmul(ps[:, 3, j * TQ:(j + 1) * TQ], gstate[b % 2][:, (j // 2) * GDV + (j % 2) * P:(j // 2) * GDV + (j % 2 + 1) * P],
                              qe[:, j // 2, b * TQ:(b + 1) * TQ], start=True, stop=True)
                for h in range(GH):
                    mm = pe.matmul(ps[:, 4 + h // 2, (h % 2) * GDV:(h % 2 + 1) * GDV], kend[0:TS, 2, h * P:(h + 1) * P],
                                   vb[b % 2][:, h * GDV:(h + 1) * GDV], start=True, stop=True)
                mm.then_inc(state_mm, 1)

            def prompt_scores(h):
                if h:
                    pe.wait_ge(pq_s, h)
                pe.matmul(ps[:, 6, 0:P], proj[:, QM + h, 0:P], proj[:, KM + h, 0:P], start=True, stop=True)
                pe.matmul(ps[:, 6, P:3 * P], proj[:, QM + h, P:T], proj[:, KM + h, 0:T], start=True, stop=True).then_inc(pq_mm, 1)

            def prompt_values(h):
                s = h % 2
                pe.wait_ge(pp_done, h + 1)
                if h:
                    pe.wait_ge(po_out, h)
                for c in range(3):
                    mm = pe.transpose(ps[:, 7, c * P:(c + 1) * P], pprob[s][:, c * P:(c + 1) * P], ident[:, :])
                mm.then_inc(pt_mm, 1)
                pe.wait_ge(pt_out, h + 1)
                v0, v1 = (vnat[:, t, 1024 + h * DH:1024 + (h + 1) * DH] for t in range(2))
                pe.matmul(ps[:, 7, 0:P], v0, pprobT[s][:, 0:P], start=True, stop=True)
                pe.matmul(ps[:, 7, P:T], v0, pprobT[s][:, P:2 * P], start=True, stop=False)
                pe.matmul(ps[:, 7, P:T], v1, pprobT[s][:, 2 * P:3 * P], start=False, stop=True).then_inc(po_mm, 1)

            pe.wait_ge(vt_out, 12)
            level(0)
            pe.wait_ge(kend_in, 2)
            for t, (lo, n) in enumerate(TT):
                for h in range(GH):
                    mm = pe.transpose(ps[0:n, 4 + t, h * P:(h + 1) * P], kendT[:, h, lo:lo + n], ident[:, :])
                mm.then_inc(kend_t, 1)
            pe.wait_ge(kend_out, 3)
            for m in range(len(LEVELS) + 1):
                prompt_scores(m)
                request_state(m)
                if m:
                    prompt_values(m - 1)
                level(m + 1)
            prompt_values(MH - 1)
            pe.wait_ge(state_new, DB)
            pe.wait_ge(lev_out, len(LEVELS) + 2)
            for j in range(8):
                h, c = j // 2, j % 2
                if j >= 2:
                    pe.wait_ge(og_out, j - 1)
                bank = 4 + j % 2
                v0, v1, v2 = (vnat[0:n, t, h * GDV + c * P:h * GDV + (c + 1) * P] for t, (_, n) in enumerate(TT))
                pe.matmul(ps[:, bank, T:N], v2, gatt_s[:, h * TS:(h + 1) * TS], start=True, stop=True)
                pe.matmul(ps[:, bank, 0:P], v0, gatt[:, h * P:(h + 1) * P], start=True, stop=True)
                pe.matmul(ps[:, bank, P:T], v0, gatt_top[:, h * P:(h + 1) * P], start=True, stop=False)
                pe.matmul(ps[:, bank, P:T], v1, gatt[:, 512 + h * P:512 + (h + 1) * P], start=False, stop=True).then_inc(og_mm, 1)
            for h in range(GH):
                for t in range(2):
                    mm = pe.matmul(ps[:, 2 + h // 2, (h % 2) * GDV:(h % 2 + 1) * GDV], kend[:, t, h * P:(h + 1) * P],
                                   vnat[:, t, h * GDV:(h + 1) * GDV], start=(t == 0), stop=(t == 1))
            mm.then_inc(gs_mm, 1)
            pe.wait_ge(po_out, MH)
            for h in range(GH):
                pe.wait_ge(og_sq, h + 1)
                if h >= 2:
                    pe.wait_ge(og_rt, h - 1)
                for c in range(2):
                    mm = pe.matmul(ps[:, 6 + h % 2, 0:N], ones[:, :], osq[:, 2 * h + c, :], start=(c == 0), stop=(c == 1))
                mm.then_inc(og_ssum, 1)

            pe.wait_ge(gs_out, 1)
            pe.wait_ge(og_done, 8)
            with pe.Fori(0, NOUT // SLOTS) as i:
                tiles(i, W_OUT, proj[:, OT:OT + KT, :])
            sum_squares(1)
            with pe.Fori(0, NPQ // SLOTS) as i:
                tiles(i, W_PQ, aT, normed_first=KT)
            pe.wait_ge(banks_free, SLOTS + NMO + NOUT + NPQ)
            pe.wait_ge(roots, 2)
            pe.wait_ge(subk_in, 16)
            for t, (lo, n) in enumerate(TT):
                if t == 2:
                    pe.wait_ge(rep_done, 8)
                for q in range(4):
                    if t:
                        pe.wait_ge(score_out, 4 * (t - 1) + q + 1)
                    for f in range(4):
                        h, hf = 4 * (q % 2) + f, q // 2
                        rows = slice(64 * hf, 64 * hf + 64)
                        lhs = qpT[rows, h, lo:lo + n] if t < 2 else qrep[rows, h, :, :].rearrange("p g n -> p (g n)")
                        mm = pe.matmul(ps[:, q, f * P:(f + 1) * P], lhs, subk[rows, h, :], start=True, stop=True)
                    mm.then_inc(score_mm, 1)
                for q in range(4):
                    if t:
                        pe.wait_ge(cn_out, 4 * (t - 1) + q + 1)
                    for f in range(4):
                        kt = 4 * q + f
                        src = aT[:, kt, lo:lo + n] if t < 2 else crep[:, kt, :, :].rearrange("p g n -> p (g n)")
                        mm = pe.transpose(ps[:, 4 + q, f * P:(f + 1) * P], src, ident[:, :])
                    mm.then_inc(cn_mm, 1)

            pe.wait_ge(score_out, 12)
            pe.wait_ge(cn_out, 12)
            for t, (lo, n) in enumerate(TT):
                with pe.Fori(sum(G[:t]), sum(G[:t + 1])) as i:
                    for x, k in enumerate(U_PE):
                        pe.wait_ge(row_in[k], (i + 1) * 16)
                        for c in range(4):
                            pe.wait_ge(rowsT_out, (i * len(U_PE) + x) * 4 + c + 1)
                            for f in range(4):
                                kt = 4 * c + f
                                mm = pe.transpose(ps[:, c, f * P:(f + 1) * P], ring[:, k, kt * P:(kt + 1) * P], ident[:, :])
                            mm.then_inc(rowsT_mm, 1)
                        pe.wait_ge(udots_read, i * len(U_PE) + x + 1)
                        for kt in range(KT):
                            if kt % 4 == 0:
                                pe.wait_ge(rowsT_out, (i * len(U_PE) + x) * 4 + kt // 4 + 1 + 4)
                            mm = pe.matmul(ps[:, 4 + x, 0:n], rowsT[:, kt * P:(kt + 1) * P], aT[:, kt, lo:lo + n],
                                           start=(kt == 0), stop=(kt == KT - 1))
                        mm.then_inc(udots_mm, 1)
            pe.wait_ge(udots_read, (GT + 1) * len(U_PE))

            pe.wait_ge(ple_in, 48)
            for j in range(NPLE):
                if j >= 8:
                    pe.wait_ge(emb_out, j - 7)
                for kt in range(PLE // P):
                    mm = pe.matmul(ps[:, j % 8, 0:N], proj_w[j][:, kt * P:(kt + 1) * P], pleT[:, kt, :],
                                   start=(kt == 0), stop=(kt == PLE // P - 1))
                mm.then_inc(emb_mm, 1)
            pe.wait_ge(emb_out, NPLE)

            def unit(w, b0, turn_, s, x, first=False):
                pe.wait_ge(diag_set, turn_ * len(ON_PE) + x + 1)
                pe.wait_ge(row_in[ON_PE[x]], (turn_ + GT + 1) * 16)
                for c in range(4):
                    mm = pe.matmul(ps[0:w, b0 + c, :], diag[:, (s * len(ON_PE) + x) % 4, 0:w], ring[:, ON_PE[x], c * 512:(c + 1) * 512],
                                   start=first, stop=False, skip_group_check=True)
                mm.then_inc(pe_units, 1)

            def back(t):
                b0, n = 4 * (t % 2), TT[t][1]
                pe.wait_ge(yn_out, 4 * t + 4)
                for kt in range(KT):
                    mm = pe.transpose(ps[:, b0 + kt // 4, (kt % 4) * P:(kt % 4) * P + n], prod[0:n, kt * P:(kt + 1) * P], ident[0:n, 0:n])
                mm.then_inc(yt_mm, 1)

            done = 0
            for t, (lo, w) in enumerate(TT):
                b0 = 4 * (t % 2)
                if t == 2:
                    pe.wait_ge(yt_out, 1)
                for s in range(2):
                    for x in range(len(ON_PE)):
                        unit(w, b0, done + s, s, x, first=(s == 0 and x == 0))
                with pe.Fori(done // 2 + 1, (done + G[t]) // 2) as i:
                    for s in range(2):
                        for x in range(len(ON_PE)):
                            unit(w, b0, 2 * i + s, s, x)
                pe.wait_ge(acc_done, t + 1)
                for c in range(4):
                    mm = pe.matmul(ps[0:w, b0 + c, :], ident[:, :] if t < 2 else fold[:, :], acc[t % 2][:, c * 512:(c + 1) * 512],
                                   start=False, stop=True, skip_group_check=True)
                mm.then_inc(acc_used, 1)
                done += G[t]
                if t == 1:
                    back(0)
            back(1)
            back(2)

            pe.wait_ge(yt_out, 3)
            with pe.Fori(0, NPLE // SLOTS) as i:
                tiles(i, W_PLE, xT)
            sum_squares(2)

        @block.vector
        def _(dve):
            own = Link(dve, dve_own)
            dve.memset(epsc, EPS).then_inc(eps_set, 1)

            def normalise(n, src, dst, gain, then):
                dve.wait_ge(roots, n)
                own(dve.reciprocal(rstd[:, :], rstd[:, :]))
                for kt in range(KT):
                    dve.scalar_tensor_tensor(out=dst[:, kt, :], in0=src[:, kt, :], scalar=gain[:, kt:kt + 1],
                                             in1=rstd[:, :], op0=ALU.mult, op1=ALU.mult).then_inc(then, 1)

            def add_square(x_):
                own(dve.tensor_tensor(sqt, x_, x_, ALU.mult))
                own(dve.tensor_tensor(rstd[:, :], rstd[:, :], sqt, ALU.add))

            dve.wait_ge(const_in, 16 * NCONST)
            for q in range(4):
                dve.wait_ge(x_in[q], 16)
            normalise(1, xT, aT, gmix, normed)
            dve.wait_ge(gate_out, GH)
            own(dve.tensor_scalar(dist_e, eq, 0.0, 1.0 / 16, ALU.min, ALU.mult))
            dve.wait_ge(loga_ln, 1)
            own(dve.scalar_tensor_tensor(out=dist_e, in0=ek, scalar=-1.0 / 16, in1=dist_e, op0=ALU.mult, op1=ALU.add))
            dve.wait_ge(ones_set, 1)
            for lo in (0, P):
                for h in range(GH):
                    ins = dve.tensor_tensor_scan(cumb[:, h, lo:lo + P], ones[:, :], dist_e[:, h, lo:lo + P],
                                                 0.0 if lo == 0 else cumb[:, h, P - 1:P], ALU.mult, ALU.add)
                own(ins)
            own(dve.tensor_copy(cumb[:, :, T:N:TQ], dist_e[:, :, T:N:TQ]))
            for j in range(1, TQ):
                own(dve.tensor_tensor(cumb[:, :, T + j:N:TQ], cumb[:, :, T + j - 1:N:TQ], dist_e[:, :, T + j:N:TQ], ALU.add))
            dve.sem_inc(sums_done, 1)
            dve.wait_ge(banks_free, SLOTS + NMO)
            own(dve.memset(st[:, 0:512], 0.0))
            iot, bs, top, idx, idf, sel = (s8[:, 8 * j:8 * j + 8] for j in range(6))
            negmax, ownmax = s8[:, 48:49], s8[:, 49:50]
            for j in range(NBLK):
                dve.memset(iot[:, j:j + 1], float(j))

            def queries(b):
                dve.tensor_copy(qpad.rearrange("p (h x) -> p h x", x=TS + TQ)[:, :, 0:TQ],
                                proj[:, QM:QM + MH, bass.ds(T + b * TQ, TQ)]).then_inc(qp_done, 1)

            def softmax(b, before=True, after=True):
                dve.wait_ge(qk_done, b + 1)
                dve.tensor_reduce(psum8[:, 0:NG], ps[:, 0, :].rearrange("q (g k) -> q g k", k=PAGE), AX.X, ALU.add).then_inc(psum_in, 1)
                if before:
                    dve.wait_ge(pT_mm, b)
                dve.scalar_tensor_tensor(out=sprob, in0=ps[:, 0, :], scalar=SCALE, in1=sbias, op0=ALU.mult, op1=ALU.add)
                own(dve.scalar_tensor_tensor(out=sownp, in0=ps[0:TS, 1, 0:TS], scalar=SCALE,
                                             in1=sown[:, bass.ds(b, 1), :].rearrange("p a k -> p (a k)"), op0=ALU.mult, op1=ALU.add))
                if after:
                    queries(b + 1)
                own(dve.tensor_reduce(ownmax, sownp, AX.X, ALU.max))
                dve.wait_ge(bsum_mm, b + 1)
                own(dve.tensor_copy(bs, ps[0:TS, 2, 0:NBLK]))
                then_plain(dve)
                own(dve.max(top, bs))
                then_plain(dve)
                own(dve.max_index(idx.bitcast(U32), top, bs))
                own(dve.tensor_copy(idf, idx.bitcast(U32)))
                own(dve.tensor_scalar(sel, iot, idf[:, 0:1], None, ALU.is_equal))
                for r in (1, 2):
                    own(dve.scalar_tensor_tensor(out=sel, in0=iot, scalar=idf[:, r:r + 1], in1=sel, op0=ALU.is_equal, op1=ALU.add))
                dve.tensor_scalar(sel, sel, -1.0, -NEG, ALU.add, ALU.mult).then_inc(sel_in, 1)
                dve.wait_ge(sel_mm, b + 1)
                s_ = sprob.rearrange("q (g k) -> q g k", k=PAGE)
                own(dve.tensor_tensor(s_, s_, ps[:, 2, 0:NG].rearrange("q (g o) -> q g o", o=1).broadcast_to([P, NG, PAGE]), ALU.add))
                dve.tensor_reduce(psum8[:, 4:5], sprob, AX.X, ALU.max).then_inc(max_in, 1)
                dve.wait_ge(max_mm, b + 1)
                own(dve.tensor_reduce(negmax, ps[0:TS, 2, 0:4], AX.X, ALU.max))
                dve.tensor_scalar(negmax, negmax, ownmax, -1.0, ALU.max, ALU.mult).then_inc(top_in, 1)
                dve.wait_ge(top_mm, b + 1)
                dve.tensor_copy(small[:, 16:17], ps[:, 2, 0:1]).then_inc(sc_out, 1)
                dve.wait_ge(den_mm, b + 1)
                dve.reciprocal(small[:, 18:19], ps[:, 2, 0:1]).then_inc(rden_done, 1)

            def heads_out(b):
                dve.wait_ge(sot_mm, b + 1)
                dve.tensor_copy(proj[:, OT + 8:OT + 16, bass.ds(T + b * TQ, TQ)],
                                ps[:, 1, TS:2 * TS].rearrange("p (h t) -> p h t", t=TQ)).then_inc(sot_out, 1)

            queries(0)
            dve.wait_ge(attn_in, 80)
            softmax(0, before=False)
            with dve.Fori(1, DB - 1) as b:
                own.enter(b - 1, 11)
                softmax(b)
                heads_out(b - 1)
                own.leave(DB - 2)
            softmax(DB - 1, after=False)
            heads_out(DB - 2)
            heads_out(DB - 1)

            for h in range(GH):
                dve.tensor_scalar(kendT[:, h, 0:T], cumb[:, h, 0:T], -1.0, cumb[:, h, T - 1:T], ALU.mult, ALU.add)
                b_ = cumb[:, h, T:N].rearrange("p (b x) -> p b x", x=TQ)
                ins = dve.tensor_tensor(kendT[:, h, T:N].rearrange("p (b x) -> p b x", x=TQ), b_[:, :, TQ - 1:TQ].broadcast_to([P, DB, TQ]), b_, ALU.subtract)
            ins.then_inc(kend_in, 1)
            dve.wait_ge(gbank_free, 1 + NIN - NMO)
            dve.tensor_scalar(proj[:, QG:QG + 4, :], proj[:, QG:QG + 4, :], float(GDK) ** -0.5, None, ALU.mult).then_inc(lev_in, 1)
            dve.wait_ge(lev_in, 1)

            def distances(m):
                B = 2 << m
                n = N if m < 2 else T
                blocks = lambda a: a.rearrange("p (c x) -> p c x", x=B)
                for h in range(GH):
                    src = blocks(cumb[:, h, 0:n])
                    ins = dve.tensor_tensor(blocks(dist_e[:, h, 0:n]), src, src[:, :, B // 2 - 1:B // 2].broadcast_to([P, n // B, B]), ALU.subtract)
                ins.then_inc(exps_in, 1)

            def decayed(m):
                n = N if m < 2 else T
                dve.wait_ge(exps_out, m + 1)
                dve.tensor_tensor(qs[:, :, 0:n], proj[:, QG:QG + 4, 0:n], eq[:, :, 0:n], ALU.mult)
                dve.tensor_tensor(ks[:, :, 0:n], proj[:, KG:KG + 4, 0:n], ek[:, :, 0:n], ALU.mult).then_inc(lev_in, 1)
                dve.wait_ge(lev_in, m + 2)

            def add_level(m):
                dve.wait_ge(lev_mm, m + 1)
                if m == len(LEVELS) + 1:
                    dve.tensor_copy(gatt_top, ps[:, 0, :]).then_inc(lev_out, 1)
                    return
                mask = ident if m == 0 else masks[:, m - 1, :]
                v = lambda a, w: a.rearrange("p (h t) -> p h t", t=w)
                parts = [(c, P, P, gatt[:, c * 512:(c + 1) * 512], gtmp[:, c * 512:(c + 1) * 512]) for c in range(2)]
                if m <= 2:
                    parts.append((2, TS, TS, gatt_s, gtmp_s))
                for c, n, w, to, tmp in parts:
                    mk = mask[0:n, 0:w].rearrange("p (o t) -> p o t", o=1).broadcast_to([n, GH, w])
                    ins = dve.tensor_tensor(v(tmp if m else to, w), v(ps[0:n, c, 0:GH * w], w), mk, ALU.mult)
                own(ins)
                if m:
                    for c, n, w, to, tmp in parts:
                        ins = dve.tensor_tensor(to, to, tmp, ALU.add)
                    own(ins)
                dve.sem_inc(lev_out, 1)

            def own_values(b):
                dve.tensor_scalar(vb[b % 2], vnat[0:TS, 2, 0:1024], tokb[:, b:b + 1], None, ALU.mult).then_inc(vb_done, 1)

            def request_state(b):
                dve.wait_ge(state_mm, b + 1)
                dve.tensor_copy(proj[:, OT:OT + 8, T + b * TQ:T + (b + 1) * TQ], ps[:, 3, 0:8 * TQ].rearrange("p (j t) -> p j t", t=TQ))
                for h in range(GH):
                    s_ = gstate[b % 2][:, h * GDV:(h + 1) * GDV]
                    ins = dve.scalar_tensor_tensor(out=s_, in0=s_, scalar=ebend[:, h, b:b + 1],
                                                   in1=ps[:, 4 + h // 2, (h % 2) * GDV:(h % 2 + 1) * GDV], op0=ALU.mult, op1=ALU.add)
                ins.then_inc(state_new, 1)

            def prompt_scores(h):
                s = h % 2
                dve.wait_ge(pb_done, h + 1)
                dve.wait_ge(pq_mm, h + 1)
                if h >= 2:
                    dve.wait_ge(pt_mm, h - 1)
                own(dve.scalar_tensor_tensor(out=pprob[s], in0=ps[:, 6, 0:384], scalar=SCALE, in1=pbias[s], op0=ALU.mult, op1=ALU.add))
                dve.tensor_reduce(small[:, 4 * s:4 * s + 1], pprob[s][:, 0:P], AX.X, ALU.max, negate=True)
                dve.tensor_reduce(small[:, 4 * s + 1:4 * s + 2], pprob[s][:, P:3 * P], AX.X, ALU.max, negate=True).then_inc(pq_s, 1)

            def prompt_probabilities(h):
                s = h % 2
                dve.wait_ge(pe_done, 2 * h + 2)
                own(dve.reciprocal(small[:, 8 + 4 * s:10 + 4 * s], small[:, 8 + 4 * s:10 + 4 * s]))
                dve.tensor_scalar(pprob[s][:, 0:P], pprob[s][:, 0:P], small[:, 8 + 4 * s:9 + 4 * s], None, ALU.mult)
                dve.tensor_scalar(pprob[s][:, P:3 * P], pprob[s][:, P:3 * P], small[:, 9 + 4 * s:10 + 4 * s], None, ALU.mult).then_inc(pp_done, 1)

            distances(0)
            dve.wait_ge(kexp_out, 3)
            dve.tensor_tensor(qe[:, :, :], qe[:, :, :], proj[:, QG:QG + 4, T:N], ALU.mult)
            dve.tensor_tensor(kendT, kendT, proj[:, KG:KG + 4, :], ALU.mult).then_inc(kend_in, 1)
            dve.wait_ge(vt_out, 12)
            for m in range(len(LEVELS) + 1):
                own_values(m)
                if m:
                    request_state(m - 1)
                prompt_scores(m)
                if m:
                    prompt_probabilities(m - 1)
                add_level(m)
                decayed(m)
                if m < len(LEVELS):
                    distances(m + 1)
            request_state(DB - 1)
            prompt_probabilities(MH - 1)
            add_level(len(LEVELS) + 1)
            for j in range(8):
                o_, b_ = proj[:, OT + j, :], ps[:, 4 + j % 2, 0:N]
                dve.wait_ge(og_mm, j + 1)
                if j == 0:
                    dve.wait_ge(state_new, DB)
                dve.tensor_copy(o_[:, 0:T], b_[:, 0:T])
                dve.tensor_tensor(o_[:, T:N], o_[:, T:N], b_[:, T:N], ALU.add).then_inc(og_out, 1)
            dve.wait_ge(og_rt, GH)
            own(dve.reciprocal(ek, ek))
            for j in range(8):
                ins = dve.scalar_tensor_tensor(out=proj[:, OT + j, :], in0=proj[:, OT + j, :], scalar=ggla[:, j % 2:j % 2 + 1],
                                               in1=ek[:, j // 2, :], op0=ALU.mult, op1=ALU.mult)
            own(ins)
            dve.wait_ge(silu_done, 1)
            for j in range(8):
                dve.tensor_tensor(proj[:, OT + j, :], proj[:, OT + j, :], proj[:, RG + j, :], ALU.mult).then_inc(og_done, 1)

            dve.wait_ge(x_again, 16)
            own(dve.memset(rstd[:, :], 0.0))
            with dve.Fori(0, NOUT // SLOTS) as i:
                own.enter(i, 2 * SLOTS)
                for k in range(SLOTS):
                    dve.wait_ge(w_slots_free, (i + W_OUT) * SLOTS + k + 1 + SLOTS)
                    x_ = xT[:, bass.ds(i * SLOTS + k, 1), :].rearrange("p a n -> p (a n)")
                    dve.tensor_tensor(x_, x_, ps[:, k, 0:N], ALU.add).then_inc(banks_free, 1)
                    dve.wait_ge(banks_free, (i + W_OUT) * SLOTS + k + 1 + SLOTS)
                    add_square(x_)
                own.leave(NOUT // SLOTS)
            dve.sem_inc(sq_added, 1)
            normalise(2, xT, aT, gffn, normed)
            dve.wait_ge(normed, 2 * KT)
            dve.wait_ge(banks_free, SLOTS + NMO + NOUT + NPQ)
            for g in range(4):
                dve.tensor_copy(qrep[:, :, g, :], qpT[:, :, T:N]).then_inc(rep_done, 1)
                dve.tensor_copy(crep[:, :, g, :], aT[:, :, T:N]).then_inc(rep_done, 1)
            for j in range(16):
                ins = dve.memset(iota16[:, j:j + 1], float(j))
            own(ins)

            def top16(lists, values, index):
                for r in range(2):
                    at = slice(8 * r, 8 * r + 8)
                    for l, x in enumerate(lists):
                        ins = dve.max(values[l][:, at], x)
                    own(ins)
                    then_plain(dve)
                    for l, x in enumerate(lists):
                        ins = dve.max_index(index[l][:, at], values[l][:, at], x)
                    own(ins)
                    then_plain(dve)
                    if r == 0:
                        for l, x in enumerate(lists):
                            ins = dve.match_replace(x, values[l][:, at], x, LOW)
                        own(ins)
                        then_plain(dve)

            def top_head(scores, a, column):
                own(dve.tensor_copy(two, scores[:, :, bass.ds(a, 1), :].rearrange("p s a k -> p s (a k)")))
                then_plain(dve)
                top16([two[:, s] for s in range(2)], [half[:, s] for s in range(2)], [halfi[:, s] for s in range(2)])
                dve.tensor_copy(halff, halfi)
                own(dve.tensor_tensor(cand.rearrange("p (i j) -> p i j", j=16),
                                      half[:, 0, :].rearrange("p (i o) -> p i o", o=1).broadcast_to([P, 16, 16]),
                                      half[:, 1, :].rearrange("p (o j) -> p o j", o=1).broadcast_to([P, 16, 16]), ALU.add))
                then_plain(dve)
                top16([cand], [top1], [pos1])
                dve.tensor_scalar(posi[:, 0], pos1, 4, None, ALU.logical_shift_right)
                dve.tensor_copy(topv[:, bass.ds(column, PK)], top1)
                own(dve.tensor_scalar(posi[:, 1], pos1, 15, None, ALU.bitwise_and))
                own(dve.tensor_copy(posf, posi))
                for s in range(2):
                    ins = dve.tensor_tensor(onehot[:, s], iota16.rearrange("p (o i) -> p o i", o=1).broadcast_to([P, 16, 16]),
                                            posf[:, s].rearrange("p (k o) -> p k o", o=1).broadcast_to([P, 16, 16]), ALU.is_equal)
                own(ins)
                for s in range(2):
                    ins = dve.tensor_tensor(onehot[:, s], onehot[:, s], halff[:, s].rearrange("p (o i) -> p o i", o=1).broadcast_to([P, 16, 16]), ALU.mult)
                own(ins)
                own(dve.tensor_reduce(exf[:, 0:2], onehot, AX.X, ALU.add))
                own(dve.scalar_tensor_tensor(out=exf[:, 2], in0=exf[:, 0], scalar=float(PKEYS), in1=exf[:, 1], op0=ALU.mult, op1=ALU.add))
                own(dve.tensor_copy(eidx[:, bass.ds(column, PK)], exf[:, 2]))

            HEAD = 19
            def turn_u(t, turn_, s):
                dve.tensor_copy(now[:, 1 - s, :], eidx[:, bass.ds((turn_ + 1) * UNITS, UNITS)]).then_inc(now_set, 1)
                n, own_token = (P, ident) if t < 2 else (TS, fold)
                for x, k in enumerate(U_DVE):
                    dve.wait_ge(row_in[k], (turn_ + 1) * 16)
                    dve.wait_ge(udve_free, (turn_ + 1) * len(U_DVE) + x)
                    dve.tensor_tensor_reduce(prod, ring[:, k, :], cnat[:, t, :], 1.0, 0.0, ALU.mult, ALU.add,
                                             dots[:, k:k + 1]).then_inc(udve_free, 1)
                    if x % 3 == 2:
                        y = x // 3
                        dve.wait_ge(udots_mm, turn_ * len(U_PE) + y + 1)
                        dve.wait_ge(udots_read, (turn_ + 1) * len(U_PE) + y)
                        dve.tensor_tensor_reduce(diag[:, y, 0:n], ps[:, 4 + y, 0:n], own_token[:, 0:n], 1.0, 0.0, ALU.mult, ALU.add,
                                                 dots[:, U_PE[y]:U_PE[y] + 1]).then_inc(udots_read, 1)
                dve.wait_ge(udve_free, (turn_ + 2) * len(U_DVE))
                dve.wait_ge(udots_read, (turn_ + 2) * len(U_PE))
                dve.tensor_copy(hid[:, bass.ds(turn_ * UNITS, UNITS)], dots).then_inc(hid_part, 1)
                dve.wait_ge(hid_part, turn_ + 1)

            own(dve.memset(hid[:, :], 0.0))
            dve.wait_ge(score_out, 4)
            top_head(score01, 0, 0)
            dve.wait_ge(cn_out, 12)
            dve.tensor_copy(now[:, 0, :], eidx[:, 0:UNITS]).then_inc(now_set, 1)
            for t in range(2):
                with dve.Fori(4 * t, 4 * t + 4 - t) as i:
                    own.enter(i - 4 * t if t else i, 3 * HEAD)
                    turn_u(t, 4 * i, 0)
                    top_head(score01, 2 * i + 1, (2 * i + 1) * PK)
                    turn_u(t, 4 * i + 1, 1)
                    top_head(score2, i, 2 * P + i * PK)
                    turn_u(t, 4 * i + 2, 0)
                    top_head(score01, 2 * i + 2, (2 * i + 2) * PK)
                    turn_u(t, 4 * i + 3, 1)
                    own.leave(4 - t)
            last = 4 * (PH - 1)
            turn_u(1, last, 0)
            top_head(score01, 2 * PH - 1, (2 * PH - 1) * PK)
            turn_u(1, last + 1, 1)
            top_head(score2, PH - 1, 2 * P + (PH - 1) * PK)
            def quarters(x):
                for g in range(1, 4):
                    part = slice(TS * g, TS * g + TS)
                    ins = dve.tensor_copy(x[part, 2 * P:2 * P + TS], x[part, 2 * P + TS * g:2 * P + TS * g + TS])
                own(ins)
            quarters(eidx)
            own(dve.tensor_copy(eidx[:, GT * UNITS:GT * UNITS + UNITS], eidx[:, 0:UNITS]))
            turn_u(1, last + 2, 0)
            turn_u(1, last + 3, 1)
            v3 = lambda x: x.rearrange("p (h k) -> p h k", k=PK)
            own(dve.tensor_copy(hsum, v3(topv)[:, :, 0:1].rearrange("p h o -> p (h o)")))
            h3 = hsum.rearrange("p (h o) -> p h o", o=1).broadcast_to([P, 3 * PH, PK])
            dve.tensor_tensor(v3(topv), v3(topv), h3, ALU.subtract).then_inc(gmax_done, 1)
            dve.wait_ge(gexp_done, 1)
            own(dve.tensor_reduce(hsum, v3(topv), AX.X, ALU.add))
            own(dve.reciprocal(hsum, hsum))
            own(dve.tensor_tensor(v3(weight), v3(topv), h3, ALU.mult))
            quarters(weight)
            with dve.Fori((G[0] + G[1]) // 2, GT // 2) as i:
                for s in range(2):
                    turn_u(2, 2 * i + s, s)
            dve.sem_inc(hid_done, 1)
            dve.wait_ge(gelu_done, 1)
            dve.tensor_tensor(coef[:, 0:GT * UNITS], weight[:, 0:GT * UNITS], hid[:, 0:GT * UNITS], ALU.mult).then_inc(coef_done, 1)
            dve.wait_ge(coef_done, 1)

            def add_back(t):
                lo, n = TT[t]
                dve.wait_ge(yt_mm, t + 1)
                for q in range(4):
                    x_ = xT[:, 4 * q:4 * q + 4, lo:lo + n]
                    ins = dve.tensor_tensor(x_, x_, ps[:, 4 * (t % 2) + q, :].rearrange("p (k n) -> p k n", n=P)[:, :, 0:n], ALU.add)
                ins.then_inc(yt_out, 1)

            done = 0
            for t in range(3):
                if t == 2:
                    dve.wait_ge(acc_used, 1)
                own(dve.memset(acc[t % 2], 0.0))
                with dve.Fori(done // 2, (done + G[t]) // 2) as i:
                    for s in range(2):
                        turn_ = 2 * i + s
                        dve.wait_ge(pe_units, turn_ * len(ON_PE) + 4)
                        dve.tensor_copy(now[:, 1 - s, :], eidx[:, bass.ds((turn_ + 1) * UNITS, UNITS)]).then_inc(now_set, 1)
                        for x, k in enumerate(ON_DVE):
                            if x or s:
                                dve.wait_ge(dve_units, turn_ * len(ON_DVE) + x)
                            else:
                                dve.wait_ge(hid_part, 1)
                            dve.wait_ge(row_in[k], (turn_ + GT + 1) * 16)
                            dve.scalar_tensor_tensor(out=acc[t % 2], in0=ring[:, k, :], scalar=coef[:, bass.ds(turn_ * UNITS + k, 1)],
                                                     in1=acc[t % 2], op0=ALU.mult, op1=ALU.add).then_inc(dve_units, 1)
                        dve.wait_ge(dve_units, (turn_ + 1) * len(ON_DVE))
                done += G[t]
                dve.sem_inc(acc_done, 1)
                if t == 1:
                    add_back(0)
            add_back(1)
            add_back(2)

            own(dve.memset(rstd[:, :], 0.0))
            with dve.Fori(0, NPLE // SLOTS) as i:
                own.enter(i, 2 * SLOTS)
                for k in range(SLOTS):
                    dve.wait_ge(sig_done, i * SLOTS + k + 1)
                    a_, x_ = (r[:, bass.ds(i * SLOTS + k, 1), :].rearrange("p a n -> p (a n)") for r in (aT, xT))
                    e_ = emb[:, bass.ds(i * SLOTS + k, 1), :].rearrange("p a n -> p (a n)")
                    dve.tensor_tensor(a_, gate[k], e_, ALU.mult).then_inc(gate_done, 1)
                    dve.wait_ge(gate_done, SLOTS + i * SLOTS + k + 1)
                    dve.tensor_tensor(a_, a_, x_, ALU.add).then_inc(banks_free, 1)
                    dve.wait_ge(banks_free, (i + W_PLE) * SLOTS + k + 1 + SLOTS)
                    add_square(a_)
                own.leave(NPLE // SLOTS)
            dve.sem_inc(sq_added, 1)
            normalise(3, aT, xT, gfin, y_ready)


def _weight_tiles(w):
    r, c = w.shape
    return w.reshape(r // P, P, c // P, P).transpose(2, 1, 0, 3).reshape(c // P, P, -1)


def _features(x):
    return x.T.reshape(-1, P, x.shape[0]).transpose(1, 0, 2)


def _constants():
    s, t = np.arange(P)[:, None], np.arange(P)[None, :]
    masks = [((s >> m) == (t >> m)) & ((s >> (m - 1)) % 2 == 0) & ((t >> (m - 1)) % 2 == 1) for m in LEVELS]
    q, k = np.arange(P)[:, None], np.arange(T)[None, :]
    dist = [np.where(q + P * i >= k, k - q - P * i, NEG) for i in range(2)]
    slope = 2.0 ** (-8.0 * np.arange(1, MH + 1) / MH)
    row_slope, row_q = np.repeat(slope, TQ)[:, None], np.tile(np.arange(TQ), MH)[:, None]
    past = (row_slope * (np.arange(PAST)[None, :] - PAST - row_q)).reshape(TS, NPG // 4, 4, PAGE).transpose(2, 0, 1, 3).reshape(P, -1)
    row = np.arange(P)[:, None]
    of_query = row % TS == np.arange(TS)
    pair = [of_query & (row // 64 == a) for a in range(2)]
    page = [of_query & (row // TS == j) for j in range(4)]
    tok = np.arange(TS)
    own = [np.where((tok // TQ == b) & (tok % TQ <= row_q), row_slope * (tok % TQ - row_q), NEG) for b in range(DB)]
    f = lambda a: np.ascontiguousarray(a, dtype=np.float32)
    return {
        "ident": f(np.eye(P)),
        "masks": f(np.stack(masks, 1)),
        "pdist": f(np.concatenate([dist[0][:, 0:P], dist[1]], 1)),
        "sbias": f(past),
        "sown": f(np.stack(own, 1)),
        "rows": f(np.concatenate(pair + page, 1)),
        "torows": f(np.concatenate([pair[0].T, pair[1].T, of_query.T], 1)),
        "alike": f(row % TS == row.T % TS),
        "tokb": f(tok[:, None] // TQ == np.arange(DB)),
        "fold": f(np.arange(P)[:, None] % TS == tok),
    }


def kernel(**inputs):
    import concourse.bacc as bacc
    from concourse.bass_utils import run_bass_kernel_spmd

    x = {k: np.asarray(v) for k, v in inputs.items()}
    w_in = x["w_in"][0]
    c = np.cumsum([0, 512, 512, 1024, 1024, RANK, 1024, 1024, 1024])
    col = lambda i: w_in[:, c[i]:c[i + 1]]
    gain = lambda g: g.reshape(-1, P).T
    tokens = np.concatenate([x["x_prompt"].reshape(T, D), x["x_sample"].reshape(TS, D)])
    ple = np.concatenate([x["p_prompt"].reshape(T, PLE), x["p_sample"].reshape(TS, PLE)])
    arrays = {
        "xT": _features(tokens),
        "pleT": _features(ple),
        "w_in": _weight_tiles(np.concatenate([col(0), col(1), col(3), col(2), col(7), col(5), col(6)], 1)),
        "w_z": col(4).reshape(KT, P, RANK).transpose(1, 0, 2),
        "w_gu": x["w_gate_up"][0],
        "b_gate": gain(x["b_gate"][0]),
        "g_mix": gain(x["g_mix"][0]),
        "g_ffn": gain(x["g_ffn"][0]),
        "g_fin": gain(x["g_final"]),
        "g_gla": gain(x["g_gla_out"][0]),
        "w_out": _weight_tiles(x["w_out"][0]),
        "w_pq": _weight_tiles(x["w_peer_q"][0]),
        "w_ple": _weight_tiles(x["w_ple_gate"][0]),
        "w_pp": _weight_tiles(x["w_ple_proj"][0]).transpose(1, 0, 2).reshape(P, -1),
        "subk": x["peer_sub_keys"][0].transpose(1, 3, 0, 2).reshape(P, PH, PKEYS),
        "u": x["peer_u"][0],
        "vt": x["peer_v"][0],
        "kT": x["cache_k"][0].transpose(0, 3, 2, 1).reshape(-1, DH, MH * PAGE),
        "v": x["cache_v"][0].reshape(-1, PAGE, MH * DH),
        "pages": x["page_table"].reshape(1, DB * NPG),
        "s0": x["state_gla"][0].transpose(0, 2, 1, 3).reshape(DB, GDK, GH * GDV),
        **_constants(),
    }
    arrays = {"in_" + k: np.ascontiguousarray(v) for k, v in arrays.items()}
    outs = {"y": (P, KT, N), "k_new": (P, MH, N), "v_new": (N, MH * DH), "s_prompt": (GDK, GH * GDV), "s_new": (DB, GDK, GH * GDV)}

    nc = bacc.Bacc("TRN2", target_bir_lowering=False, num_devices=1)
    A = {k[3:]: nc.dram_tensor(k, v.shape, mybir.dt.from_np(v.dtype), kind="ExternalInput").ap() for k, v in arrays.items()}
    O = {k: nc.dram_tensor("out_" + k, list(v), F32, kind="ExternalOutput").ap() for k, v in outs.items()}
    program(nc, A, O)
    r = run_bass_kernel_spmd(nc, [arrays], core_ids=[0]).results[0]

    y = r["out_y"].transpose(2, 1, 0).reshape(N, D)
    k_new = r["out_k_new"].transpose(2, 1, 0)
    v_new = r["out_v_new"].reshape(N, MH, DH)
    state = lambda s: s.reshape(-1, GDK, GH, GDV).transpose(0, 2, 1, 3)[None]
    return (y[:T].reshape(1, T, D), y[T:].reshape(DB, TQ, D), k_new[:T].reshape(1, 1, T, MH, DH),
            v_new[:T].reshape(1, 1, T, MH, DH), state(r["out_s_prompt"]), k_new[T:].reshape(1, DB, TQ, MH, DH),
            v_new[T:].reshape(1, DB, TQ, MH, DH), state(r["out_s_new"]))
```
